# Optimizing a Trainium2 kernel written in Bass

```python
import jax, jax.numpy as jnp
from jax import lax
import numpy as np
import math

D_MODEL = 1024
BATCH = 1
SEQ = 512
DEPTH = 1

N_MEM = 256
RMS_EPS = 1e-6
GN_EPS = 1e-5
ATT_HEADS = 8
ATT_HEAD_DIM = 64
ATT_WIDTH = ATT_HEADS * ATT_HEAD_DIM
ROT_DIM = ATT_HEAD_DIM // 4
ROPE_THETA = 500000.0
DILATED_PATTERNS = ((128, 1), (512, 4), (2048, 16))
RET_HEADS = 4
RET_HEAD_DIM = 128
RET_WIDTH = RET_HEADS * RET_HEAD_DIM
RET_CHUNK = 128
RET_ROPE_THETA = 10000.0
MIX_WIDTH = ATT_WIDTH + RET_WIDTH
IN_PROJ_WIDTH = 3 * ATT_WIDTH + 4 * RET_WIDTH
XATT_HEADS = 4
XATT_HEAD_DIM = D_MODEL // XATT_HEADS
FFN_HIDDEN = -(-(8 * D_MODEL) // (3 * 256)) * 256


def rms_norm(x, g):
    xf = x.astype(jnp.float32)
    y = xf * lax.rsqrt(jnp.mean(xf * xf, axis=-1, keepdims=True) + RMS_EPS)
    return (y * g.astype(jnp.float32)).astype(x.dtype)

def rope(x, pos, rot_dim, theta):
    inv = theta ** (-(jnp.arange(0, rot_dim, 2, dtype=jnp.float32) / rot_dim))
    ang = pos.astype(jnp.float32)[:, None] * inv[None, :]
    cos, sin = jnp.cos(ang), jnp.sin(ang)
    xr = x[..., :rot_dim].astype(jnp.float32)
    x1, x2 = xr[..., : rot_dim // 2], xr[..., rot_dim // 2:]
    rot = jnp.concatenate([x1 * cos - x2 * sin, x2 * cos + x1 * sin], axis=-1)
    return jnp.concatenate([rot.astype(x.dtype), x[..., rot_dim:]], axis=-1)

def window_attn_by_stride(q, k, v, window, dilation):
    B, H, S, dh = q.shape
    n_keys = window // dilation
    L = S // dilation
    nb = -(-L // n_keys)
    Lp = nb * n_keys

    def to_classes(t):
        t = t.reshape(B, H, L, dilation, dh).transpose(0, 1, 3, 2, 4)
        return jnp.pad(t, [(0, 0)] * 3 + [(0, Lp - L), (0, 0)])

    def with_prev(t):
        cur = t.reshape(B, H, dilation, nb, n_keys, dh)
        prev = jnp.pad(cur, [(0, 0)] * 3 + [(1, 0), (0, 0), (0, 0)])[:, :, :, :nb]
        return jnp.concatenate([prev, cur], axis=-2)

    qb = to_classes(q).reshape(B, H, dilation, nb, n_keys, dh)
    kb = with_prev(to_classes(k))
    vb = with_prev(to_classes(v)).astype(jnp.float32)
    s = jnp.einsum('bhrnid,bhrnjd->bhrnij', qb, kb).astype(jnp.float32) * (dh ** -0.5)
    i = jnp.arange(n_keys)[:, None]
    j = jnp.arange(2 * n_keys)[None, :]
    band = (j >= i) & (j <= i + n_keys)
    not_before_start = (jnp.arange(nb)[:, None, None] > 0) | (j[None] >= n_keys)
    mask = band[None] & not_before_start
    s = jnp.where(mask, s, -jnp.inf)
    m = jnp.max(s, axis=-1)
    p = jnp.exp(s - m[..., None])
    l = jnp.sum(p, axis=-1)
    o = jnp.einsum('bhrnij,bhrnjd->bhrnid', p, vb) / l[..., None]

    def back(t, has_d):
        if has_d:
            t = t.reshape(B, H, dilation, Lp, dh)[:, :, :, :L]
            return t.transpose(0, 1, 3, 2, 4).reshape(B, H, S, dh)
        t = t.reshape(B, H, dilation, Lp)[:, :, :, :L]
        return t.transpose(0, 1, 3, 2).reshape(B, H, S)

    return back(o, True), back(m, False), back(l, False)

def dilated_attention(q, k, v):
    outs = [window_attn_by_stride(q, k, v, w, r) for (w, r) in DILATED_PATTERNS]
    m_all = jnp.max(jnp.stack([m for _, m, _ in outs], axis=0), axis=0)
    wts = [l * jnp.exp(m - m_all) for _, m, l in outs]
    num = sum(wt[..., None] * o for wt, (o, _, _) in zip(wts, outs))
    den = sum(wts)
    return num / den[..., None]

def retention(q, k, v):
    B, H, S, dk = q.shape
    dv = v.shape[-1]
    C = RET_CHUNK
    nc = S // C
    log_g = jnp.log(1.0 - 2.0 ** (-5.0 - jnp.arange(H, dtype=jnp.float32)))
    n = jnp.arange(C, dtype=jnp.float32)
    rel = n[:, None] - n[None, :]
    decay_mask = jnp.where(rel >= 0, jnp.exp(log_g[:, None, None] * jnp.maximum(rel, 0.0)), 0.0)
    xi = jnp.exp(log_g[:, None] * (n + 1.0))
    zeta = jnp.exp(log_g[:, None] * (C - 1.0 - n))
    chunk_decay = jnp.exp(log_g * C)

    def chunks(t):
        return t.reshape(B, H, nc, C, t.shape[-1]).transpose(2, 0, 1, 3, 4)

    def step(R, qkv):
        qc, kc, vc = qkv
        inner = jnp.einsum('bhnd,bhmd->bhnm', qc, kc) * decay_mask
        o = jnp.einsum('bhnm,bhme->bhne', inner, vc)
        o = o + jnp.einsum('bhnd,bhde->bhne', qc, R) * xi[:, :, None]
        R = R * chunk_decay[:, None, None] + jnp.einsum('bhmd,bhme->bhde', kc * zeta[:, :, None], vc)
        return R, o

    R0 = jnp.zeros((B, H, dk, dv), jnp.float32)
    _, o = lax.scan(step, R0, (chunks(q), chunks(k), chunks(v)))
    return o.transpose(1, 2, 0, 3, 4).reshape(B, H, S, dv)

def hybrid_mixer(h, w_in, attn_gn_g, ret_gn_g, w_out):
    B, S, _ = h.shape
    proj = h @ w_in
    splits = list(np.cumsum([ATT_WIDTH] * 3 + [RET_WIDTH] * 3))
    aq, ak, av, rq, rk, rv, rg = jnp.split(proj, splits, axis=-1)
    pos = jnp.arange(S)

    def heads(t, nh, d):
        return t.reshape(B, S, nh, d).transpose(0, 2, 1, 3)

    aq = rope(heads(aq, ATT_HEADS, ATT_HEAD_DIM), pos, ROT_DIM, ROPE_THETA)
    ak = rope(heads(ak, ATT_HEADS, ATT_HEAD_DIM), pos, ROT_DIM, ROPE_THETA)
    a = dilated_attention(aq, ak, heads(av, ATT_HEADS, ATT_HEAD_DIM))
    a = a * lax.rsqrt(jnp.mean(a * a, axis=-1, keepdims=True) + RMS_EPS)
    a = a.transpose(0, 2, 1, 3).reshape(B, S, ATT_WIDTH) * attn_gn_g.astype(jnp.float32)

    rq = rope(heads(rq, RET_HEADS, RET_HEAD_DIM).astype(jnp.float32), pos, RET_HEAD_DIM, RET_ROPE_THETA)
    rk = rope(heads(rk, RET_HEADS, RET_HEAD_DIM).astype(jnp.float32), pos, RET_HEAD_DIM, RET_ROPE_THETA)
    rk = rk * (RET_HEAD_DIM ** -0.5)
    r = retention(rq, rk, heads(rv, RET_HEADS, RET_HEAD_DIM).astype(jnp.float32))
    mu = jnp.mean(r, axis=-1, keepdims=True)
    var = jnp.mean(jnp.square(r - mu), axis=-1, keepdims=True)
    r = (r - mu) * lax.rsqrt(var + GN_EPS)
    r = r.transpose(0, 2, 1, 3).reshape(B, S, RET_WIDTH) * ret_gn_g.astype(jnp.float32)
    r = jax.nn.silu(rg.astype(jnp.float32)) * r

    y = jnp.concatenate([a, r], axis=-1).astype(h.dtype)
    return y @ w_out

def memory_cross_attn(h, mem, mem_norm_g, w_q, w_kv, w_o):
    B, S, _ = h.shape
    mh = rms_norm(mem, mem_norm_g)
    q = (h @ w_q).reshape(B, S, XATT_HEADS, XATT_HEAD_DIM)
    k, v = jnp.split(mh @ w_kv, 2, axis=-1)
    k = k.reshape(B, N_MEM, XATT_HEADS, XATT_HEAD_DIM)
    v = v.reshape(B, N_MEM, XATT_HEADS, XATT_HEAD_DIM)
    s = jnp.einsum('bshd,bmhd->bhsm', q, k).astype(jnp.float32) * (XATT_HEAD_DIM ** -0.5)
    p = jax.nn.softmax(s, axis=-1)
    o = jnp.einsum('bhsm,bmhd->bshd', p.astype(v.dtype), v).reshape(B, S, D_MODEL)
    return o @ w_o

def swiglu(h, w_gate_up, w_down):
    g, u = jnp.split(h @ w_gate_up, 2, axis=-1)
    return (jax.nn.silu(g) * u) @ w_down

def first_inputs(seed: int = 0) -> dict:
    key = jax.random.key(seed)
    ks = jax.random.split(key, 20)

    def w(k, shape, fan_in):
        return jax.random.normal(k, shape, jnp.float32) * (fan_in ** -0.5)

    def gain(k, n):
        return 1.0 + 0.05 * jax.random.normal(k, (DEPTH, n), jnp.float32)

    return {
        "x": jax.random.normal(ks[0], (BATCH, SEQ, D_MODEL), jnp.float32),
        "mem": jax.random.normal(ks[1], (BATCH, N_MEM, D_MODEL), jnp.float32),
        "pre_mix_g": gain(ks[2], D_MODEL),
        "post_mix_g": gain(ks[3], D_MODEL),
        "w_in": w(ks[4], (DEPTH, D_MODEL, IN_PROJ_WIDTH), D_MODEL),
        "attn_gn_g": gain(ks[5], ATT_WIDTH),
        "ret_gn_g": gain(ks[6], RET_WIDTH),
        "w_out": w(ks[7], (DEPTH, MIX_WIDTH, D_MODEL), MIX_WIDTH),
        "pre_mem_g": gain(ks[8], D_MODEL),
        "post_mem_g": gain(ks[9], D_MODEL),
        "mem_norm_g": gain(ks[10], D_MODEL),
        "w_q_mem": w(ks[11], (DEPTH, D_MODEL, D_MODEL), D_MODEL),
        "w_kv_mem": w(ks[12], (DEPTH, D_MODEL, 2 * D_MODEL), D_MODEL),
        "w_o_mem": w(ks[13], (DEPTH, D_MODEL, D_MODEL), D_MODEL),
        "pre_ffn_g": gain(ks[14], D_MODEL),
        "post_ffn_g": gain(ks[15], D_MODEL),
        "w_gate_up": w(ks[16], (DEPTH, D_MODEL, 2 * FFN_HIDDEN), D_MODEL),
        "w_down": w(ks[17], (DEPTH, FFN_HIDDEN, D_MODEL), FFN_HIDDEN),
    }

def first_block(x, mem, pre_mix_g, post_mix_g, w_in, attn_gn_g, ret_gn_g, w_out,
              pre_mem_g, post_mem_g, mem_norm_g, w_q_mem, w_kv_mem, w_o_mem,
              pre_ffn_g, post_ffn_g, w_gate_up, w_down):
    for l in range(DEPTH):
        y = hybrid_mixer(rms_norm(x, pre_mix_g[l]), w_in[l], attn_gn_g[l], ret_gn_g[l], w_out[l])
        x = x + rms_norm(y, post_mix_g[l])
        y = memory_cross_attn(rms_norm(x, pre_mem_g[l]), mem, mem_norm_g[l],
                              w_q_mem[l], w_kv_mem[l], w_o_mem[l])
        x = x + rms_norm(y, post_mem_g[l])
        y = swiglu(rms_norm(x, pre_ffn_g[l]), w_gate_up[l], w_down[l])
        x = x + rms_norm(y, post_ffn_g[l])
    return x


DEPTH_2 = 2

HEAD_DIM = 64
LRU_WIDTH = D_MODEL // 2
LRU_BLOCKS = LRU_WIDTH // HEAD_DIM
SB_HEADS = D_MODEL // 256
FOX_HEADS = D_MODEL // 256
SB_WIDTH = SB_HEADS * HEAD_DIM
FOX_WIDTH = FOX_HEADS * HEAD_DIM
D_MIX = LRU_WIDTH + SB_WIDTH + FOX_WIDTH
CONV_WIDTH = 4
LRU_C = 8.0
D_FF = 2816
Q_BLOCK = 128
N_SUB = 3
EPS = 1e-6

SPLIT_SIZES = (LRU_WIDTH, LRU_WIDTH,
               SB_WIDTH, SB_WIDTH, SB_WIDTH,
               FOX_WIDTH, FOX_WIDTH, FOX_WIDTH,
               FOX_HEADS)
N_IN = sum(SPLIT_SIZES)
SPLIT_POINTS = tuple(int(v) for v in np.cumsum(SPLIT_SIZES)[:-1])


def _rms(x):
    xf = x.astype(jnp.float32)
    y = xf * lax.rsqrt(jnp.mean(xf * xf, axis=-1, keepdims=True) + EPS)
    return y.astype(x.dtype)

def _swiglu(h, w_up, w_down):
    gu = h @ w_up
    g, u = jnp.split(gu, 2, axis=-1)
    return (jax.nn.silu(g) * u) @ w_down

def _causal_depthwise_conv(x, w, b):
    y = lax.conv_general_dilated(
        x, w[:, None, :], window_strides=(1,), padding=[(CONV_WIDTH - 1, 0)],
        dimension_numbers=("NWC", "WIO", "NWC"), feature_group_count=x.shape[-1])
    return y + b

def _lru_combine(left, right):
    a1, b1 = left
    a2, b2 = right
    return a1 * a2, a2 * b1 + b2

def _rg_lru(u, w_r, b_r, w_i, b_i, lam):
    B, S, _ = u.shape
    ub = u.reshape(B, S, LRU_BLOCKS, HEAD_DIM)
    r = jax.nn.sigmoid(jnp.einsum("bshi,hij->bshj", ub, w_r).reshape(B, S, LRU_WIDTH) + b_r)
    i = jax.nn.sigmoid(jnp.einsum("bshi,hij->bshj", ub, w_i).reshape(B, S, LRU_WIDTH) + b_i)
    r = r.astype(jnp.float32)
    log_a = -LRU_C * r * jax.nn.softplus(-lam.astype(jnp.float32))
    a = jnp.exp(log_a)
    mult = jnp.sqrt(-jnp.expm1(2.0 * log_a))
    bt = mult * (i.astype(jnp.float32) * u.astype(jnp.float32))
    _, h = lax.associative_scan(_lru_combine, (a, bt), axis=1)
    return h.astype(u.dtype)

def _to_heads(t, n_heads):
    B, S, _ = t.shape
    return t.reshape(B, S, n_heads, HEAD_DIM).transpose(0, 2, 1, 3)

def _from_blocks(out):
    nb, B, H, Q, Dh = out.shape
    return out.transpose(1, 0, 3, 2, 4).reshape(B, nb * Q, H * Dh)

def _stick_breaking_attention(q, k, v):
    S = q.shape[2]
    scale = HEAD_DIM ** -0.5
    key_pos = jnp.arange(S)

    def block(bi):
        start = bi * Q_BLOCK
        qb = lax.dynamic_slice_in_dim(q, start, Q_BLOCK, axis=2)
        z = jnp.einsum("bhqd,bhkd->bhqk", qb, k).astype(jnp.float32) * scale
        q_pos = start + jnp.arange(Q_BLOCK)
        past = key_pos[None, :] < q_pos[:, None]
        log_beta = jax.nn.log_sigmoid(z)
        log_1mb = jnp.where(past, jax.nn.log_sigmoid(-z), 0.0)
        after = lax.cumsum(log_1mb, axis=3, reverse=True) - log_1mb
        w = jnp.where(past, jnp.exp(log_beta + after), 0.0)
        return jnp.einsum("bhqk,bhkd->bhqd", w.astype(v.dtype), v)

    return _from_blocks(lax.map(block, jnp.arange(S // Q_BLOCK)))

def _forgetting_attention(q, k, v, log_f):
    S = q.shape[2]
    scale = HEAD_DIM ** -0.5
    key_pos = jnp.arange(S)
    F = jnp.cumsum(log_f, axis=-1)

    def block(bi):
        start = bi * Q_BLOCK
        qb = lax.dynamic_slice_in_dim(q, start, Q_BLOCK, axis=2)
        Fq = lax.dynamic_slice_in_dim(F, start, Q_BLOCK, axis=2)
        logits = jnp.einsum("bhqd,bhkd->bhqk", qb, k).astype(jnp.float32) * scale
        logits = logits + Fq[..., :, None] - F[..., None, :]
        q_pos = start + jnp.arange(Q_BLOCK)
        causal = key_pos[None, :] <= q_pos[:, None]
        logits = jnp.where(causal, logits, -jnp.inf)
        p = jax.nn.softmax(logits, axis=-1)
        return jnp.einsum("bhqk,bhkd->bhqd", p.astype(v.dtype), v)

    return _from_blocks(lax.map(block, jnp.arange(S // Q_BLOCK)))

def _mixer(h, w_in, b_fgate, conv_w, conv_b, w_rgate, b_rgate, w_igate, b_igate,
           lru_lambda, g_qk, g_mix_out, w_out):
    proj = h @ w_in
    (lru_x, lru_g, sb_q, sb_k, sb_v, fx_q, fx_k, fx_v, fx_f) = jnp.split(proj, SPLIT_POINTS, axis=-1)

    u = _causal_depthwise_conv(lru_x, conv_w, conv_b)
    y_lru = _rg_lru(u, w_rgate, b_rgate, w_igate, b_igate, lru_lambda) * jax.nn.gelu(lru_g)

    y_sb = _stick_breaking_attention(_to_heads(sb_q, SB_HEADS), _to_heads(sb_k, SB_HEADS),
                                     _to_heads(sb_v, SB_HEADS))

    fq = _rms(_to_heads(fx_q, FOX_HEADS)) * g_qk[0]
    fk = _rms(_to_heads(fx_k, FOX_HEADS)) * g_qk[1]
    log_f = jax.nn.log_sigmoid(fx_f.astype(jnp.float32) + b_fgate.astype(jnp.float32))
    y_fox = _forgetting_attention(fq, fk, _to_heads(fx_v, FOX_HEADS), log_f.transpose(0, 2, 1))

    y = jnp.concatenate([_rms(y_lru), _rms(y_sb), _rms(y_fox)], axis=-1) * g_mix_out
    return y @ w_out

def second_inputs(seed: int = 0) -> dict:
    key = jax.random.key(seed)
    ks = jax.random.split(key, 20)
    f32 = jnp.float32
    nrm = lambda k, shape, s: jax.random.normal(k, shape, f32) * s
    x = jax.random.normal(ks[0], (BATCH, SEQ, D_MODEL), f32)
    c = jax.random.normal(ks[1], (BATCH, D_MODEL), f32)
    w_ada = nrm(ks[2], (DEPTH_2, D_MODEL, N_SUB * 3 * D_MODEL), 0.1 * D_MODEL ** -0.5)
    b_ada = nrm(ks[3], (DEPTH_2, N_SUB * 3 * D_MODEL), 0.01)
    g_norm = 1.0 + nrm(ks[4], (DEPTH_2, N_SUB, D_MODEL), 0.05)
    w_ffn_up = nrm(ks[5], (DEPTH_2, 2, D_MODEL, 2 * D_FF), D_MODEL ** -0.5)
    w_ffn_down = nrm(ks[6], (DEPTH_2, 2, D_FF, D_MODEL), D_FF ** -0.5)
    w_in = nrm(ks[7], (DEPTH_2, D_MODEL, N_IN), D_MODEL ** -0.5)
    b_fgate = 3.0 + nrm(ks[8], (DEPTH_2, FOX_HEADS), 0.1)
    conv_w = nrm(ks[9], (DEPTH_2, CONV_WIDTH, LRU_WIDTH), CONV_WIDTH ** -0.5)
    conv_b = nrm(ks[10], (DEPTH_2, LRU_WIDTH), 0.01)
    w_rgate = nrm(ks[11], (DEPTH_2, LRU_BLOCKS, HEAD_DIM, HEAD_DIM), HEAD_DIM ** -0.5)
    b_rgate = nrm(ks[12], (DEPTH_2, LRU_WIDTH), 0.01)
    w_igate = nrm(ks[13], (DEPTH_2, LRU_BLOCKS, HEAD_DIM, HEAD_DIM), HEAD_DIM ** -0.5)
    b_igate = nrm(ks[14], (DEPTH_2, LRU_WIDTH), 0.01)
    a_c = jax.random.uniform(ks[15], (DEPTH_2, LRU_WIDTH), f32, 0.9, 0.999)
    s = a_c ** (1.0 / LRU_C)
    lru_lambda = jnp.log(s) - jnp.log1p(-s)
    g_qk = 1.0 + nrm(ks[16], (DEPTH_2, 2, HEAD_DIM), 0.05)
    g_mix_out = 1.0 + nrm(ks[17], (DEPTH_2, D_MIX), 0.05)
    w_out = nrm(ks[18], (DEPTH_2, D_MIX, D_MODEL), D_MIX ** -0.5)
    return {"x": x, "c": c, "w_ada": w_ada, "b_ada": b_ada, "g_norm": g_norm,
            "w_ffn_up": w_ffn_up, "w_ffn_down": w_ffn_down, "w_in": w_in,
            "b_fgate": b_fgate, "conv_w": conv_w, "conv_b": conv_b,
            "w_rgate": w_rgate, "b_rgate": b_rgate, "w_igate": w_igate,
            "b_igate": b_igate, "lru_lambda": lru_lambda, "g_qk": g_qk,
            "g_mix_out": g_mix_out, "w_out": w_out}

def second_block(x, c, w_ada, b_ada, g_norm, w_ffn_up, w_ffn_down, w_in, b_fgate, conv_w,
              conv_b, w_rgate, b_rgate, w_igate, b_igate, lru_lambda, g_qk, g_mix_out, w_out):
    B = x.shape[0]
    c_act = jax.nn.silu(c)
    for l in range(DEPTH_2):
        mod = (c_act @ w_ada[l] + b_ada[l]).reshape(B, N_SUB, 3, D_MODEL)

        def norm_mod(h, j):
            shift = mod[:, j, 0][:, None, :]
            scale = mod[:, j, 1][:, None, :]
            return _rms(h) * g_norm[l, j] * (1.0 + scale) + shift

        def gate(j):
            return (1.0 + mod[:, j, 2])[:, None, :]

        x = x + 0.5 * gate(0) * _swiglu(norm_mod(x, 0), w_ffn_up[l, 0], w_ffn_down[l, 0])
        x = x + gate(1) * _mixer(norm_mod(x, 1), w_in[l], b_fgate[l], conv_w[l], conv_b[l],
                                 w_rgate[l], b_rgate[l], w_igate[l], b_igate[l],
                                 lru_lambda[l], g_qk[l], g_mix_out[l], w_out[l])
        x = x + 0.5 * gate(2) * _swiglu(norm_mod(x, 2), w_ffn_up[l, 1], w_ffn_down[l, 1])
    return x


def setup_inputs(seed=0):
    out = dict(first_inputs(seed))
    for name, value in second_inputs(seed + 1).items():
        if name != "x":
            out[name + "_2"] = value
    return out


def reference(
    x, mem, pre_mix_g, post_mix_g, w_in, attn_gn_g, ret_gn_g, w_out, pre_mem_g, post_mem_g,
    mem_norm_g, w_q_mem, w_kv_mem, w_o_mem, pre_ffn_g, post_ffn_g, w_gate_up, w_down, c_2,
    w_ada_2, b_ada_2, g_norm_2, w_ffn_up_2, w_ffn_down_2, w_in_2, b_fgate_2, conv_w_2, conv_b_2,
    w_rgate_2, b_rgate_2, w_igate_2, b_igate_2, lru_lambda_2, g_qk_2, g_mix_out_2, w_out_2,
):
    x = first_block(
        x, mem, pre_mix_g, post_mix_g, w_in, attn_gn_g, ret_gn_g, w_out, pre_mem_g, post_mem_g,
        mem_norm_g, w_q_mem, w_kv_mem, w_o_mem, pre_ffn_g, post_ffn_g, w_gate_up, w_down,
    )
    return second_block(
        x, c_2, w_ada_2, b_ada_2, g_norm_2, w_ffn_up_2, w_ffn_down_2, w_in_2, b_fgate_2,
        conv_w_2, conv_b_2, w_rgate_2, b_rgate_2, w_igate_2, b_igate_2, lru_lambda_2, g_qk_2,
        g_mix_out_2, w_out_2,
    )


_drawn_inputs = setup_inputs


def setup_inputs(seed=0):
    import zlib

    import numpy as np

    out = dict(_drawn_inputs(seed))
    spreads = {}
    factors = {'b_ada_2': 2.966,
     'b_fgate_2': 47.184,
     'conv_b_2': 5.288,
     'b_rgate_2': 63.413,
     'b_igate_2': 24.999,
     'g_qk_2': 5.613}
    for name, (base, spread) in spreads.items():
        noise = np.random.default_rng([zlib.crc32(name.encode()), seed]).standard_normal(out[name].shape)
        drawn = base * np.exp(spread * noise) if base else spread * noise
        out[name] = __import__('jax').numpy.asarray(drawn.astype(out[name].dtype))
    for name, factor in factors.items():
        out[name] = (out[name] * factor).astype(out[name].dtype)
    return out
```

```python
from collections import deque
from contextlib import ExitStack

import numpy as np
import concourse.bass as bass
from concourse import mybir

F32 = mybir.dt.float32
F32R = mybir.dt.float32r
ALU = mybir.AluOpType
ACT = mybir.ActivationFunctionType
AX = mybir.AxisListType

D = 1024
S = 512
KT = 8
TT = 4
NMEM = 256
FF = 2816
HALF = 11
RMS_EPS = 1e-6
GN_EPS = 1e-5
NEG = -1e30

C_ID, C_TRI, C_NT, C_NONE, C_SADD, C_CADD, C_SMUL, C_PA, C_PR, C_SEL, C_ONE = (
    0, 128, 640, 768, 896, 1024, 1152, 1280, 1408, 1536, 1538)
CB_W = 1540
T_MASK, T_ROPE, T_DEC = 0, 512, 512 + 4 * 512
CT_W = T_DEC + 4 * 512


def const_tables():
    p = np.arange(128)[:, None]
    c = np.arange(128)[None, :]
    cb = np.zeros((128, CB_W), np.float32)
    cb[:, C_ID:C_ID + 128] = (p == c)
    cb[:, C_TRI:C_TRI + 512] = (p <= np.arange(512)[None, :])
    cb[:, C_NT:C_NT + 128] = -1.0 * (p >= c)
    cb[:, C_NONE:C_NONE + 128] = -1.0
    cb[:, C_SADD:C_SADD + 128] = np.where(p >= c, NEG, 0.0)
    cb[:, C_CADD:C_CADD + 128] = np.where(c > p, NEG, 0.0)
    cb[:, C_SMUL:C_SMUL + 128] = (p < c)
    i = c % 64
    partner = np.where(i < 8, c + 8, np.where(i < 16, c - 8, -1))
    cb[:, C_PA:C_PA + 128] = (p == partner)
    cb[:, C_PR:C_PR + 128] = (p == (c + 64) % 128)
    cb[:, C_SEL] = (np.arange(128) < 64)
    cb[:, C_SEL + 1] = (np.arange(128) >= 64)
    cb[:, C_ONE:C_ONE + 2] = 1.0

    ct = np.zeros((128, CT_W), np.float32)
    n = np.arange(512)
    delta = 128 * (3 - n[None, :] // 128) + p - n[None, :] % 128
    count = ((delta >= 0) & (delta <= 128)).astype(int) + ((delta >= 0) & (delta % 4 == 0)) \
        + ((delta >= 0) & (delta % 16 == 0))
    ct[:, T_MASK:T_MASK + 512] = np.where(count > 0, 8.0 * np.log(np.maximum(count, 1)), NEG)
    pos = np.arange(512, dtype=np.float32)
    for at, dim, theta, width in ((0, 16, 500000.0, 64), (2, 128, 10000.0, 128)):
        inv = np.float32(theta) ** (-(np.arange(0, dim, 2, dtype=np.float32) / np.float32(dim)))
        ang = (pos[None, :] * inv.astype(np.float32)[:, None]).astype(np.float32)
        cos, sin = np.cos(ang), np.sin(ang)
        h = dim // 2
        cr = np.ones((width, 512), np.float32)
        sr = np.zeros((width, 512), np.float32)
        cr[:h], cr[h:dim] = cos, cos
        sr[:h], sr[h:dim] = -sin, sin
        ct[:, T_ROPE + at * 512:T_ROPE + (at + 1) * 512] = np.tile(cr, (128 // width, 1))
        ct[:, T_ROPE + (at + 1) * 512:T_ROPE + (at + 2) * 512] = np.tile(sr, (128 // width, 1))
    for h in range(4):
        log_g = np.log(1.0 - 2.0 ** (-5.0 - h))
        rel = n[None, :] - p
        ct[:, T_DEC + h * 512:T_DEC + (h + 1) * 512] = np.where(
            rel >= 0, np.exp(log_g * np.maximum(rel, 0)) * 128.0 ** -0.5, 0.0)
    return cb, ct


def op_matmul(e, *a, **k):
    return e.matmul(*a, **k)


def op_transpose(e, *a, **k):
    return e.transpose(*a, **k)


def op_activation(e, *a, **k):
    return e.activation(*a, **k)


def op_tensor_tensor(e, *a, **k):
    return e.tensor_tensor(*a, **k)


def op_tensor_scalar(e, *a, **k):
    return e.tensor_scalar(*a, **k)


def op_scalar_tensor_tensor(e, *a, **k):
    return e.scalar_tensor_tensor(*a, **k)


def op_tensor_tensor_scan(e, *a, **k):
    return e.tensor_tensor_scan(*a, **k)


def op_tensor_tensor_reduce(e, *a, **k):
    return e.tensor_tensor_reduce(*a, **k)


def op_tensor_reduce(e, *a, **k):
    return e.tensor_reduce(*a, **k)


def op_tensor_copy(e, *a, **k):
    return e.tensor_copy(*a, **k)


def op_reciprocal(e, *a, **k):
    return e.reciprocal(*a, **k)


def op_memset(e, *a, **k):
    return e.memset(*a, **k)


def op_dma_start(e, *a, **k):
    return e.dma_start(*a, **k)


class Queues:

    def __init__(self):
        self.todo = {e: [] for e in ("sp", "pe", "act", "dve", "pool")}
        self.count = {}

    def put(self, engine, op, after, sem, by, args, kw):
        flat = []
        stack = list(after)
        while stack:
            t = stack.pop()
            if isinstance(t, list):
                stack += t
            elif t is not None:
                flat.append(t)
        if sem is not None:
            self.count[sem] = self.count.get(sem, 0) + by
        self.todo[engine].append((op, args, kw, flat, sem, by))
        return (sem, self.count[sem]) if sem is not None else None

    def pe(self, op, after, *args, mark=False, **kw):
        return self.put("pe", op, after, "pe" if mark else None, 1, args, kw)

    def act(self, op, after, *args, **kw):
        return self.put("act", op, after, "act", 1, args, kw)

    def dve(self, op, after, *args, **kw):
        return self.put("dve", op, after, "dve", 1, args, kw)

    def pool(self, op, after, *args, **kw):
        return self.put("pool", op, after, "pool", 1, args, kw)

    def dma(self, sem, op, after, *args, engine="sp", **kw):
        return self.put(engine, op, after, sem, 16, args, kw)

    def last(self, *engines):
        return [(e, self.count[e]) for e in engines if self.count.get(e)]

    def run(self, name, engine, sems):
        seen = {}
        for op, args, kw, after, sem, by in self.todo[name]:
            need = {}
            for s, v in after:
                need[s] = max(need.get(s, 0), v)
            for s in sorted(need):
                if seen.get(s, 0) < need[s]:
                    engine.wait_ge(sems[s], need[s])
                    seen[s] = need[s]
            ins = op(engine, *args, **kw)
            if sem is not None:
                ins.then_inc(sems[sem], by)


def build(nc, I, out):
    Q = Queues()
    base = (nc.sbuf_base + 127) // 128 * 128
    TB = 2048

    def at(name, off_bytes, shape, dt=F32):
        return nc.alloc_sbuf_tensor_at(name, shape, dt, offset=base + off_bytes)

    X = at("X", 0, [128, KT, S])
    HH = at("HH", 8 * TB, [128, KT, S], F32R)
    HL = at("HL", 16 * TB, [128, KT, S], F32R)
    NS, NW, SLAB = 3, 3, 2048
    WS = at("WS", 24 * TB, [128, NS, SLAB])
    WH = at("WH", 36 * TB, [128, NW, SLAB], F32R)
    WL = at("WL", 48 * TB, [128, NW, SLAB], F32R)
    coff = [60 * TB]

    def const(name, shape, dt=F32):
        t = at(name, coff[0], shape, dt)
        coff[0] += (4 * int(np.prod(shape[1:])) + 31) // 32 * 32
        assert coff[0] <= 66 * TB
        return t

    CB = const("CB", [128, CB_W])
    ACC = const("ACC", [128, 512])
    PC = const("PC", [128, 340])
    MOD = const("MOD", [128, 2, 72])
    MA = const("MA", [128, 24])
    MG = const("MG", [128, 24])
    NSM = 6
    SD = const("SD", [128, NSM, 16])
    RC = const("RC", [128, NSM, 16])
    CC = const("CC", [128, 8])
    CS = const("CS", [128, 8])
    EPS = const("EPS", [128, 4])
    SM = const("SM", [128, 4, 4])
    LAM = const("LAM", [128, 4, 4])
    FG = const("FG", [128, 6, 16])
    BF = const("BF", [128, 4])

    R0 = 66

    def region(name, t, shape, dt=F32):
        n = 4 * int(np.prod(shape[1:]))
        assert (R0 + t) * TB + n <= 103 * TB
        return at(name, int((R0 + t) * TB), shape, dt)

    SQ = region("SQ", 33, [128, 2, S])
    TM = region("TM", 35, [128, 2, S])
    XTM = region("XTM", 0, [128, TT, D])
    PR = region("PR", 20, [128, 5, 128])
    AQ = region("AQ", 0, [128, 4, S])
    AK = region("AK", 4, [128, 4, S])
    RG = region("RG", 4, [128, 4, S])
    AV = region("AV", 8, [128, TT, 512])
    RQ = region("RQ", 12, [128, 4, S])
    RK = region("RK", 16, [128, 4, S])
    RV = region("RV", 20, [128, TT, 512])
    MSK = region("MSK", 24, [128, 512])
    ROPE = region("ROPE", 25, [128, 4, 512])
    DEC = region("DEC", 25, [128, 4, 512])
    SS = region("SS", 29, [128, 2, S])
    PT = region("PT", 31, [128, 2, S])
    MH = region("MH", 0, [128, KT, NMEM], F32R)
    ML = region("ML", 4, [128, KT, NMEM], F32R)
    KM = region("KM", 8, [128, KT, NMEM])
    VM = region("VM", 12, [128, 2, D])
    Y = region("Y", 16, [128, KT, S])
    XQ = region("XQ", 16, [128, KT, S])
    XS = region("XS", 24, [128, 2, S])
    XP = region("XP", 26, [128, 2, S])
    MTM = region("MTM", 28, [128, 2, D])
    GH = region("GH", 0, [128, HALF, S], F32R)
    GL = region("GL", 11, [128, HALF, S], F32R)
    Y1 = region("Y1", 22, [128, KT, S])
    SG = region("SG", 30, [128, 2, S])
    FXQ = region("FXQ", 0, [128, 2, S])
    FXK = region("FXK", 2, [128, 2, S])
    FXV = region("FXV", 4, [128, TT, 256])
    SBQ = region("SBQ", 6, [128, 2, S])
    SBK = region("SBK", 8, [128, 2, S])
    SBV = region("SBV", 10, [128, TT, 256])
    LA = region("LA", 12, [128, 4, S])
    LB = region("LB", 16, [128, 4, S])
    LC = region("LC", 20, [128, 4, S])
    FB = region("FB", 20, [128, 4, S])
    LD = region("LD", 24, [128, 4, S])
    BD = region("BD", 24, [128, 2, 4, 128])
    FS = region("FS", 28, [128, 2, S])
    FP = region("FP", 30, [128, 2, S])
    SP = region("SP", 28, [128, 1280])
    ST = region("ST", 31, [128, S])
    SW = region("SW", 32, [128, S])
    LG = region("LG", 2, [128, 4, S])
    OT = region("OT", 0, [128, TT, D])

    PB = [nc.alloc_psum_tensor(f"PB{i}", [128, 512], F32) for i in range(8)]
    free = {b: None for b in range(8)}
    ring = deque([0, 1, 2, 3])

    def take():
        b = ring.popleft()
        ring.append(b)
        return b

    ident = CB[:, C_ID:C_ID + 128]

    def f(ap):
        return ap.bitcast(F32)

    def mm(out_, l, r, start, stop, *after, mark=False, skip=False):
        return Q.pe(op_matmul, (*after,), out_, l, r, start=start, stop=stop, skip_group_check=skip, mark=mark)

    side = deque()
    later = []

    def pump(n=1):
        for x in later:
            x[0] -= 1
        while later and later[0][0] <= 0:
            later.pop(0)[1]()
        for _ in range(n):
            while side:
                try:
                    next(side[0])
                    break
                except StopIteration:
                    side.popleft()

    def drain():
        while later or side:
            pump()

    def defer(fn, n=2):
        later.append([n, fn])

    credit = [0.0]

    def run(gen, rate=1.0):
        for _ in gen:
            credit[0] += rate
            n = int(credit[0])
            credit[0] -= n
            pump(n)

    def pipeline(n, stages, lags):
        at_ = [sum(lags[:s + 1]) for s in range(len(stages))]
        for t in range(n + at_[-1]):
            for s in reversed(range(len(stages))):
                i = t - at_[s]
                if 0 <= i < n:
                    stages[s](i)
            yield

    items = []

    def w_cols(w, c0, n, kt=KT):
        v = w.rearrange("(k p) c -> p k c", p=128)
        items.append(("w", v[:, 0:kt, c0:c0 + n], (kt, n)))

    def w_rows(w, k0, kn, c0, n):
        v = w.rearrange("(k p) c -> p k c", p=128)
        items.append(("w", v[:, k0:k0 + kn, c0:c0 + n], (kn, n)))

    def w_up(w, m):
        v = w.rearrange("(k p) (t c) -> p k t c", p=128, t=2)
        items.append(("w2", v[:, :, :, m * 128:(m + 1) * 128], (KT, 2, 128)))

    def plan_ffn(up, down):
        for half in range(2):
            for m in range(HALF):
                w_up(up, half * HALF + m)
            for k0, kn in ((0, 4), (4, 4), (8, 3)):
                w_rows(down, half * HALF + k0, kn, 0, 512)
            for m in range(4, 8):
                w_rows(down, half * HALF, HALF, m * 128, 128)

    def plan():
        w_in = I["w_in"][0]
        for c in range(14):
            w_cols(w_in, c * 256, 256)
        for c in range(4):
            w_cols(I["w_out"][0], c * 256, 256)
        for c in range(8):
            w_cols(I["w_kv_mem"][0], c * 256, 256)
        for c in range(4):
            w_cols(I["w_q_mem"][0], c * 256, 256)
        for c in range(4):
            w_cols(I["w_o_mem"][0], c * 256, 256)
        plan_ffn(I["w_gate_up"][0], I["w_down"][0])
        for l in range(2):
            plan_ffn(I["w_ffn_up_2"][l, 0], I["w_ffn_down_2"][l, 0])
            w2 = I["w_in_2"][l]
            w_cols(w2, 2560, 4)
            for c0 in (1792, 2048, 2304, 0, 256, 1024, 1280, 1536, 512, 768):
                w_cols(w2, c0, 256)
            for c in range(4):
                w_cols(I["w_out_2"][l], c * 256, 256)
            plan_ffn(I["w_ffn_up_2"][l, 1], I["w_ffn_down_2"][l, 1])

    plan()
    weights = items
    items = []
    ada = []
    for l in range(2):
        v = I["w_ada_2"][l].rearrange("(p k) n -> p k n", k=8)
        for n in range(18):
            for kh in range(2):
                ada.append(("ada", v[:, 4 * kh:4 * kh + 4, n * 512:(n + 1) * 512], (l, n, kh)))
    n1 = 14 + 4 + 8 + 4 + 4 + 36
    order = []
    ai = 0
    for wi, w in enumerate(weights):
        order.append(w)
        due = 36 * min(1.0, (wi + 1) / (n1 - 6)) if wi < n1 - 6 else 36 + 36 * min(1.0, (wi - n1 + 7) / 76)
        while ai < min(due, 72) - 1e-9:
            order.append(ada[ai])
            ai += 1
    order += ada[ai:]

    ws_free = [None] * NS
    ws_in = [None] * NS
    wh_free = [None] * NW
    ready = {}
    pos = {"dma": 0, "use": 0, "w": 0, "slab": 0}

    def emit_dma():
        i = pos["dma"]
        if i >= len(order):
            return
        pos["dma"] += 1
        kind, src, dims = order[i]
        s = i % NS
        if kind == "ada":
            dst = WS[:, s, :].rearrange("p (k n) -> p k n", k=4)
        elif kind == "w2":
            dst = WS[:, s, 0:2048].rearrange("p (k t c) -> p k t c", k=KT, t=2)
        else:
            dst = WS[:, s, 0:dims[0] * dims[1]].rearrange("p (k c) -> p k c", k=dims[0])
        if kind == "w2":
            for t in range(2):
                ws_in[s] = Q.dma(f"ws{s}", op_dma_start, (ws_free[s],), dst[:, :, t, :], src[:, :, t, :])
        else:
            ws_in[s] = Q.dma(f"ws{s}", op_dma_start, (ws_free[s],), dst, src)

    pend = []
    acc_free = [None]
    mod_tok = [None, None]

    def flush_ada():
        while pend:
            l, n, tok = pend.pop(0)
            b = take()
            for q in range(4):
                t = mm(PB[b][:, q:q + 1], ACC[:, q * 128:(q + 1) * 128], CB[:, C_ONE:C_ONE + 1],
                       True, True, free[b], tok, cb_in, mark=(q == 3))
            acc_free[0] = t
            bias = PC[:, 196 + 72 * l + 4 * n:196 + 72 * l + 4 * n + 4]
            free[b] = Q.dve(op_tensor_tensor, (t, pc_tok,), MOD[:, l, 4 * n:4 * n + 4], PB[b][:, 0:4], bias, ALU.add)
            mod_tok[l] = free[b]

    def emit_use():
        i = pos["use"]
        pos["use"] += 1
        kind, src, dims = order[i]
        s = i % NS
        if kind == "ada":
            l, n, kh = dims
            if kh == 0:
                flush_ada()
            t = None
            for q in range(4):
                w = WS[:, s, q * 512:(q + 1) * 512]
                c = CS[:, 4 * kh + q:4 * kh + q + 1]
                if kh == 0 and q == 0:
                    t = Q.dve(op_tensor_scalar, (ws_in[s], acc_free[0], cs_tok,), ACC[:, :], w, c, None, ALU.mult)
                else:
                    t = Q.dve(op_scalar_tensor_tensor, (ws_in[s], Q.last("dve"),), out=ACC[:, :], in0=w, scalar=c, in1=ACC[:, :], op0=ALU.mult, op1=ALU.add)
            ws_free[s] = t
            if kh == 1:
                pend.append((l, n, t))
        else:
            j = pos["w"]
            pos["w"] += 1
            n = int(np.prod(dims))
            h = j % NW
            hi = Q.act(op_activation, (ws_in[s], wh_free[h],), WH[:, h, 0:n], WS[:, s, 0:n], ACT.Copy)
            lo = Q.dve(op_tensor_tensor, (ws_in[s], hi, wh_free[h],), WL[:, h, 0:n], WS[:, s, 0:n], f(WH[:, h, 0:n]), ALU.subtract)
            ws_free[s] = lo
            ready[j] = [hi, lo]
        emit_dma()

    def use_until(j):
        while pos["w"] <= j and pos["use"] < len(order):
            emit_use()

    def next_slab():
        i = pos["slab"]
        pos["slab"] += 1
        use_until(i)
        use_until(i + 2)
        flush = [x for x in pend]
        if flush:
            defer(flush_ada, 3)
        kind, _, dims = weights[i]
        h = i % NW
        n = int(np.prod(dims))
        if kind == "w2":
            vh = WH[:, h, 0:n].rearrange("p (k t c) -> p k t c", k=dims[0], t=2)
            vl = WL[:, h, 0:n].rearrange("p (k t c) -> p k t c", k=dims[0], t=2)
        else:
            vh = WH[:, h, 0:n].rearrange("p (k c) -> p k c", k=dims[0])
            vl = WL[:, h, 0:n].rearrange("p (k c) -> p k c", k=dims[0])
        return i, vh, vl, ready[i]

    def done_slab(i, tok):
        wh_free[i % NW] = tok

    def mm3_w(out_, wh, wl, xh, xl, start, stop, *after, mark=False, skip=False):
        mm(out_, wh, xh, start, False, *after, skip=skip)
        mm(out_, wh, xl, False, False, skip=skip)
        return mm(out_, wl, xh, False, stop, mark=mark, skip=skip)

    def mm3_x(out_, xh, xl, wh, wl, start, stop, *after, mark=False):
        mm(out_, xh, wh, start, False, *after)
        mm(out_, xh, wl, False, False)
        return mm(out_, xl, wh, False, stop, mark=mark)

    def proj_fm(ntile, xh, xl, xt, evac, kouter, ntok=S, m0=0, unit=2):
        i, vh, vl, wt = next_slab()
        banks = [take() for _ in range(ntile)]
        seq = [(k, m) for k in range(KT) for m in range(ntile)] if kouter else \
              [(k, m) for m in range(ntile) for k in range(KT)]
        for c, (k, m) in enumerate(seq):
            first, last = k == 0, k == KT - 1
            t = mm3_w(PB[banks[m]][:, 0:ntok], vh[:, k, m * 128:(m + 1) * 128],
                      vl[:, k, m * 128:(m + 1) * 128], xh[:, k, 0:ntok], xl[:, k, 0:ntok], first, last,
                      wt, xt[k], free[banks[m]] if first else None, mark=last)
            if last:
                free[banks[m]] = evac(m0 + m, PB[banks[m]][:, 0:ntok], t)
                done_slab(i, t)
            if c % unit == unit - 1:
                yield

    def proj_tm(ntok, xh, xl, xt, evac):
        i, vh, vl, wt = next_slab()
        for b2 in range(ntok // 2):
            b = take()
            for u in range(2):
                j = 2 * b2 + u
                for k in range(KT):
                    t = mm3_x(PB[b][:, u * 256:(u + 1) * 256], xh[:, k, j * 128:(j + 1) * 128],
                              xl[:, k, j * 128:(j + 1) * 128], vh[:, k, :], vl[:, k, :],
                              k == 0, k == KT - 1, wt, xt[k], free[b] if k == 0 and u == 0 else None,
                              mark=(k == KT - 1))
                    if k % 4 == 3:
                        yield
            done_slab(i, t)
            free[b] = evac(b2, PB[b][:, :].rearrange("p (u c) -> p u c", u=2), t)

    small = [0]

    def stat(tile, b, sel, ng, first, tok, col=0, ntok=TT, last=True):
        for j in range(ntok):
            t = mm(PB[b][:, col + j * ng:col + (j + 1) * ng], tile[:, j * 128:(j + 1) * 128], sel,
                   first and j == 0, last and j == ntok - 1, tok, cb_in,
                   free[b] if first and j == 0 else None, mark=(j == ntok - 1), skip=True)
        return t

    def root(b, n, scale, eps, tok):
        s = small[0] % NSM
        small[0] += 1
        a = Q.act(op_activation, (tok, eps_tok, Q.last("dve"),), SD[:, s, 0:n], PB[b][:, 0:n], ACT.Sqrt, bias=EPS[:, eps:eps + 1],
                                         scale=scale)
        free[b] = a
        r = Q.dve(op_reciprocal, (a, Q.last("pe"),), RC[:, s, 0:n], SD[:, s, 0:n])
        return s, r

    def spread(b, s, ng, tok, ntok=TT):
        w = 128 // ng
        for j in range(ntok):
            for g in range(ng):
                c = j * ng + g
                t = mm(PB[b][g * w:(g + 1) * w, j * 128:(j + 1) * 128], RC[:, s, c:c + 1].to_broadcast([128, w]),
                       ident, True, True, tok, free[b] if j == 0 else None,
                       mark=(j == ntok - 1 and g == ng - 1))
        return t

    one = CB[:, C_ONE:C_ONE + 1]
    x_tok = [None] * KT
    sq_free = [None, None]
    h_tok = [None] * KT
    sqn = [0]

    def square(src, tok):
        i = sqn[0] % 2
        sqn[0] += 1
        t = Q.act(op_activation, (tok, sq_free[i],), SQ[:, i, :], src, ACT.Square)
        return i, t

    def watch(tile, toks, sqs, least=1):
        for m in range(KT):
            while len(toks) <= max(m, least - 1):
                yield
            i, sq = square(tile(m), toks[m])
            yield
            sqs.append(add_stat(i, sq, 6, m == 0, m == KT - 1))

    def add_stat(i, t, b, first, last):
        u = stat(SQ[:, i, :], b, one, 1, first, t, last=last)
        sq_free[i] = u
        return u

    def make_h(a_col, s_col, rb, rt, par):
        for k in range(KT):
            i = k % 2
            t = Q.dve(op_scalar_tensor_tensor, (rt, x_tok[k], par, Q.last("act") if k == 0 else None, Q.last("dve") if k == 0 else None,), out=TM[:, i, :], in0=X[:, k, :], scalar=a_col(k), in1=PB[rb][:, :], op0=ALU.mult,
                op1=ALU.mult)
            if k == KT - 1:
                free[rb] = t
            if s_col is None:
                hi = Q.act(op_activation, (t,), HH[:, k, :], TM[:, i, :], ACT.Copy)
                lo = Q.dve(op_tensor_tensor, (t, hi,), HL[:, k, :], TM[:, i, :], f(HH[:, k, :]), ALU.subtract)
            else:
                hi = Q.act(op_activation, (t, par,), HH[:, k, :], TM[:, i, :], ACT.Identity,
                                                            bias=s_col(k))
                lo = Q.dve(op_scalar_tensor_tensor, (t, hi,), out=HL[:, k, :], in0=TM[:, i, :], scalar=s_col(k), in1=f(HH[:, k, :]), op0=ALU.add,
                    op1=ALU.subtract)
            h_tok[k] = [hi, lo]
            yield

    def rms_h(tok, a_col, s_col, par, sb=6, rb=5):
        s, r = root(sb, TT, 1.0 / D, 0, tok)
        yield
        rt = spread(rb, s, 1, r)
        yield from make_h(a_col, s_col, rb, rt, par)

    def split_into(k, src, tok):
        hi = Q.act(op_activation, (tok,), HH[:, k, :], src, ACT.Copy)
        lo = Q.dve(op_tensor_tensor, (tok, hi,), HL[:, k, :], src, f(HH[:, k, :]), ALU.subtract)
        h_tok[k] = [hi, lo]

    x_in = [Q.dma(f"x{j}", op_dma_start, (), XTM[:, j, :], I["x"][0, j * 128:(j + 1) * 128, :])
            for j in range(2)]
    cb_in = Q.dma("cb", op_dma_start, (), CB[:, :], I["c_b"], engine="act")
    x_in += [Q.dma(f"x{j}", op_dma_start, (), XTM[:, j, :], I["x"][0, j * 128:(j + 1) * 128, :])
             for j in range(2, 4)]

    z_tok = Q.pool(op_memset, (), PR[:, :, :], 0.0)
    pr = []
    at_row = 0

    def rows(tile, r0, v, w=128):
        pr.append(Q.dma("pr", op_dma_start, (z_tok,), PR[r0:r0 + v.shape[0], tile, 0:v.shape[1]], v, engine="act"))

    gains = {}
    for name in ("pre_mix_g", "post_mix_g", "pre_mem_g", "post_mem_g", "mem_norm_g", "pre_ffn_g",
                 "post_ffn_g"):
        rows(0, at_row, I[name][0].rearrange("(a b) -> a b", b=128))
        gains[name] = at_row
        at_row += 8
    for name in ("attn_gn_g", "ret_gn_g"):
        rows(0, at_row, I[name][0].rearrange("(a b) -> a b", b=128))
        gains[name] = at_row
        at_row += 4
    P2 = {}
    for l in range(2):
        at_row = 0

        def add(name, v, n):
            nonlocal at_row
            rows(1 + l, at_row, v)
            P2[(name, l)] = 64 + 66 * l + at_row
            at_row += n

        add("g_norm", I["g_norm_2"][l].rearrange("j (a b) -> (j a) b", b=128), 24)
        add("conv_w", I["conv_w_2"][l].rearrange("j (a b) -> (j a) b", b=128), 16)
        for nm in ("conv_b_2", "b_rgate_2", "b_igate_2", "lru_lambda_2"):
            add(nm, I[nm][l].rearrange("(a b) -> a b", b=128), 4)
        add("g_mix", I["g_mix_out_2"][l].rearrange("(a b) -> a b", b=128), 8)
        for u in range(2):
            pr.append(Q.dma("pr", op_dma_start, (z_tok,), PR[at_row:at_row + 2, 1 + l, 64 * u:64 * u + 64], I["g_qk_2"][l], engine="act"))
        P2[("g_qk", l)] = 64 + 66 * l + at_row
        rows(3 + l, 0, I["b_ada_2"][l].rearrange("(a b) -> a b", b=128))
    pr_tok = pr[-1]
    cc_in = Q.dma("cc", op_dma_start, (), CC[:, :], I["c_2"].rearrange("o (p k) -> p (o k)", k=8), engine="act")
    msk_in = Q.dma("ct", op_dma_start, (), MSK[:, :], I["c_t"][:, T_MASK:T_MASK + 512], engine="act")
    rope_in = Q.dma("ct", op_dma_start, (), ROPE[:, :, :], I["c_t"][:, T_ROPE:T_DEC].rearrange("p (a b) -> p a b", a=4), engine="act")
    for _ in range(NS):
        emit_dma()

    e0 = Q.dve(op_memset, (), EPS[:, 0:1], RMS_EPS)
    e0 = Q.dve(op_memset, (), EPS[:, 1:2], GN_EPS)
    eps_tok = Q.dve(op_memset, (), EPS[:, 2:3], 1.0)

    for m in range(KT):
        b = take()
        for j in range(TT):
            t = Q.pe(op_transpose, (x_in[j], cb_in, free[b] if j == 0 else None,), PB[b][:, j * 128:(j + 1) * 128], XTM[:, j, m * 128:(m + 1) * 128], ident, mark=(j == TT - 1))
        if m % 2:
            x_tok[m] = free[b] = Q.act(op_activation, (t,), X[:, m, :], PB[b][:, :], ACT.Copy)
        else:
            x_tok[m] = free[b] = Q.dve(op_tensor_copy, (t,), X[:, m, :], PB[b][:, :])
    for m in range(KT):
        i, t = square(X[:, m, :], x_tok[m])
        st = add_stat(i, t, 6, m == 0, m == KT - 1)

    widths = [(0, 0, 64), (1, 64, 66), (2, 130, 66), (3, 196, 72), (4, 268, 72)]
    b = 4
    for tl, c0, w in widths:
        t = Q.pe(op_transpose, (pr_tok, z_tok, cb_in, free[4],), PB[4][:, 0:128], PR[:, tl, :], ident, mark=True)
        pc_tok = free[4] = Q.dve(op_tensor_copy, (t,), PC[:, c0:c0 + w], PB[4][:, 0:w])
    cs_tok = Q.act(op_activation, (cc_in,), CS[:, :], CC[:, :], ACT.Silu)

    def col(c):
        return PC[:, c:c + 1]

    def gcol(name):
        return lambda k: col(gains[name] + k)

    side.append(rms_h(st, gcol("pre_mix_g"), None, pc_tok))
    drain()

    rp = {}
    rope_n = [0]
    tm_free = [None, None]

    def rope_out(dst, table, perm, banks, key):
        def evac(m, ps, t):
            i = rope_n[0] % 2
            rope_n[0] += 1
            c = Q.act(op_activation, (t, sq_free[i], Q.last("dve"),), SQ[:, i, :], ps, ACT.Copy)
            bk = banks[i % len(banks)]

            def rest():
                p = mm(PB[bk][:, :], CB[:, perm:perm + 128], SQ[:, i, :], True, True, c, free[bk], mark=True)
                u = Q.dve(op_tensor_tensor, (c, rope_in, tm_free[i],), TM[:, i, :], SQ[:, i, :], ROPE[:, table, :], ALU.mult)
                v = Q.dve(op_tensor_tensor, (p,), dst[:, m, :], PB[bk][:, :], ROPE[:, table + 1, :],
                                                    ALU.mult)
                free[bk] = v
                sq_free[i] = [u, p]
                rp[key, m] = Q.dve(op_tensor_tensor, (u, v,), dst[:, m, :], dst[:, m, :], TM[:, i, :],
                                                             ALU.add)
                tm_free[i] = rp[key, m]
            defer(rest, 2)
            return c
        return evac

    for c in range(2):
        run(proj_fm(2, HH, HL, h_tok, rope_out(AQ, 0, C_PA, (4, 5), "aq"), c == 0, m0=2 * c))
    for c in range(2):
        run(proj_fm(2, HH, HL, h_tok, rope_out(AK, 0, C_PA, (4, 5), "ak"), False, m0=2 * c))

    def tm_out(dst, c, key):
        def evac(b2, ps, t):
            tk = Q.act(op_activation, (t,), dst[:, 2 * b2:2 * b2 + 2, c * 256:(c + 1) * 256], ps, ACT.Copy)
            rp[key, c, b2] = tk
            return tk
        return evac

    for c in range(2):
        run(proj_tm(TT, HH, HL, h_tok, tm_out(AV, c, "av")))
    pump(3)

    sm_free = [None] * 4

    def soft_attention(n_heads, score, n_of, v_of, ss, pt, finish, key, obank=(7,), vt=None, ptb=6):
        st_ = {}
        ss_free = [None, None]
        pt_free = [None, None]

        def s0(it):
            h, i = divmod(it, TT)
            sb = 4 + it % 2
            st_[it] = {"s": score(h, i, sb, ss[:, it % 2, :], SM[:, it % 4, :], ss_free[it % 2],
                                  sm_free[it % 4])}

        def s1(it):
            h, i = divmod(it, TT)
            n = n_of(i)
            blocks = n // 128
            for j in range(blocks):
                t = Q.pe(op_transpose, (st_[it]["s"], free[ptb] if j == 0 else None,), PB[ptb][:, j * 128:(j + 1) * 128],
                                                    ss[:, it % 2, j * 128:(j + 1) * 128], ident, mark=(j == blocks - 1))
            ss_free[it % 2] = t
            c = Q.act(op_activation, (t, pt_free[it % 2],), pt[:, it % 2, 0:n], PB[ptb][:, 0:n], ACT.Copy)
            free[ptb] = c
            st_[it]["p"] = c

        def s2(it):
            h, i = divmod(it, TT)
            pt_free[it % 2] = finish(h, i, pt[:, it % 2, :], st_.pop(it)["p"], n_of(i) // 128)

        yield from pipeline(n_heads * TT, [s0, s1, s2], [0, 1, 1])

    def norm_rows(sstile, sm, n, tok):
        r = Q.dve(op_reciprocal, (tok,), sm[:, 3:4], sm[:, 2:3])
        return Q.dve(op_tensor_scalar, (tok, r,), sstile[:, 0:n], sstile[:, 0:n], sm[:, 3:4], None, ALU.mult)

    def dil_score(h, i, sb, sst, sm, f1, f2):
        n = 128 * (i + 1)
        po, m = 64 * (h % 2), h // 2
        t = mm(PB[sb][:, 0:n], AQ[po:po + 64, m, i * 128:(i + 1) * 128], AK[po:po + 64, m, 0:n], True, True,
               rp["aq", m], rp["ak", m], free[sb], mark=True)
        a = Q.dve(op_tensor_tensor_reduce, (t, msk_in, f1, f2,), out=sst[:, 0:n], in0=PB[sb][:, 0:n], in1=MSK[:, 512 - n:512], scale=0.125, scalar=-3e38,
            op0=ALU.add, op1=ALU.max, accum_out=sm[:, 0:1])
        free[sb] = a
        g = Q.dve(op_tensor_scalar, (a,), sm[:, 1:2], sm[:, 0:1], -1.0, None, ALU.mult)
        x = Q.act(op_activation, (g,), sst[:, 0:n], sst[:, 0:n], ACT.Exp, bias=sm[:, 1:2],
                                         accum_out=sm[:, 2:3])
        return norm_rows(sst, sm, n, x)

    an = {}

    def att_norm(m, src, gain, key, dst=None):
        i, t = square(src[:, m, :], an[key, m])
        u = stat(SQ[:, i, :], 6, CB[:, C_SEL:C_SEL + 2], 2, True, t)
        sq_free[i] = u
        s, r = root(6, 2 * TT, 1.0 / 64, 0, u)
        yield
        rt = spread(6, s, 2, r)
        an[key, m] = free[6] = Q.dve(op_scalar_tensor_tensor, (rt, t, pc_tok, Q.last("dve"),), out=src[:, m, :], in0=src[:, m, :], scalar=gain, in1=PB[6][:, :], op0=ALU.mult, op1=ALU.mult)
        yield

    def head_pair_finish(v, vkeys, dst, key, cw):
        def finish(h, i, ptt, tok, blocks):
            po, m = 64 * (h % 2), h // 2
            for j in range(blocks):
                t = mm(PB[7][po:po + 64, i * 128:(i + 1) * 128], v[:, j, h * 64:(h + 1) * 64],
                       ptt[:, j * 128:(j + 1) * 128], j == 0, j == blocks - 1, tok,
                       [rp[k] for k in vkeys(h)], free[7] if h % 2 == 0 and i == 0 else None,
                       mark=(j == blocks - 1))
            if h % 2 == 1 and i == TT - 1:
                an[key, m] = free[7] = Q.act(op_activation, (t,), dst[:, m, :], PB[7][:, :], ACT.Copy)
            return t
        return finish

    def dil():
        yield from soft_attention(8, dil_score, lambda i: 128 * (i + 1), None, SS, PT,
                                  head_pair_finish(AV, lambda h: [("av", h // 4, 0), ("av", h // 4, 1)],
                                                   AQ, "a", None), "a")
        for m in range(4):
            yield from att_norm(m, AQ, col(gains["attn_gn_g"] + m), "a")

    side.append(dil())
    RATE = 0.8
    for c in range(2):
        run(proj_fm(2, HH, HL, h_tok, rope_out(RQ, 2, C_PR, (6,), "rq"), False, m0=2 * c), RATE)
    for c in range(2):
        run(proj_fm(2, HH, HL, h_tok, rope_out(RK, 2, C_PR, (6,), "rk"), False, m0=2 * c), RATE)
    for c in range(2):
        run(proj_tm(TT, HH, HL, h_tok, tm_out(RV, c, "rv")), RATE)
    drain()
    dec_in = Q.dma("dec", op_dma_start, (Q.last("dve"),), DEC[:, :, :], I["c_t"][:, T_DEC:CT_W].rearrange("p (a b) -> p a b", a=4), engine="act")

    def ret():
        st_ = {}
        ssf = [None, None]

        def s0(it):
            h, j = divmod(it, TT)
            n = S - 128 * j
            sb = 4 + it % 2
            t = mm(PB[sb][:, 0:n], RK[:, h, j * 128:(j + 1) * 128], RQ[:, h, j * 128:S], True, True,
                   rp["rq", h], rp["rk", h], free[sb], mark=True)
            free[sb] = st_[it] = Q.dve(op_tensor_tensor, (t, dec_in, ssf[it % 2],), SS[:, it % 2, 0:n], PB[sb][:, 0:n], DEC[:, h, 0:n], ALU.mult)

        def s1(it):
            h, j = divmod(it, TT)
            n = S - 128 * j
            t = mm(PB[7][:, j * 128:S], RV[:, j, h * 128:(h + 1) * 128], SS[:, it % 2, 0:n], j == 0, j == 3,
                   st_.pop(it), rp["rv", h // 2, 0], rp["rv", h // 2, 1], free[7] if j == 0 else None, mark=True)
            ssf[it % 2] = t
            if j == 3:
                rp["r", h] = free[7] = Q.act(op_activation, (t,), RQ[:, h, :], PB[7][:, :], ACT.Copy)

        yield from pipeline(16, [s0, s1], [0, 1])

    def ret_norm(h):
        u = stat(RQ[:, h, :], 6, one, 1, True, rp["r", h])
        s = small[0] % NSM
        small[0] += 1
        c = Q.dve(op_tensor_scalar, (u,), RC[:, s, 0:TT], PB[6][:, 0:TT], 1.0 / 128, None, ALU.mult)
        free[6] = c
        yield
        rt = spread(6, s, 1, c)
        d = free[6] = Q.dve(op_tensor_tensor, (rt, rp["r", h],), RQ[:, h, :], RQ[:, h, :], PB[6][:, :], ALU.subtract)
        i, t = square(RQ[:, h, :], d)
        yield
        u = stat(SQ[:, i, :], 6, one, 1, True, t)
        sq_free[i] = u
        s, r = root(6, TT, 1.0 / 128, 1, u)
        yield
        rt = spread(6, s, 1, r)
        v = free[6] = Q.dve(op_scalar_tensor_tensor, (rt, t, d,), out=RQ[:, h, :], in0=RQ[:, h, :], scalar=col(gains["ret_gn_g"] + h), in1=PB[6][:, :],
            op0=ALU.mult, op1=ALU.mult)
        rp["rn", h] = v
        yield

    side.append(ret())
    for h in range(4):
        side.append(ret_norm(h))

    def rg_out(m, ps, t):
        rp["rg", m] = Q.act(op_activation, (t, dil_done,), RG[:, m, :], ps, ACT.Silu)
        return rp["rg", m]

    dil_done = Q.last("pe", "dve")
    for c in range(2):
        run(proj_fm(2, HH, HL, h_tok, rg_out, False, m0=2 * c), 1.3)
    for m in range(4):
        split_into(m, AQ[:, m, :], [an["a", m], rp["rg", 3]])
    drain()
    for h in range(4):
        g = Q.dve(op_tensor_tensor, (rp["rn", h], rp["rg", h],), RQ[:, h, :], RQ[:, h, :], RG[:, h, :], ALU.mult)
        split_into(4 + h, RQ[:, h, :], g)

    y_tok = {}

    def y_evac(dst, toks):
        def evac(m, ps, t):
            y_tok[m] = Q.act(op_activation, (t,), dst[:, m, :], ps, ACT.Copy)
            toks.append(y_tok[m])
            return y_tok[m]
        return evac

    def post(src, gname, a_col, s_col, par, sqs):
        s, r = root(6, TT, 1.0 / D, 0, sqs[-1])
        yield
        rt = spread(5, s, 1, r)
        last = None
        for m in range(KT):
            i = m % 2
            t = Q.dve(op_scalar_tensor_tensor, (rt, y_tok[m], pc_tok,), out=TM[:, i, :], in0=src[:, m, :], scalar=col(gains[gname] + m), in1=PB[5][:, :],
                op0=ALU.mult, op1=ALU.mult)
            if m == KT - 1:
                free[5] = t
            x_tok[m] = Q.dve(op_tensor_tensor, (t,), X[:, m, :], X[:, m, :], TM[:, i, :], ALU.add)
            q, sq = square(X[:, m, :], x_tok[m])
            if m:
                add_stat(last[0], last[1], 6, m == 1, False)
            last = (q, sq)
            yield
        st2 = add_stat(last[0], last[1], 6, False, True)
        yield from rms_h(st2, a_col, s_col, par)

    mem_tok = {}

    def mem_load():
        w = Q.last("pe", "act", "dve")
        mem_in = Q.dma("mem", op_dma_start, (w,), MTM[:, :, :], I["mem"][0].rearrange("(a p) d -> p a d", p=128), engine="act")
        yield
        s = small[0] % NSM
        small[0] += 1
        for a in range(2):
            for hf in range(2):
                t = Q.act(op_activation, (mem_in, sq_free[0], sq_free[1], Q.last("act"),), SQ[:, hf, :], MTM[:, a, hf * 512:(hf + 1) * 512], ACT.Square,
                    accum_out=SD[:, s, 4 + 2 * a + hf:5 + 2 * a + hf])
        sq_free[0] = sq_free[1] = t
        u = Q.dve(op_tensor_tensor, (t,), SD[:, s, 8:10], SD[:, s, 4:8:2], SD[:, s, 5:8:2], ALU.add)
        v = Q.act(op_activation, (u,), SD[:, s, 0:2], SD[:, s, 8:10], ACT.Sqrt, bias=EPS[:, 0:1],
                                         scale=1.0 / D)
        r = Q.dve(op_reciprocal, (v,), RC[:, s, 0:2], SD[:, s, 0:2])
        yield
        for a in range(2):
            sc = Q.act(op_activation, (r, t,), MTM[:, a, :], MTM[:, a, :], ACT.Copy, scale=RC[:, s, a:a + 1])
        yield
        for k in range(KT):
            bk = 4
            for a in range(2):
                p = Q.pe(op_transpose, (sc, free[bk] if a == 0 else None,), PB[bk][:, a * 128:(a + 1) * 128], MTM[:, a, k * 128:(k + 1) * 128], ident, mark=(a == 1))
            hi = Q.act(op_activation, (p, w,), MH[:, k, :], PB[bk][:, 0:NMEM], ACT.Copy,
                                                   scale=col(gains["mem_norm_g"] + k))
            lo = Q.dve(op_scalar_tensor_tensor, (hi, w,), out=ML[:, k, :], in0=PB[bk][:, 0:NMEM], scalar=col(gains["mem_norm_g"] + k),
                in1=f(MH[:, k, :]), op0=ALU.mult, op1=ALU.subtract)
            free[bk] = lo
            mem_tok[k] = [hi, lo]
            yield

    side.append(mem_load())
    sqs, yt = [], []
    for c in range(4):
        run(proj_fm(2, HH, HL, h_tok, y_evac(Y, yt), c == 0, m0=2 * c), 0.7)
    side.append(watch(lambda m: Y[:, m, :], yt, sqs))
    drain()

    side.append(post(Y, "post_mix_g", gcol("pre_mem_g"), None, pc_tok, sqs))
    km = {}

    def km_out(m, ps, t):
        km[m] = Q.act(op_activation, (t,), KM[:, m, :], ps, ACT.Copy)
        return km[m]

    def vm_out(c):
        def evac(b2, ps, t):
            km["v", c] = Q.act(op_activation, (t,), VM[:, :, c * 256:(c + 1) * 256], ps, ACT.Copy)
            return km["v", c]
        return evac

    for c in range(4):
        run(proj_fm(2, MH, ML, mem_tok, km_out, False, ntok=NMEM, m0=2 * c), 1.0)
    for c in range(4):
        run(proj_tm(2, MH, ML, mem_tok, vm_out(c)), 1.0)
    drain()

    xq = {}

    def xq_out(m, ps, t):
        xq[m] = Q.act(op_activation, (t,), XQ[:, m, :], ps, ACT.Copy)
        return xq[m]

    def x_score(h, i, sb, sst, sm, f1, f2):
        for c in range(2):
            t = mm(PB[sb][:, 0:NMEM], XQ[:, 2 * h + c, i * 128:(i + 1) * 128], KM[:, 2 * h + c, :], c == 0,
                   c == 1, xq[2 * h + c], km[2 * h + c], free[sb] if c == 0 else None, mark=(c == 1))
        a = Q.dve(op_tensor_reduce, (t, f2,), sm[:, 0:1], PB[sb][:, 0:NMEM], AX.X, ALU.max)
        g = Q.dve(op_tensor_scalar, (a,), sm[:, 1:2], sm[:, 0:1], -1.0 / 16, None, ALU.mult)
        x = Q.act(op_activation, (g, f1,), sst[:, 0:NMEM], PB[sb][:, 0:NMEM], ACT.Exp, bias=sm[:, 1:2],
                                         scale=1.0 / 16, accum_out=sm[:, 2:3])
        free[sb] = x
        return norm_rows(sst, sm, NMEM, x)

    ox = {}

    def x_finish(h, i, ptt, tok, blocks):
        for c in range(2):
            bk = 7 - c
            for a in range(2):
                t = mm(PB[bk][:, i * 128:(i + 1) * 128], VM[:, a, h * 256 + c * 128:h * 256 + (c + 1) * 128],
                       ptt[:, a * 128:(a + 1) * 128], a == 0, a == 1, tok, km["v", h],
                       free[bk] if i == 0 else None, mark=(a == 1))
            if i == TT - 1:
                ox[2 * h + c] = free[bk] = Q.act(op_activation, (t,), XQ[:, 2 * h + c, :], PB[bk][:, :], ACT.Copy)
        return t

    def x_att(h):
        ssf = [None, None]
        ptf = [None, None]
        st_ = {}

        def s0(i):
            st_[i] = x_score(h, i, 4, XS[:, i % 2, :], SM[:, i, :], ssf[i % 2], None)

        def s1(i):
            for j in range(2):
                t = Q.pe(op_transpose, (st_[i], free[5] if j == 0 else None,), PB[5][:, j * 128:(j + 1) * 128],
                                                    XS[:, i % 2, j * 128:(j + 1) * 128], ident, mark=(j == 1))
            ssf[i % 2] = t
            free[5] = st_[i] = Q.act(op_activation, (t, ptf[i % 2],), XP[:, i % 2, 0:NMEM], PB[5][:, 0:NMEM], ACT.Copy)

        def s2(i):
            ptf[i % 2] = x_finish(h, i, XP[:, i % 2, :], st_.pop(i), 2)

        yield from pipeline(TT, [s0, s1, s2], [0, 1, 1])

    for h in range(4):
        run(proj_fm(2, HH, HL, h_tok, xq_out, h == 0, m0=2 * h), 0.8)
        side.append(x_att(h))
    q_done = Q.last("pe")
    drain()
    for k in range(KT):
        split_into(k, XQ[:, k, :], [ox[k], q_done])
    sqs, yt = [], []
    y_done = Q.last("act", "dve")

    def y_evac2(m, ps, t):
        return y_evac(Y, yt)(m, ps, [t, y_done])

    side.append(watch(lambda m: Y[:, m, :], yt, sqs))
    for c in range(4):
        run(proj_fm(2, HH, HL, h_tok, y_evac2, c == 0, m0=2 * c), 1.0)
    drain()
    side.append(post(Y, "post_mem_g", gcol("pre_ffn_g"), None, pc_tok, sqs))
    drain()

    gh_free = [None] * HALF
    sg_free = [None, None]

    def ffn(down_evac):
        for half in range(2):
            g_tok = [None] * HALF

            def up(m):
                i, vh, vl, wt = next_slab()
                b2 = [take(), take()]
                seq = [(k, u) for k in range(KT) for u in range(2)] if m == 0 else \
                      [(k, u) for u in range(2) for k in range(KT)]
                t2 = [None, None]
                for n, (k, u) in enumerate(seq):
                    t = mm3_w(PB[b2[u]][:, :], vh[:, k, u, :], vl[:, k, u, :], HH[:, k, :], HL[:, k, :],
                              k == 0, k == KT - 1, wt, h_tok[k], free[b2[u]] if k == 0 else None,
                              mark=(k == KT - 1))
                    if k == KT - 1:
                        t2[u] = t
                        if u == 0:
                            sg = Q.act(op_activation, (t, sg_free[m % 2],), SG[:, m % 2, :], PB[b2[0]][:, :], ACT.Silu)
                            free[b2[0]] = sg
                    if n % 2:
                        yield
                done_slab(i, t2[1])
                p = Q.dve(op_tensor_tensor, (t2[1], sg, Q.last("dve"),), TM[:, m % 2, :], PB[b2[1]][:, :], SG[:, m % 2, :],
                                                    ALU.mult)
                sg_free[m % 2] = free[b2[1]] = p
                hi = Q.act(op_activation, (p, gh_free[m],), GH[:, m, :], TM[:, m % 2, :], ACT.Copy)
                lo = Q.dve(op_tensor_tensor, (hi, p, gh_free[m],), GL[:, m, :], TM[:, m % 2, :], f(GH[:, m, :]),
                                                     ALU.subtract)
                g_tok[m] = [hi, lo]

            for m in range(HALF):
                yield from up(m)
            for k0, kn in ((0, 4), (4, 4), (8, 3)):
                i, vh, vl, wt = next_slab()
                for kk in range(kn):
                    k = k0 + kk
                    for m in range(4):
                        t = mm3_w(PB[4 + m][:, :], vh[:, kk, m * 128:(m + 1) * 128],
                                  vl[:, kk, m * 128:(m + 1) * 128], GH[:, k, :], GL[:, k, :], k == 0,
                                  k == HALF - 1, wt, g_tok[k], free[4 + m] if k == 0 else None,
                                  mark=(k == HALF - 1 or (m == 3 and kk == kn - 1)))
                        if k == HALF - 1:
                            free[4 + m] = down_evac(half, m, PB[4 + m][:, :], t)
                        if m % 2:
                            yield
                done_slab(i, t)
            for m in range(4, 8):
                i, vh, vl, wt = next_slab()
                b = take()
                for k in range(HALF):
                    t = mm3_w(PB[b][:, :], vh[:, k, :], vl[:, k, :], GH[:, k, :], GL[:, k, :], k == 0,
                              k == HALF - 1, wt, g_tok[k], free[b] if k == 0 else None,
                              mark=(k == HALF - 1 or m == 7))
                    if m == 7:
                        gh_free[k] = t
                    if k % 2:
                        yield
                done_slab(i, t)
                free[b] = down_evac(half, m, PB[b][:, :], t)

    def ffn1_evac(half, m, ps, t):
        if half == 0:
            y_tok[m] = Q.act(op_activation, (t,), Y1[:, m, :], ps, ACT.Copy)
            return y_tok[m]
        y_tok[m] = Q.dve(op_tensor_tensor, (t, y_tok[m],), Y1[:, m, :], ps, Y1[:, m, :], ALU.add)
        yt.append(y_tok[m])
        return y_tok[m]

    sqs, yt = [], []
    side.append(watch(lambda m: Y1[:, m, :], yt, sqs, 4))
    run(ffn(ffn1_evac), 1.0)
    drain()
    flush_ada()

    def mod_cols(l):
        g0 = P2["g_norm", l]
        toks = []
        for j in range(3):
            c = (3 * j + 1) * 8
            toks.append(Q.dve(op_scalar_tensor_tensor, (mod_tok[l], pc_tok, Q.last("pe", "act"),), out=MA[:, 8 * j:8 * j + 8], in0=MOD[:, l, c:c + 8], scalar=1.0, in1=PC[:, g0 + 8 * j:g0 + 8 * j + 8],
                op0=ALU.add, op1=ALU.mult))
            c2 = (3 * j + 2) * 8
            hf = 1.0 if j == 1 else 0.5
            toks.append(Q.dve(op_tensor_scalar, (mod_tok[l],), MG[:, 8 * j:8 * j + 8], MOD[:, l, c2:c2 + 8], hf, hf, ALU.mult, ALU.add))
        return toks[-1]

    def a2(j):
        return lambda k: MA[:, 8 * j + k:8 * j + k + 1]

    def s2(l, j):
        return lambda k: MOD[:, l, 24 * j + k:24 * j + k + 1]

    def g2(j):
        return lambda k: MG[:, 8 * j + k:8 * j + k + 1]

    def x_add(j, toks):
        def evac(m, ps, t, whole=True):
            x_tok[m] = Q.dve(op_scalar_tensor_tensor, (t, x_tok[m]), out=X[:, m, :], in0=ps, scalar=g2(j)(m),
                             in1=X[:, m, :], op0=ALU.mult, op1=ALU.add)
            if whole:
                toks.append(x_tok[m])
            return x_tok[m]
        return evac

    def ffn2(j, want):
        sqs, xt = [], []
        ev = x_add(j, xt)
        if want:
            side.append(watch(lambda m: X[:, m, :], xt, sqs, 4))
        run(ffn(lambda half, m, ps, t: ev(m, ps, t, whole=half == 1)), 1.0)
        drain()
        return sqs

    mt = mod_cols(0)
    side.append(post(Y1, "post_ffn_g", a2(0), s2(0, 0), mt, sqs))
    drain()

    def mixer2(l):
        hdone = []
        w_done = Q.last("pe", "act", "dve")
        c8 = LAM[:, 3, :]
        lam = P2["lru_lambda_2", l]
        t = Q.act(op_activation, (pc_tok, w_done,), LAM[:, 0, :], PC[:, lam:lam + 4], ACT.Abs)
        t = Q.act(op_activation, (t,), LAM[:, 0, :], LAM[:, 0, :], ACT.Exp, scale=-1.0)
        t = Q.act(op_activation, (t, eps_tok,), LAM[:, 0, :], LAM[:, 0, :], ACT.Ln, bias=EPS[:, 2:3])
        u = Q.dve(op_tensor_scalar, (w_done,), LAM[:, 1, :], PC[:, lam:lam + 4], -1.0, 0.0, ALU.mult, ALU.max)
        u = Q.dve(op_tensor_tensor, (t, u,), LAM[:, 2, :], LAM[:, 1, :], LAM[:, 0, :], ALU.add)
        u = Q.dve(op_tensor_scalar, (u,), LAM[:, 3, :], LAM[:, 2, :], 8.0, None, ALU.mult)
        c8t = Q.dve(op_tensor_scalar, (u,), LAM[:, 1, :], LAM[:, 3, :], -1.0, None, ALU.mult)
        bz = Q.pool(op_memset, (w_done,), BD[:, :, :, :], 0.0)
        for g, nm in ((0, "w_rgate_2"), (1, "w_igate_2")):
            v = I[nm][l].rearrange("(m u) i j -> u i m j", u=2)
            for u2 in range(2):
                bd_in = Q.dma("bd", op_dma_start, (bz,), BD[64 * u2:64 * u2 + 64, g, :, 64 * u2:64 * u2 + 64], v[u2], engine="act")
        bf_in = Q.dma("bf", op_dma_start, (w_done,), BF[:, :], I["b_fgate_2"][l:l + 1, :].to_broadcast([128, 4]), engine="act")

        i, vh, vl, wt = next_slab()
        b = take()
        for j in range(TT):
            for k in range(KT):
                t = mm3_x(PB[b][:, 4 * j:4 * j + 4], HH[:, k, j * 128:(j + 1) * 128],
                          HL[:, k, j * 128:(j + 1) * 128], vh[:, k, :], vl[:, k, :], k == 0, k == KT - 1,
                          wt, h_tok[k], free[b] if j == 0 and k == 0 else None, mark=(k == KT - 1))
        done_slab(i, t)
        t = Q.dve(op_tensor_tensor, (t, bf_in, w_done,), FG[:, 0, :].rearrange("p (j h) -> p j h", h=4), PB[b][:, 0:16].rearrange("p (j h) -> p j h", h=4),
            BF[:, :].unsqueeze(1).to_broadcast([128, 4, 4]), ALU.add)
        free[b] = t
        t1 = Q.act(op_activation, (t, w_done,), FG[:, 1, :], FG[:, 0, :], ACT.Abs)
        t1 = Q.act(op_activation, (t1,), FG[:, 1, :], FG[:, 1, :], ACT.Exp, scale=-1.0)
        t1 = Q.act(op_activation, (t1,), FG[:, 1, :], FG[:, 1, :], ACT.Ln, bias=EPS[:, 2:3])
        t2 = Q.dve(op_tensor_scalar, (t,), FG[:, 2, :], FG[:, 0, :], 0.0, None, ALU.min)
        lf = Q.dve(op_tensor_tensor, (t1, t2,), FG[:, 3, :], FG[:, 2, :], FG[:, 1, :], ALU.subtract)
        nf = Q.dve(op_tensor_scalar, (lf,), FG[:, 4, :], FG[:, 3, :], -1.0, None, ALU.mult)
        fx = {}

        def fgates():
            for i_ in range(TT):
                for jj in range(i_ + 1):
                    l_ = CB[:, C_TRI:C_TRI + 128] if jj == i_ else CB[:, C_TRI + 128:C_TRI + 256]
                    t = mm(PB[4][:, 4 * i_:4 * i_ + 4], l_, FG[:, 3, 4 * jj:4 * jj + 4], jj == 0, jj == i_,
                           lf, free[4] if i_ == 0 else None, mark=(i_ == TT - 1 and jj == i_))
            fx["q"] = free[4] = Q.act(op_activation, (t,), FG[:, 5, :], PB[4][:, 0:16], ACT.Copy)
            yield
            for h in range(4):
                bk = 4 + (h + 1) % 2
                for jj in range(TT):
                    n = S - 128 * jj
                    t = mm(PB[bk][:, jj * 128:S], FG[:, 4, 4 * jj + h:4 * jj + h + 1].to_broadcast([128, 128]),
                           CB[:, C_TRI:C_TRI + n], jj == 0, jj == TT - 1, nf, free[bk] if jj == 0 else None,
                           mark=(jj == TT - 1))
                fx["k", h] = free[bk] = Q.act(op_activation, (t, w_done,), FB[:, h, :], PB[bk][:, :], ACT.Copy)
                yield

        side.append(fgates())

        def fm_out(dst, key, scale=1.0):
            def evac(m, ps, t):
                an[key, m] = Q.act(op_activation, (t, w_done,), dst[:, m, :], ps, ACT.Copy, scale=scale)
                return an[key, m]
            return evac

        def tm_out1(dst, key):
            def evac(b2, ps, t):
                rp[key, b2] = Q.act(op_activation, (t, w_done,), dst[:, 2 * b2:2 * b2 + 2, :], ps, ACT.Copy)
                return rp[key, b2]
            return evac

        run(proj_fm(2, HH, HL, h_tok, fm_out(FXQ, "fq"), False))
        run(proj_fm(2, HH, HL, h_tok, fm_out(FXK, "fk"), False))
        gq = P2["g_qk", l]
        for m in range(2):
            side.append(att_norm(m, FXQ, col(gq), "fq"))
            side.append(att_norm(m, FXK, col(gq + 1), "fk"))
        run(proj_tm(TT, HH, HL, h_tok, tm_out1(FXV, "fv")))

        def fox_score(h, i, sb, sst, sm, f1, f2):
            n = 128 * (i + 1)
            po, m = 64 * (h % 2), h // 2
            mm(PB[sb][:, 0:n], FXQ[po:po + 64, m, i * 128:(i + 1) * 128], FXK[po:po + 64, m, 0:n], True, False,
               an["fq", m], an["fk", m], free[sb])
            t = mm(PB[sb][:, n - 128:n], ident, CB[:, C_CADD:C_CADD + 128], False, True, mark=True)
            a = Q.dve(op_scalar_tensor_tensor, (t, fx["k", h], f1,), out=sst[:, 0:n], in0=PB[sb][:, 0:n], scalar=0.125, in1=FB[:, h, 0:n], op0=ALU.mult,
                op1=ALU.add)
            free[sb] = a
            a = Q.dve(op_tensor_scalar, (a, fx["q"],), sst[:, 0:n], sst[:, 0:n], FG[:, 5, 4 * i + h:4 * i + h + 1], None,
                                                ALU.add)
            a = Q.dve(op_tensor_reduce, (a, f2,), sm[:, 0:1], sst[:, 0:n], AX.X, ALU.max)
            g = Q.dve(op_tensor_scalar, (a,), sm[:, 1:2], sm[:, 0:1], -1.0, None, ALU.mult)
            x = Q.act(op_activation, (g,), sst[:, 0:n], sst[:, 0:n], ACT.Exp, bias=sm[:, 1:2],
                                             accum_out=sm[:, 2:3])
            return norm_rows(sst, sm, n, x)

        side.append(soft_attention(4, fox_score, lambda i: 128 * (i + 1), None, FS, FP,
                                   head_pair_finish(FXV, lambda h: [("fv", 0), ("fv", 1)], FXQ, "fo", None), "f"))

        cw, cbias = P2["conv_w", l], P2["conv_b_2", l]
        lx = {}

        def lx_out(m, ps, t):
            lx[m] = Q.act(op_activation, (t, w_done,), LA[:, m, :], ps, ACT.Copy)
            return lx[m]

        def conv(m):
            t = Q.act(op_activation, (lx[m], w_done,), LB[:, m, :], LA[:, m, :], ACT.Identity, bias=col(cbias + m),
                                             scale=col(cw + 12 + m))
            for s_ in range(1, 4):
                t = Q.dve(op_scalar_tensor_tensor, (t,), out=LB[:, m, s_:S], in0=LA[:, m, 0:S - s_], scalar=col(cw + (3 - s_) * 4 + m),
                    in1=LB[:, m, s_:S], op0=ALU.mult, op1=ALU.add)
            lx["u", m] = t
            yield

        for c in range(2):
            run(proj_fm(2, HH, HL, h_tok, lx_out, False, m0=2 * c), 0.8)
        run(proj_fm(2, HH, HL, h_tok, fm_out(SBQ, "sq", 0.125), False), 0.8)
        run(proj_fm(2, HH, HL, h_tok, fm_out(SBK, "sk"), False), 0.8)
        for m in range(4):
            side.append(conv(m))
        run(proj_tm(TT, HH, HL, h_tok, tm_out1(SBV, "sv")), 0.8)
        drain()
        fox_done = Q.last("pe", "act", "dve")

        def lru():
            for g, dst, bias in ((0, LC, "b_rgate_2"), (1, LA, "b_igate_2")):
                for m in range(4):
                    bk = 6
                    t = mm(PB[bk][:, :], BD[:, g, m, :], LB[:, m, :], True, True, bd_in, bz, lx["u", m],
                           free[bk], mark=True)
                    lx[g, m] = free[bk] = Q.act(op_activation, (t, fox_done,), dst[:, m, :], PB[6][:, :], ACT.Sigmoid, bias=col(P2[bias, l] + m))
                    yield
            gates = Q.last("pe")
            for m in range(4):
                lx["a", m] = Q.act(op_activation, (lx[0, m], gates, c8t,), LD[:, m, :], LC[:, m, :], ACT.Exp,
                                                               scale=LAM[:, 1, m:m + 1])
                lx["t", m] = Q.act(op_activation, (lx["a", m], c8t,), LC[:, m, :], LC[:, m, :], ACT.Tanh,
                                                               scale=LAM[:, 3, m:m + 1])
                i_ = Q.dve(op_tensor_tensor, (lx[1, m], lx["u", m], gates,), LB[:, m, :], LB[:, m, :], LA[:, m, :], ALU.mult)
                a_ = Q.dve(op_tensor_tensor, (lx["a", m], i_,), LA[:, m, :], LD[:, m, :], LD[:, m, :], ALU.mult)
                lx["m", m] = Q.dve(op_scalar_tensor_tensor, (a_, lx["t", m],), out=LA[:, m, :], in0=LA[:, m, :], scalar=1.0, in1=LC[:, m, :], op0=ALU.add, op1=ALU.mult)
                yield
            for m in range(4):
                lx["r", m] = Q.act(op_activation, (lx["m", m],), LA[:, m, :], LA[:, m, :], ACT.Sqrt)
                t = Q.dve(op_tensor_tensor, (lx["r", m],), LB[:, m, :], LB[:, m, :], LA[:, m, :], ALU.mult)
                lx["h", m] = Q.dve(op_tensor_tensor_scan, (t, lx["t", m],), LC[:, m, :], LD[:, m, :], LB[:, m, :], 0.0, ALU.mult, ALU.add)
                yield

        def sb_att():
            offs = [0, 512, 896, 1152]
            sp_free = [None]
            st_free = [None]
            w_free = [None]
            for h in range(4):
                po, m = 64 * (h % 2), h // 2
                spt = {}
                for j in (3, 2, 1, 0):
                    n = S - 128 * j
                    bk = 4 + j % 2
                    o = offs[j]
                    t = mm(PB[bk][:, 0:n], SBK[po:po + 64, m, j * 128:(j + 1) * 128],
                           SBQ[po:po + 64, m, j * 128:S], True, True, an["sq", m], an["sk", m],
                           free[bk], mark=True)
                    u = Q.act(op_activation, (t, st_free[0], fox_done,), ST[:, 0:n], PB[bk][:, 0:n], ACT.Abs)
                    u = Q.act(op_activation, (u,), ST[:, 0:n], ST[:, 0:n], ACT.Exp, scale=-1.0)
                    u = Q.act(op_activation, (u,), ST[:, 0:n], ST[:, 0:n], ACT.Ln, bias=EPS[:, 2:3])
                    v = Q.dve(op_scalar_tensor_tensor, (u, sp_free[0], fox_done,), out=SP[:, o:o + n], in0=PB[bk][:, 0:n], scalar=0.0, in1=ST[:, 0:n], op0=ALU.max,
                        op1=ALU.add)
                    st_free[0] = v
                    v = Q.dve(op_tensor_tensor, (v,), SP[:, o:o + 128], SP[:, o:o + 128],
                                                        CB[:, C_SMUL:C_SMUL + 128], ALU.mult)
                    spt[j] = v
                    yield
                    mm(PB[bk][:, 0:128], ident, CB[:, C_SADD:C_SADD + 128], False, False, v, skip=True)
                    t = mm(PB[bk][:, 0:n], CB[:, C_NT:C_NT + 128], SP[:, o:o + n], False, j == 3, v,
                           mark=(j == 3), skip=True)
                    for j2 in range(j + 1, TT):
                        n2 = S - 128 * j2
                        t = mm(PB[bk][:, n - n2:n], CB[:, C_NONE:C_NONE + 128],
                               SP[:, offs[j2]:offs[j2] + n2], False, j2 == 3, spt[j2], mark=(j2 == 3), skip=True)
                    w = Q.act(op_activation, (t, w_free[0], fox_done,), SW[:, 0:n], PB[bk][:, 0:n], ACT.Exp)
                    free[bk] = w
                    if j == 0:
                        sp_free[0] = t
                    yield
                    p = mm(PB[7][po:po + 64, j * 128:S], SBV[:, j, h * 64:(h + 1) * 64], SW[:, 0:n], j == 3,
                           j == 0, w, rp["sv", 0], rp["sv", 1],
                           free[7] if h % 2 == 0 and j == 3 else None, mark=True, skip=True)
                    w_free[0] = p
                if h % 2:
                    an["so", m] = free[7] = Q.act(op_activation, (p,), SBQ[:, m, :], PB[7][:, :],
                                                                              ACT.Copy)

        def width_norm(src, n, gain, key, k0):
            for m in range(n):
                i_, t = square(src[:, m, :], an[key, m])
                u = stat(SQ[:, i_, :], 6, one, 1, m == 0, t, last=m == n - 1)
                sq_free[i_] = u
            s_, r = root(6, TT, 1.0 / (128 * n), 0, u)
            yield
            rt = spread(6, s_, 1, r)
            for m in range(n):
                i_ = m % 2
                t = Q.dve(op_scalar_tensor_tensor, (rt, an[key, m], pc_tok,), out=TM[:, i_, :], in0=src[:, m, :], scalar=gain(m), in1=PB[6][:, :], op0=ALU.mult,
                    op1=ALU.mult)
                hi = Q.act(op_activation, (t, hdone,), HH[:, k0 + m, :], TM[:, i_, :], ACT.Copy)
                lo = Q.dve(op_tensor_tensor, (hi, t, hdone,), HL[:, k0 + m, :], TM[:, i_, :], f(HH[:, k0 + m, :]), ALU.subtract)
                h_tok[k0 + m] = [hi, lo]
                yield
            free[6] = t

        side.append(lru())
        side.append(sb_att())

        def lg_out(m, ps, t):
            lx["g", m] = Q.act(op_activation, (t, fox_done,), LG[:, m, :], ps, ACT.Gelu_apprx_tanh)
            return lx["g", m]

        for c in range(2):
            run(proj_fm(2, HH, HL, h_tok, lg_out, False, m0=2 * c), 1.5)
        hdone.extend(Q.last("pe"))
        drain()
        for m in range(4):
            an["ly", m] = Q.dve(op_tensor_tensor, (lx["h", m], lx["g", m]), LC[:, m, :], LC[:, m, :], LG[:, m, :],
                                ALU.mult)
        gm = P2["g_mix", l]
        side.append(width_norm(FXQ, 2, lambda m: col(gm + 6 + m), "fo", 6))
        side.append(width_norm(SBQ, 2, lambda m: col(gm + 4 + m), "so", 4))
        side.append(width_norm(LC, 4, lambda m: col(gm + m), "ly", 0))
        drain()
        sqs, xt = [], []
        side.append(watch(lambda m: X[:, m, :], xt, sqs))
        for c in range(4):
            run(proj_fm(2, HH, HL, h_tok, x_add(1, xt), c == 0, m0=2 * c))
        drain()
        return sqs

    for l in range(2):
        if l:
            mt = mod_cols(1)
            side.append(rms_h(sqs[-1], a2(0), s2(1, 0), mt))
            drain()
        sqs = ffn2(0, True)
        side.append(rms_h(sqs[-1], a2(1), s2(l, 1), mt))
        drain()
        sqs = mixer2(l)
        side.append(rms_h(sqs[-1], a2(2), s2(l, 2), mt))
        drain()
        sqs = ffn2(2, l == 0)

    for j in range(TT):
        toks = []
        for hf in range(2):
            b = take()
            for q in range(4):
                t = Q.pe(op_transpose, (x_tok[4 * hf + q], free[b] if q == 0 else None), PB[b][:, q * 128:(q + 1) * 128],
                         X[:, 4 * hf + q, j * 128:(j + 1) * 128], ident, mark=q == 3)
            o = OT[:, j, hf * 512:(hf + 1) * 512]
            if hf:
                t = Q.act(op_activation, (t,), o, PB[b][:, :], ACT.Copy)
            else:
                t = Q.dve(op_tensor_copy, (t,), o, PB[b][:, :])
            free[b] = t
            toks.append(t)
        out_tok = Q.dma("out", op_dma_start, toks, out[0, j * 128:(j + 1) * 128, :], OT[:, j, :])

    with ExitStack() as ctx:
        sems = {name: ctx.enter_context(nc.semaphore("s_" + name)) for name in Q.count}
        block = ctx.enter_context(nc.Block())

        @block.sync
        def _(e):
            Q.run("sp", e, sems)
            e.wait_ge(sems["out"], out_tok[1])

        @block.gpsimd
        def _(e):
            Q.run("pool", e, sems)

        @block.scalar
        def _(e):
            Q.run("act", e, sems)

        @block.vector
        def _(e):
            Q.run("dve", e, sems)

        @block.tensor
        def _(e):
            Q.run("pe", e, sems)


_NAMES = ["x", "mem", "pre_mix_g", "post_mix_g", "w_in", "attn_gn_g", "ret_gn_g", "w_out", "pre_mem_g",
          "post_mem_g", "mem_norm_g", "w_q_mem", "w_kv_mem", "w_o_mem", "pre_ffn_g", "post_ffn_g", "w_gate_up",
          "w_down", "c_2", "w_ada_2", "b_ada_2", "g_norm_2", "w_ffn_up_2", "w_ffn_down_2", "w_in_2", "b_fgate_2",
          "conv_w_2", "conv_b_2", "w_rgate_2", "b_rgate_2", "w_igate_2", "b_igate_2", "lru_lambda_2", "g_qk_2",
          "g_mix_out_2", "w_out_2"]


def kernel(**inputs):
    import numpy as _np
    import concourse.bacc as _bacc
    from concourse import mybir as _mybir
    from concourse.bass_utils import run_bass_kernel_spmd as _run

    nc = _bacc.Bacc("TRN2", target_bir_lowering=False, num_devices=1)
    arrays, aps = {}, {}
    cb, ct = const_tables()
    for name, a in [(n, _np.ascontiguousarray(inputs[n])) for n in _NAMES] + [("c_b", cb), ("c_t", ct)]:
        arrays["in_" + name] = a
        aps[name] = nc.dram_tensor("in_" + name, a.shape, _mybir.dt.from_np(a.dtype), kind="ExternalInput").ap()
    out = nc.dram_tensor("out_0_dram", (1, S, D), _mybir.dt.float32, kind="ExternalOutput").ap()
    build(nc, aps, out)
    r = _run(nc, [arrays], core_ids=[0])
    return r.results[0]["out_0_dram"]
```

```python
from collections import deque
from contextlib import ExitStack

import numpy as np
import concourse.bass as bass
from concourse import mybir

F32 = mybir.dt.float32
F32R = mybir.dt.float32r
ALU = mybir.AluOpType
ACT = mybir.ActivationFunctionType
AX = mybir.AxisListType

D = 1024
S = 512
KT = 8
TT = 4
NMEM = 256
FF = 2816
HALF = 11
RMS_EPS = 1e-6
GN_EPS = 1e-5
NEG = -1e30

C_ID, C_TRI, C_NT, C_NONE, C_SADD, C_CADD, C_SMUL, C_PA, C_PR, C_SEL, C_ONE = (
    0, 128, 640, 768, 896, 1024, 1152, 1280, 1408, 1536, 1538)
CB_W = 1540
T_MASK, T_ROPE, T_DEC = 0, 512, 512 + 4 * 512
CT_W = T_DEC + 4 * 512


def const_tables():
    p = np.arange(128)[:, None]
    c = np.arange(128)[None, :]
    cb = np.zeros((128, CB_W), np.float32)
    cb[:, C_ID:C_ID + 128] = (p == c)
    cb[:, C_TRI:C_TRI + 512] = (p <= np.arange(512)[None, :])
    cb[:, C_NT:C_NT + 128] = -1.0 * (p >= c)
    cb[:, C_NONE:C_NONE + 128] = -1.0
    cb[:, C_SADD:C_SADD + 128] = np.where(p >= c, NEG, 0.0)
    cb[:, C_CADD:C_CADD + 128] = np.where(c > p, NEG, 0.0)
    cb[:, C_SMUL:C_SMUL + 128] = (p < c)
    i = c % 64
    partner = np.where(i < 8, c + 8, np.where(i < 16, c - 8, -1))
    cb[:, C_PA:C_PA + 128] = (p == partner)
    cb[:, C_PR:C_PR + 128] = (p == (c + 64) % 128)
    cb[:, C_SEL] = (np.arange(128) < 64)
    cb[:, C_SEL + 1] = (np.arange(128) >= 64)
    cb[:, C_ONE:C_ONE + 2] = 1.0

    ct = np.zeros((128, CT_W), np.float32)
    n = np.arange(512)
    delta = 128 * (3 - n[None, :] // 128) + p - n[None, :] % 128
    count = ((delta >= 0) & (delta <= 128)).astype(int) + ((delta >= 0) & (delta % 4 == 0)) \
        + ((delta >= 0) & (delta % 16 == 0))
    ct[:, T_MASK:T_MASK + 512] = np.where(count > 0, 8.0 * np.log(np.maximum(count, 1)), NEG)
    pos = np.arange(512, dtype=np.float32)
    for at, dim, theta, width in ((0, 16, 500000.0, 64), (2, 128, 10000.0, 128)):
        inv = np.float32(theta) ** (-(np.arange(0, dim, 2, dtype=np.float32) / np.float32(dim)))
        ang = (pos[None, :] * inv.astype(np.float32)[:, None]).astype(np.float32)
        cos, sin = np.cos(ang), np.sin(ang)
        h = dim // 2
        cr = np.ones((width, 512), np.float32)
        sr = np.zeros((width, 512), np.float32)
        cr[:h], cr[h:dim] = cos, cos
        sr[:h], sr[h:dim] = -sin, sin
        ct[:, T_ROPE + at * 512:T_ROPE + (at + 1) * 512] = np.tile(cr, (128 // width, 1))
        ct[:, T_ROPE + (at + 1) * 512:T_ROPE + (at + 2) * 512] = np.tile(sr, (128 // width, 1))
    for h in range(4):
        log_g = np.log(1.0 - 2.0 ** (-5.0 - h))
        rel = n[None, :] - p
        ct[:, T_DEC + h * 512:T_DEC + (h + 1) * 512] = np.where(
            rel >= 0, np.exp(log_g * np.maximum(rel, 0)) * 128.0 ** -0.5, 0.0)
    return cb, ct


def op_matmul(e, *a, **k):
    return e.matmul(*a, **k)


def op_transpose(e, *a, **k):
    return e.transpose(*a, **k)


def op_activation(e, *a, **k):
    return e.activation(*a, **k)


def op_tensor_tensor(e, *a, **k):
    return e.tensor_tensor(*a, **k)


def op_tensor_scalar(e, *a, **k):
    return e.tensor_scalar(*a, **k)


def op_scalar_tensor_tensor(e, *a, **k):
    return e.scalar_tensor_tensor(*a, **k)


def op_tensor_tensor_scan(e, *a, **k):
    return e.tensor_tensor_scan(*a, **k)


def op_tensor_tensor_reduce(e, *a, **k):
    return e.tensor_tensor_reduce(*a, **k)


def op_tensor_reduce(e, *a, **k):
    return e.tensor_reduce(*a, **k)


def op_tensor_copy(e, *a, **k):
    return e.tensor_copy(*a, **k)


def op_reciprocal(e, *a, **k):
    return e.reciprocal(*a, **k)


def op_memset(e, *a, **k):
    return e.memset(*a, **k)


def op_preload(e, name):
    return e.preload_act_table_set(name)


def op_dma_start(e, *a, **k):
    return e.dma_start(*a, **k)


class Queues:

    def __init__(self):
        self.todo = {e: [] for e in ("sp", "pe", "act", "dve", "pool")}
        self.count = {}
        self.clock = dict.fromkeys(("sp", "pe", "act", "dve", "pool", "dma"), 0.0)
        self.done = {}

    @staticmethod
    def price(engine, op, args, kw):
        if op is op_dma_start:
            return int(np.prod(args[0].shape)) * 4 / 350e3
        if op is op_preload:
            return 1.3
        out = kw["out"] if "out" in kw else args[0]
        n = int(np.prod(out.shape[1:]))
        if op is op_matmul:
            return max(n, 64) * (4 if args[1].dtype == F32 else 1) / 2400
        if op is op_transpose:
            return 0.06
        if engine == "act":
            return 0.19 + n / 1200
        if op is op_reciprocal:
            n *= 6
        elif op is op_tensor_tensor_scan:
            n *= 2
        return 0.07 + n / 960

    def put(self, engine, op, after, sem, by, args, kw):
        flat = []
        stack = list(after)
        while stack:
            t = stack.pop()
            if isinstance(t, list):
                stack += t
            elif t is not None:
                flat.append(t)
        if sem is not None:
            self.count[sem] = self.count.get(sem, 0) + by
        self.todo[engine].append((op, args, kw, flat, sem, by))
        unit = "dma" if op is op_dma_start else engine
        start = max([self.clock[unit]] + [self.done.get(t, 0.0) + 0.1 for t in flat])
        self.clock[unit] = start + self.price(engine, op, args, kw)
        if sem is not None:
            self.done[(sem, self.count[sem])] = self.clock[unit] + (2.0 if unit == "dma" else 0.0)
        return (sem, self.count[sem]) if sem is not None else None

    def pe(self, op, after, *args, mark=False, **kw):
        return self.put("pe", op, after, "pe" if mark else None, 1, args, kw)

    def act(self, op, after, *args, **kw):
        return self.put("act", op, after, "act", 1, args, kw)

    def table(self, name):
        self.put("act", op_preload, (), None, 0, (name,), {})

    def dve(self, op, after, *args, **kw):
        return self.put("dve", op, after, "dve", 1, args, kw)

    def pool(self, op, after, *args, **kw):
        return self.put("pool", op, after, "pool", 1, args, kw)

    def dma(self, sem, op, after, *args, engine="sp", **kw):
        return self.put(engine, op, after, sem, 16, args, kw)

    def when(self, need):
        if need is None:
            return 0.0
        if isinstance(need, list):
            return max([0.0] + [self.when(x) for x in need])
        return self.done.get(need, 0.0) + 0.1

    def last(self, *engines):
        return [(e, self.count[e]) for e in engines if self.count.get(e)]

    def run(self, name, engine, sems):
        seen = {}
        for op, args, kw, after, sem, by in self.todo[name]:
            need = {}
            for s, v in after:
                need[s] = max(need.get(s, 0), v)
            for s in sorted(need):
                if seen.get(s, 0) < need[s]:
                    engine.wait_ge(sems[s], need[s])
                    seen[s] = need[s]
            ins = op(engine, *args, **kw)
            if sem is not None:
                ins.then_inc(sems[sem], by)


def build(nc, I, out):
    Q = Queues()
    base = (nc.sbuf_base + 127) // 128 * 128
    TB = 2048

    def at(name, off_bytes, shape, dt=F32):
        return nc.alloc_sbuf_tensor_at(name, shape, dt, offset=base + off_bytes)

    X = at("X", 0, [128, KT, S])
    HH = at("HH", 8 * TB, [128, KT, S], F32R)
    HL = at("HL", 16 * TB, [128, KT, S], F32R)
    NS, NW, SLAB = 3, 3, 2048
    WS = at("WS", 24 * TB, [128, NS, SLAB])
    WH = at("WH", 36 * TB, [128, NW, SLAB], F32R)
    WL = at("WL", 48 * TB, [128, NW, SLAB], F32R)
    coff = [60 * TB]

    def const(name, shape, dt=F32):
        t = at(name, coff[0], shape, dt)
        coff[0] += (4 * int(np.prod(shape[1:])) + 31) // 32 * 32
        assert coff[0] <= 66 * TB
        return t

    CB = const("CB", [128, CB_W])
    ACC = const("ACC", [128, 512])
    PC = const("PC", [128, 340])
    MOD = const("MOD", [128, 2, 72])
    MA = const("MA", [128, 24])
    MG = const("MG", [128, 24])
    NSM = 6
    SD = const("SD", [128, NSM, 16])
    RC = const("RC", [128, NSM, 16])
    CC = const("CC", [128, 8])
    CS = const("CS", [128, 8])
    EPS = const("EPS", [128, 4])
    SM = const("SM", [128, 4, 4])
    LAM = const("LAM", [128, 4, 4])
    FG = const("FG", [128, 6, 16])
    BF = const("BF", [128, 4])

    R0 = 66

    def region(name, t, shape, dt=F32):
        n = 4 * int(np.prod(shape[1:]))
        assert (R0 + t) * TB + n <= 103 * TB
        return at(name, int((R0 + t) * TB), shape, dt)

    SQ = region("SQ", 33, [128, 2, S])
    TM = region("TM", 35, [128, 2, S])
    XTM = region("XTM", 0, [128, TT, D])
    PR = region("PR", 20, [128, 5, 128])
    AQ = region("AQ", 0, [128, 4, S])
    AK = region("AK", 4, [128, 4, S])
    RG = region("RG", 4, [128, 4, S])
    AV = region("AV", 8, [128, TT, 512])
    RQ = region("RQ", 12, [128, 4, S])
    RK = region("RK", 16, [128, 4, S])
    RV = region("RV", 20, [128, TT, 512])
    MSK = region("MSK", 24, [128, 512])
    ROPE = region("ROPE", 25, [128, 4, 512])
    SS = region("SS", 29, [128, 2, S])
    PT = region("PT", 31, [128, 2, S])
    MH = region("MH", 0, [128, KT, NMEM], F32R)
    ML = region("ML", 4, [128, KT, NMEM], F32R)
    KM = region("KM", 8, [128, KT, NMEM])
    VM = region("VM", 12, [128, 2, D])
    Y = region("Y", 16, [128, KT, S])
    XQ = region("XQ", 16, [128, KT, S])
    XS = region("XS", 24, [128, 4, NMEM])
    XP = region("XP", 26, [128, 4, NMEM])
    MTM = region("MTM", 28, [128, 2, D])
    GH = region("GH", 0, [128, HALF, S], F32R)
    GL = region("GL", 11, [128, HALF, S], F32R)
    Y1 = region("Y1", 22, [128, KT, S])
    SG = region("SG", 30, [128, 2, S])
    FXQ = region("FXQ", 0, [128, 2, S])
    FXK = region("FXK", 2, [128, 2, S])
    FXV = region("FXV", 4, [128, TT, 256])
    SBQ = region("SBQ", 6, [128, 2, S])
    SBK = region("SBK", 8, [128, 2, S])
    SBV = region("SBV", 10, [128, TT, 256])
    LA = region("LA", 12, [128, 4, S])
    LB = region("LB", 16, [128, 4, S])
    LC = region("LC", 20, [128, 4, S])
    FB = region("FB", 24, [128, 4, S])
    LD = region("LD", 6, [128, 4, S])
    BD = region("BD", 10, [128, 2, 4, 128])
    FS = region("FS", 28, [128, 2, S])
    FS2 = region("FS2", 32, [128, S])[:, :]
    FP = region("FP", 30, [128, 2, S])
    SP = region("SP", 12, [128, 1408])
    ST = region("ST", 15, [128, 2, S])
    SW = region("SW", 17, [128, 2, S])
    LG = region("LG", 24, [128, 4, S])
    FF4 = region("FF4", 28, [128, 4, S])
    OT = region("OT", 0, [128, TT, D])

    PB = [nc.alloc_psum_tensor(f"PB{i}", [128, 512], F32) for i in range(8)]
    free = {b: None for b in range(8)}
    ring = deque([0, 1, 2, 3])

    held = set()

    def take(hold=False):
        b = next(x for x in ring if x not in held)
        ring.remove(b)
        ring.append(b)
        if hold:
            held.add(b)
        return b

    def let_go(b, tok):
        free[b] = tok
        held.discard(b)

    ident = CB[:, C_ID:C_ID + 128]

    def f(ap):
        return ap.bitcast(F32)

    def mm(out_, l, r, start, stop, *after, mark=False, skip=False):
        return Q.pe(op_matmul, (*after,), out_, l, r, start=start, stop=stop, skip_group_check=skip, mark=mark)

    BLOCKED = 1e9

    def asks(need):
        if isinstance(need, list):
            return max([0.0] + [asks(x) for x in need])
        if callable(need):
            return 0.0 if need() else BLOCKED
        return Q.when(need)

    class Task:
        def __init__(self, gen):
            self.gen, self.need, self.over, self.steps = gen, None, False, 0

        def at(self):
            return asks(self.need)

        def step(self):
            try:
                self.need = next(self.gen)
                self.steps += 1
            except StopIteration:
                self.over = True

    class Window:

        def __init__(self, gens, width, gate=None):
            self.rest, self.live, self.width = deque(gens), [], width
            self.over = not self.rest
            self.gate = gate
            self.begun = 0

        def options(self):
            for i, t in enumerate(self.live):
                if i == 0 or self.live[i - 1].steps > t.steps:
                    yield t.at(), t
            if self.rest and len(self.live) < self.width and (not self.live or self.live[-1].steps > 0):
                yield (0.0 if self.gate is None or self.gate(self.begun) else BLOCKED), None

        def at(self):
            return min((x[0] for x in self.options()), default=BLOCKED)

        def step(self):
            best = min(self.options(), key=lambda x: x[0])
            t = best[1]
            if t is None:
                t = Task(self.rest.popleft())
                self.live.append(t)
                self.begun += 1
            t.step()
            if t.over:
                self.live.remove(t)
            self.over = not self.rest and not self.live

    chains = {}

    def chain(name, work):
        chains.setdefault(name, deque()).append(work if isinstance(work, Window) else Task(work))

    def best():
        for c in chains.values():
            while c and c[0].over:
                c.popleft()
        live = [(c[0].at(), n) for n, c in chains.items() if c]
        return min(live) if live else (None, None)

    def pump(most=3):
        for _ in range(most):
            at_, name = best()
            if name is None or at_ > Q.clock["pe"]:
                return
            if max(Q.clock["act"], Q.clock["dve"]) > Q.clock["pe"] + AHEAD:
                return
            chains[name][0].step()

    AHEAD = 8.0

    def drain(*names):
        while True:
            at_, name = best()
            if name is None or (names and not any(chains.get(n) for n in names)):
                return
            assert at_ < BLOCKED
            chains[name][0].step()

    def run(gen):
        for _ in gen:
            pump()

    items = []

    def w_cols(w, c0, n, kt=KT):
        v = w.rearrange("(k p) c -> p k c", p=128)
        items.append(("w", v[:, 0:kt, c0:c0 + n], (kt, n)))

    def w_rows(w, k0, kn, c0, n):
        v = w.rearrange("(k p) c -> p k c", p=128)
        items.append(("w", v[:, k0:k0 + kn, c0:c0 + n], (kn, n)))

    def w_up(w, m):
        v = w.rearrange("(k p) (t c) -> p k t c", p=128, t=2)
        items.append(("w2", v[:, :, :, m * 128:(m + 1) * 128], (KT, 2, 128)))

    def plan_ffn(up, down):
        for half in range(2):
            for m in range(HALF):
                w_up(up, half * HALF + m)
            for k0, kn in ((0, 4), (4, 4), (8, 3)):
                w_rows(down, half * HALF + k0, kn, 0, 512)
            for m in range(4, 8):
                w_rows(down, half * HALF, HALF, m * 128, 128)

    def plan():
        w_in = I["w_in"][0]
        for c in range(14):
            w_cols(w_in, c * 256, 256)
        for c in range(4):
            w_cols(I["w_out"][0], c * 256, 256)
        for c in range(8):
            w_cols(I["w_kv_mem"][0], c * 256, 256)
        for c in range(4):
            w_cols(I["w_q_mem"][0], c * 256, 256)
        for c in range(4):
            w_cols(I["w_o_mem"][0], c * 256, 256)
        plan_ffn(I["w_gate_up"][0], I["w_down"][0])
        for l in range(2):
            plan_ffn(I["w_ffn_up_2"][l, 0], I["w_ffn_down_2"][l, 0])
            w2 = I["w_in_2"][l]
            w_cols(w2, 0, 256)
            w_cols(w2, 256, 256)
            w_cols(w2, 2560, 4)
            for c0 in (1792, 2048, 2304, 1024, 1280, 1536, 512, 768):
                w_cols(w2, c0, 256)
            for c in range(4):
                w_cols(I["w_out_2"][l], c * 256, 256)
            plan_ffn(I["w_ffn_up_2"][l, 1], I["w_ffn_down_2"][l, 1])

    plan()
    weights = items
    items = []
    ada = []
    for l in range(2):
        v = I["w_ada_2"][l].rearrange("(p k) n -> p k n", k=8)
        for n in range(18):
            for kh in range(2):
                ada.append(("ada", v[:, 4 * kh:4 * kh + 4, n * 512:(n + 1) * 512], (l, n, kh)))
    n1 = 14 + 4 + 8 + 4 + 4 + 36
    order = []
    ai = 0
    for wi, w in enumerate(weights):
        order.append(w)
        due = 36 * min(1.0, (wi + 1) / (n1 - 6)) if wi < n1 - 6 else 36 + 36 * min(1.0, (wi - n1 + 7) / 76)
        while ai < min(due, 72) - 1e-9:
            order.append(ada[ai])
            ai += 1
    order += ada[ai:]

    ws_free = [None] * NS
    ws_in = [None] * NS
    wh_free = [None] * NW
    ready = {}
    pos = {"dma": 0, "use": 0, "w": 0, "slab": 0}

    def emit_dma():
        i = pos["dma"]
        if i >= len(order):
            return
        pos["dma"] += 1
        kind, src, dims = order[i]
        s = i % NS
        if kind == "ada":
            dst = WS[:, s, :].rearrange("p (k n) -> p k n", k=4)
        elif kind == "w2":
            dst = WS[:, s, 0:2048].rearrange("p (k t c) -> p k t c", k=KT, t=2)
        else:
            dst = WS[:, s, 0:dims[0] * dims[1]].rearrange("p (k c) -> p k c", k=dims[0])
        if kind == "w2":
            for t in range(2):
                ws_in[s] = Q.dma(f"ws{s}", op_dma_start, (ws_free[s],), dst[:, :, t, :], src[:, :, t, :])
        else:
            ws_in[s] = Q.dma(f"ws{s}", op_dma_start, (ws_free[s],), dst, src)

    pend = []
    acc_free = [None]
    mod_tok = [None, None]

    def flush_ada():
        while pend:
            l, n, tok = pend.pop(0)
            b = take()
            for q in range(4):
                t = mm(PB[b][:, q:q + 1], ACC[:, q * 128:(q + 1) * 128], CB[:, C_ONE:C_ONE + 1],
                       True, True, free[b], tok, cb_in, mark=(q == 3))
            acc_free[0] = t
            bias = PC[:, 196 + 72 * l + 4 * n:196 + 72 * l + 4 * n + 4]
            free[b] = Q.dve(op_tensor_tensor, (t, pc_tok,), MOD[:, l, 4 * n:4 * n + 4], PB[b][:, 0:4], bias, ALU.add)
            mod_tok[l] = free[b]

    def flushing():
        yield [x[2] for x in pend]
        flush_ada()

    def emit_use():
        i = pos["use"]
        pos["use"] += 1
        kind, src, dims = order[i]
        s = i % NS
        if kind == "ada":
            l, n, kh = dims
            if kh == 0:
                flush_ada()
            t = None
            for q in range(4):
                w = WS[:, s, q * 512:(q + 1) * 512]
                c = CS[:, 4 * kh + q:4 * kh + q + 1]
                if kh == 0 and q == 0:
                    t = Q.dve(op_tensor_scalar, (ws_in[s], acc_free[0], cs_tok,), ACC[:, :], w, c, None, ALU.mult)
                else:
                    t = Q.dve(op_scalar_tensor_tensor, (ws_in[s], Q.last("dve"),), out=ACC[:, :], in0=w, scalar=c, in1=ACC[:, :], op0=ALU.mult, op1=ALU.add)
            ws_free[s] = t
            if kh == 1:
                pend.append((l, n, t))
        else:
            j = pos["w"]
            pos["w"] += 1
            n = int(np.prod(dims))
            h = j % NW
            hi = Q.act(op_activation, (ws_in[s], wh_free[h],), WH[:, h, 0:n], WS[:, s, 0:n], ACT.Copy)
            lo = Q.dve(op_tensor_tensor, (ws_in[s], hi, wh_free[h],), WL[:, h, 0:n], WS[:, s, 0:n], f(WH[:, h, 0:n]), ALU.subtract)
            ws_free[s] = lo
            ready[j] = [hi, lo]
        emit_dma()

    def use_until(j):
        while pos["w"] <= j and pos["use"] < len(order):
            emit_use()

    def next_slab():
        i = pos["slab"]
        pos["slab"] += 1
        use_until(i)
        use_until(i + 2)
        if pend and not chains.get("ada"):
            chain("ada", flushing())
        kind, _, dims = weights[i]
        h = i % NW
        n = int(np.prod(dims))
        if kind == "w2":
            vh = WH[:, h, 0:n].rearrange("p (k t c) -> p k t c", k=dims[0], t=2)
            vl = WL[:, h, 0:n].rearrange("p (k t c) -> p k t c", k=dims[0], t=2)
        else:
            vh = WH[:, h, 0:n].rearrange("p (k c) -> p k c", k=dims[0])
            vl = WL[:, h, 0:n].rearrange("p (k c) -> p k c", k=dims[0])
        return i, vh, vl, ready[i]

    def done_slab(i, tok):
        wh_free[i % NW] = tok

    def mm3_w(out_, wh, wl, xh, xl, start, stop, *after, mark=False, skip=False):
        mm(out_, wh, xh, start, False, *after, skip=skip)
        mm(out_, wh, xl, False, False, skip=skip)
        return mm(out_, wl, xh, False, stop, mark=mark, skip=skip)

    def mm3_x(out_, xh, xl, wh, wl, start, stop, *after, mark=False):
        mm(out_, xh, wh, start, False, *after)
        mm(out_, xh, wl, False, False)
        return mm(out_, xl, wh, False, stop, mark=mark)

    def proj_fm(ntile, xh, xl, xt, evac, kouter, ntok=S, m0=0, unit=2, ks=tuple(range(KT))):
        i, vh, vl, wt = next_slab()
        banks = [take(True) for _ in range(ntile)]
        seq = [(k, m) for k in ks for m in range(ntile)] if kouter else \
              [(k, m) for m in range(ntile) for k in ks]
        for c, (k, m) in enumerate(seq):
            first, last = k == ks[0], k == ks[-1]
            t = mm3_w(PB[banks[m]][:, 0:ntok], vh[:, k, m * 128:(m + 1) * 128],
                      vl[:, k, m * 128:(m + 1) * 128], xh[:, k, 0:ntok], xl[:, k, 0:ntok], first, last,
                      wt, xt[k], free[banks[m]] if first else None, mark=last)
            if last:
                let_go(banks[m], evac(m0 + m, PB[banks[m]][:, 0:ntok], t))
                done_slab(i, t)
            if c % unit == unit - 1:
                yield

    def proj_tm(ntok, xh, xl, xt, evac):
        i, vh, vl, wt = next_slab()
        for b2 in range(ntok // 2):
            b = take(True)
            for u in range(2):
                j = 2 * b2 + u
                for k in range(KT):
                    t = mm3_x(PB[b][:, u * 256:(u + 1) * 256], xh[:, k, j * 128:(j + 1) * 128],
                              xl[:, k, j * 128:(j + 1) * 128], vh[:, k, :], vl[:, k, :],
                              k == 0, k == KT - 1, wt, xt[k], free[b] if k == 0 and u == 0 else None,
                              mark=(k == KT - 1))
                    if k % 4 == 3:
                        yield
            done_slab(i, t)
            let_go(b, evac(b2, PB[b][:, :].rearrange("p (u c) -> p u c", u=2), t))

    small = [0]

    def stat(tile, b, sel, ng, first, tok, col=0, ntok=TT, last=True):
        for j in range(ntok):
            t = mm(PB[b][:, col + j * ng:col + (j + 1) * ng], tile[:, j * 128:(j + 1) * 128], sel,
                   first and j == 0, last and j == ntok - 1, tok, cb_in,
                   free[b] if first and j == 0 else None, mark=(j == ntok - 1), skip=True)
        return t

    def root(b, n, scale, eps, tok):
        s = small[0] % NSM
        small[0] += 1
        a = Q.act(op_activation, (tok, eps_tok, Q.last("dve"),), SD[:, s, 0:n], PB[b][:, 0:n], ACT.Sqrt, bias=EPS[:, eps:eps + 1],
                                         scale=scale)
        free[b] = a
        r = Q.dve(op_reciprocal, (a, Q.last("pe"),), RC[:, s, 0:n], SD[:, s, 0:n])
        return s, r

    def spread(b, s, ng, tok, ntok=TT):
        w = 128 // ng
        for j in range(ntok):
            for g in range(ng):
                c = j * ng + g
                t = mm(PB[b][g * w:(g + 1) * w, j * 128:(j + 1) * 128], RC[:, s, c:c + 1].to_broadcast([128, w]),
                       ident, True, True, tok, free[b] if j == 0 else None,
                       mark=(j == ntok - 1 and g == ng - 1))
        return t

    one = CB[:, C_ONE:C_ONE + 1]
    x_tok = [None] * KT
    sq_free = [None, None]
    h_tok = [None] * KT
    sqn = [0]

    def square(src, tok):
        i = sqn[0] % 2
        sqn[0] += 1
        t = Q.act(op_activation, (tok, sq_free[i],), SQ[:, i, :], src, ACT.Square)
        return i, t

    def watch(tile, toks, sqs, least=1):
        for m in range(KT):
            if len(toks) <= max(m, least - 1):
                yield lambda m=m: len(toks) > max(m, least - 1)
            i, sq = square(tile(m), toks[m])
            yield sq
            sqs.append(add_stat(i, sq, 6, m == 0, m == KT - 1))

    def add_stat(i, t, b, first, last):
        u = stat(SQ[:, i, :], b, one, 1, first, t, last=last)
        sq_free[i] = u
        return u

    def make_h(a_col, s_col, rb, rt, par):
        for k in range(KT):
            i = k % 2
            t = Q.dve(op_scalar_tensor_tensor, (rt, x_tok[k], par, Q.last("act") if k == 0 else None, Q.last("dve") if k == 0 else None,), out=TM[:, i, :], in0=X[:, k, :], scalar=a_col(k), in1=PB[rb][:, :], op0=ALU.mult,
                op1=ALU.mult)
            if k == KT - 1:
                free[rb] = t
            if s_col is None:
                hi = Q.act(op_activation, (t,), HH[:, k, :], TM[:, i, :], ACT.Copy)
                lo = Q.dve(op_tensor_tensor, (t, hi,), HL[:, k, :], TM[:, i, :], f(HH[:, k, :]), ALU.subtract)
            else:
                hi = Q.act(op_activation, (t, par,), HH[:, k, :], TM[:, i, :], ACT.Identity,
                                                            bias=s_col(k))
                lo = Q.dve(op_scalar_tensor_tensor, (t, hi,), out=HL[:, k, :], in0=TM[:, i, :], scalar=s_col(k), in1=f(HH[:, k, :]), op0=ALU.add,
                    op1=ALU.subtract)
            h_tok[k] = [hi, lo]
            yield

    def rms_h(tok, a_col, s_col, par, sb=6, rb=5):
        s, r = root(sb, TT, 1.0 / D, 0, tok)
        yield r
        rt = spread(rb, s, 1, r)
        yield from make_h(a_col, s_col, rb, rt, par)

    def split_into(k, src, tok):
        hi = Q.act(op_activation, (tok,), HH[:, k, :], src, ACT.Copy)
        lo = Q.dve(op_tensor_tensor, (tok, hi,), HL[:, k, :], src, f(HH[:, k, :]), ALU.subtract)
        h_tok[k] = [hi, lo]

    x_in = [Q.dma(f"x{j}", op_dma_start, (), XTM[:, j, :], I["x"][0, j * 128:(j + 1) * 128, :])
            for j in range(2)]
    cb_in = Q.dma("cb", op_dma_start, (), CB[:, :], I["c_b"], engine="act")
    x_in += [Q.dma(f"x{j}", op_dma_start, (), XTM[:, j, :], I["x"][0, j * 128:(j + 1) * 128, :])
             for j in range(2, 4)]

    z_tok = Q.pool(op_memset, (), PR[:, :, :], 0.0)
    pr = []
    at_row = 0

    def rows(tile, r0, v, w=128):
        pr.append(Q.dma("pr", op_dma_start, (z_tok,), PR[r0:r0 + v.shape[0], tile, 0:v.shape[1]], v, engine="act"))

    gains = {}
    for name in ("pre_mix_g", "post_mix_g", "pre_mem_g", "post_mem_g", "mem_norm_g", "pre_ffn_g",
                 "post_ffn_g"):
        rows(0, at_row, I[name][0].rearrange("(a b) -> a b", b=128))
        gains[name] = at_row
        at_row += 8
    for name in ("attn_gn_g", "ret_gn_g"):
        rows(0, at_row, I[name][0].rearrange("(a b) -> a b", b=128))
        gains[name] = at_row
        at_row += 4
    P2 = {}
    for l in range(2):
        at_row = 0

        def add(name, v, n):
            nonlocal at_row
            rows(1 + l, at_row, v)
            P2[(name, l)] = 64 + 66 * l + at_row
            at_row += n

        add("g_norm", I["g_norm_2"][l].rearrange("j (a b) -> (j a) b", b=128), 24)
        add("conv_w", I["conv_w_2"][l].rearrange("j (a b) -> (j a) b", b=128), 16)
        for nm in ("conv_b_2", "b_rgate_2", "b_igate_2", "lru_lambda_2"):
            add(nm, I[nm][l].rearrange("(a b) -> a b", b=128), 4)
        add("g_mix", I["g_mix_out_2"][l].rearrange("(a b) -> a b", b=128), 8)
        for u in range(2):
            pr.append(Q.dma("pr", op_dma_start, (z_tok,), PR[at_row:at_row + 2, 1 + l, 64 * u:64 * u + 64], I["g_qk_2"][l], engine="act"))
        P2[("g_qk", l)] = 64 + 66 * l + at_row
        rows(3 + l, 0, I["b_ada_2"][l].rearrange("(a b) -> a b", b=128))
    pr_tok = pr[-1]
    cc_in = Q.dma("cc", op_dma_start, (), CC[:, :], I["c_2"].rearrange("o (p k) -> p (o k)", k=8), engine="act")
    msk_in = Q.dma("ct", op_dma_start, (), MSK[:, :], I["c_t"][:, T_MASK:T_MASK + 512], engine="act")
    rope_in = Q.dma("ct", op_dma_start, (), ROPE[:, :, :], I["c_t"][:, T_ROPE:T_DEC].rearrange("p (a b) -> p a b", a=4), engine="act")
    for _ in range(NS):
        emit_dma()

    e0 = Q.dve(op_memset, (), EPS[:, 0:1], RMS_EPS)
    e0 = Q.dve(op_memset, (), EPS[:, 1:2], GN_EPS)
    eps_tok = Q.dve(op_memset, (), EPS[:, 2:3], 1.0)

    for m in range(KT):
        b = take()
        for j in range(TT):
            t = Q.pe(op_transpose, (x_in[j], cb_in, free[b] if j == 0 else None,), PB[b][:, j * 128:(j + 1) * 128], XTM[:, j, m * 128:(m + 1) * 128], ident, mark=(j == TT - 1))
        if m % 2:
            x_tok[m] = free[b] = Q.act(op_activation, (t,), X[:, m, :], PB[b][:, :], ACT.Copy)
        else:
            x_tok[m] = free[b] = Q.dve(op_tensor_copy, (t,), X[:, m, :], PB[b][:, :])
    for m in range(KT):
        i, t = square(X[:, m, :], x_tok[m])
        st = add_stat(i, t, 6, m == 0, m == KT - 1)

    widths = [(0, 0, 64), (1, 64, 66), (2, 130, 66), (3, 196, 72), (4, 268, 72)]
    b = 4
    for tl, c0, w in widths:
        t = Q.pe(op_transpose, (pr_tok, z_tok, cb_in, free[4],), PB[4][:, 0:128], PR[:, tl, :], ident, mark=True)
        pc_tok = free[4] = Q.dve(op_tensor_copy, (t,), PC[:, c0:c0 + w], PB[4][:, 0:w])
    cs_tok = Q.act(op_activation, (cc_in,), CS[:, :], CC[:, :], ACT.Silu)

    def col(c):
        return PC[:, c:c + 1]

    def gcol(name):
        return lambda k: col(gains[name] + k)

    chain("s", rms_h(st, gcol("pre_mix_g"), None, pc_tok))
    drain()

    rp = {}
    rope_n = [0]
    tm_free = [None, None]

    def after(need, fn):
        yield need
        fn()

    def rope_out(dst, table, perm, banks, key):
        def evac(m, ps, t):
            i = rope_n[0] % 2
            rope_n[0] += 1
            c = Q.act(op_activation, (t, sq_free[i], Q.last("dve"),), SQ[:, i, :], ps, ACT.Copy)
            bk = banks[i % len(banks)]

            def rest():
                p = mm(PB[bk][:, :], CB[:, perm:perm + 128], SQ[:, i, :], True, True, c, free[bk], mark=True)
                u = Q.dve(op_tensor_tensor, (c, rope_in, tm_free[i],), TM[:, i, :], SQ[:, i, :], ROPE[:, table, :], ALU.mult)
                v = Q.dve(op_tensor_tensor, (p,), dst[:, m, :], PB[bk][:, :], ROPE[:, table + 1, :],
                                                    ALU.mult)
                free[bk] = v
                sq_free[i] = [u, p]
                rp[key, m] = Q.dve(op_tensor_tensor, (u, v,), dst[:, m, :], dst[:, m, :], TM[:, i, :],
                                                             ALU.add)
                tm_free[i] = rp[key, m]
            chain("rope", after(c, rest))
            return c
        return evac

    for c in range(2):
        run(proj_fm(2, HH, HL, h_tok, rope_out(AQ, 0, C_PA, (4, 5), "aq"), c == 0, m0=2 * c))
    for c in range(2):
        run(proj_fm(2, HH, HL, h_tok, rope_out(AK, 0, C_PA, (4, 5), "ak"), False, m0=2 * c))

    def tm_out(dst, c, key):
        def evac(b2, ps, t):
            tk = Q.act(op_activation, (t,), dst[:, 2 * b2:2 * b2 + 2, c * 256:(c + 1) * 256], ps, ACT.Copy)
            rp[key, c, b2] = tk
            return tk
        return evac

    for c in range(2):
        run(proj_tm(TT, HH, HL, h_tok, tm_out(AV, c, "av")))
    pump(3)

    sm_free = [None] * 4

    def soft_attention(items, score, n_of, ss, pt, finish, ptb, shift=0):
        ssf = [None] * len(ss)
        ptf = [None] * len(pt)
        over = set()

        def item(it, h, i):
            a, p, sm = it % len(ss), it % len(pt), it % 4
            n = n_of(i)
            tok = score(h, i, 4 + it % 2 if ptb == 6 else 4, ss[a], SM[:, sm, :], ssf[a])
            yield [tok, lambda: it < len(pt) or it - len(pt) in over]
            tb = take() if ptb is None else ptb
            for j in range(n // 128):
                t = Q.pe(op_transpose, (tok, free[tb] if j == 0 else None), PB[tb][:, j * 128:(j + 1) * 128],
                         ss[a][:, j * 128:(j + 1) * 128], ident, mark=(j == n // 128 - 1))
            ssf[a] = t
            c = free[tb] = Q.act(op_activation, (t, ptf[p]), pt[p][:, 0:n], PB[tb][:, 0:n], ACT.Copy)
            yield c
            ptf[p] = finish(h, i, pt[p], c, n // 128)
            over.add(it)

        return [item(it, h, i) for it, (h, i) in enumerate(items)]

    def norm_rows(sstile, sm, n, tok):
        r = Q.dve(op_reciprocal, (tok,), sm[:, 3:4], sm[:, 2:3])
        return Q.dve(op_tensor_scalar, (tok, r,), sstile[:, 0:n], sstile[:, 0:n], sm[:, 3:4], None, ALU.mult)

    def dil_score(h, i, sb, sst, sm, f1):
        n = 128 * (i + 1)
        po, m = 64 * (h % 2), h // 2
        t = mm(PB[sb][:, 0:n], AQ[po:po + 64, m, i * 128:(i + 1) * 128], AK[po:po + 64, m, 0:n], True, True,
               rp["aq", m], rp["ak", m], free[sb], mark=True)
        a = Q.dve(op_tensor_tensor_reduce, (t, msk_in, f1), out=sst[:, 0:n], in0=PB[sb][:, 0:n], in1=MSK[:, 512 - n:512], scale=0.125, scalar=-3e38,
            op0=ALU.add, op1=ALU.max, accum_out=sm[:, 0:1])
        free[sb] = a
        g = Q.dve(op_tensor_scalar, (a,), sm[:, 1:2], sm[:, 0:1], -1.0, None, ALU.mult)
        x = Q.act(op_activation, (g,), sst[:, 0:n], sst[:, 0:n], ACT.Exp, bias=sm[:, 1:2],
                                         accum_out=sm[:, 2:3])
        return norm_rows(sst, sm, n, x)

    an = {}

    def att_norm(m, src, gain, key, dst=None):
        i, t = square(src[:, m, :], an[key, m])
        yield t
        u = stat(SQ[:, i, :], 6, CB[:, C_SEL:C_SEL + 2], 2, True, t)
        sq_free[i] = u
        s, r = root(6, 2 * TT, 1.0 / 64, 0, u)
        yield r
        rt = spread(6, s, 2, r)
        an[key, m] = free[6] = Q.dve(op_scalar_tensor_tensor, (rt, t, pc_tok, Q.last("dve"),), out=src[:, m, :], in0=src[:, m, :], scalar=gain, in1=PB[6][:, :], op0=ALU.mult, op1=ALU.mult)
        yield

    def head_pair_finish(v, vkeys, dst, key):
        def finish(h, i, ptt, tok, blocks):
            po, m = 64 * (h % 2), h // 2
            for j in range(blocks):
                t = mm(PB[7][po:po + 64, i * 128:(i + 1) * 128], v[:, j, h * 64:(h + 1) * 64],
                       ptt[:, j * 128:(j + 1) * 128], j == 0, j == blocks - 1, tok,
                       [rp[k] for k in vkeys(h)], free[7] if h % 2 == 0 and i == TT - 1 else None,
                       mark=(j == blocks - 1))
            if h % 2 == 1 and i == 0:
                an[key, m] = free[7] = Q.act(op_activation, (t,), dst[:, m, :], PB[7][:, :], ACT.Copy)
            return t
        return finish

    SSX = region("SSX", 25, [128, 2, S])
    chain("s", Window(soft_attention(
        [(h, i) for h in range(8) for i in (3, 2, 1, 0)], dil_score, lambda i: 128 * (i + 1),
        [SS[:, 0, :], SS[:, 1, :], SSX[:, 0, :], SSX[:, 1, :]], [PT[:, 0, :], PT[:, 1, :]],
        head_pair_finish(AV, lambda h: [("av", h // 4, 0), ("av", h // 4, 1)], AQ, "a"), 6), 4))
    for m in range(4):
        chain("s", att_norm(m, AQ, col(gains["attn_gn_g"] + m), "a"))

    for c in range(2):
        run(proj_fm(2, HH, HL, h_tok, rope_out(RQ, 2, C_PR, (6,), "rq"), False, m0=2 * c))
    for c in range(2):
        run(proj_fm(2, HH, HL, h_tok, rope_out(RK, 2, C_PR, (6,), "rk"), False, m0=2 * c))
    drain("rope")
    rope_done = Q.last("dve")
    DEC = region("DEC", 27, [128, 2, 512])
    dec_free = [rope_done, rope_done]
    dec_in = {}

    def load_dec(h):
        dec_in[h] = Q.dma(f"dec{h % 2}", op_dma_start, (dec_free[h % 2],), DEC[:, h % 2, :],
                          I["c_t"][:, T_DEC + h * 512:T_DEC + (h + 1) * 512])

    for h in range(2):
        load_dec(h)
    for c in range(2):
        run(proj_tm(TT, HH, HL, h_tok, tm_out(RV, c, "rv")))

    def ret():
        ssf = [None, None]

        def item(it, h, j):
            n = S - 128 * j
            sb = 4 + it % 2
            if j == 0 and 1 <= h < 3:
                dec_free[(h + 1) % 2] = Q.last("dve")
                load_dec(h + 1)
            t = mm(PB[sb][:, 0:n], RK[:, h, j * 128:(j + 1) * 128], RQ[:, h, j * 128:S], True, True,
                   rp["rq", h], rp["rk", h], free[sb], mark=True)
            sc = free[sb] = Q.dve(op_tensor_tensor, (t, dec_in[h], ssf[it % 2]), SS[:, it % 2, 0:n], PB[sb][:, 0:n],
                                  DEC[:, h % 2, 0:n], ALU.mult)
            yield sc
            t = mm(PB[7][:, j * 128:S], RV[:, j, h * 128:(h + 1) * 128], SS[:, it % 2, 0:n], j == 0, j == 3,
                   sc, rp["rv", h // 2, 0], rp["rv", h // 2, 1], free[7] if j == 0 else None, mark=True)
            ssf[it % 2] = t
            if j == 3:
                rp["r", h] = free[7] = Q.act(op_activation, (t,), RQ[:, h, :], PB[7][:, :], ACT.Copy)

        return [item(4 * h + j, h, j) for h in range(4) for j in range(4)]

    def ret_norm(h):
        yield rp["r", h]
        u = stat(RQ[:, h, :], 6, one, 1, True, rp["r", h])
        s = small[0] % NSM
        small[0] += 1
        c = Q.dve(op_tensor_scalar, (u,), RC[:, s, 0:TT], PB[6][:, 0:TT], 1.0 / 128, None, ALU.mult)
        free[6] = c
        yield c
        rt = spread(6, s, 1, c)
        d = free[6] = Q.dve(op_tensor_tensor, (rt, rp["r", h],), RQ[:, h, :], RQ[:, h, :], PB[6][:, :], ALU.subtract)
        i, t = square(RQ[:, h, :], d)
        yield t
        u = stat(SQ[:, i, :], 6, one, 1, True, t)
        sq_free[i] = u
        s, r = root(6, TT, 1.0 / 128, 1, u)
        yield r
        rt = spread(6, s, 1, r)
        v = free[6] = Q.dve(op_scalar_tensor_tensor, (rt, t, d,), out=RQ[:, h, :], in0=RQ[:, h, :], scalar=col(gains["ret_gn_g"] + h), in1=PB[6][:, :],
            op0=ALU.mult, op1=ALU.mult)
        rp["rn", h] = v

    chain("s", Window(ret(), 2))
    chain("s", Window([ret_norm(h) for h in range(4)], 2))

    def rg_out(m, ps, t):
        rp["rg", m] = Q.act(op_activation, (t, dil_done,), RG[:, m, :], ps, ACT.Silu)
        return rp["rg", m]

    while not all(("a", m) in an for m in range(4)) or any(isinstance(w, Task) for w in list(chains["s"])[:1]):
        chains["s"][0].step()
        best()
    dil_done = Q.last("pe", "dve")
    for c in range(2):
        run(proj_fm(2, HH, HL, h_tok, rg_out, False, m0=2 * c))
    h_free = Q.last("pe")
    for m in range(4):
        split_into(m, AQ[:, m, :], [an["a", m], h_free])
    drain()
    for h in range(4):
        g = Q.dve(op_tensor_tensor, (rp["rn", h], rp["rg", h]), RQ[:, h, :], RQ[:, h, :], RG[:, h, :], ALU.mult)
        split_into(4 + h, RQ[:, h, :], g)

    y_tok = {}

    def y_evac(dst, toks):
        def evac(m, ps, t):
            y_tok[m] = Q.act(op_activation, (t,), dst[:, m, :], ps, ACT.Copy)
            toks.append(y_tok[m])
            return y_tok[m]
        return evac

    def post(src, gname, a_col, s_col, par, sqs):
        s, r = root(6, TT, 1.0 / D, 0, sqs[-1])
        yield r
        rt = spread(5, s, 1, r)
        last = None
        for m in range(KT):
            i = m % 2
            t = Q.dve(op_scalar_tensor_tensor, (rt, y_tok[m], pc_tok,), out=TM[:, i, :], in0=src[:, m, :], scalar=col(gains[gname] + m), in1=PB[5][:, :],
                op0=ALU.mult, op1=ALU.mult)
            if m == KT - 1:
                free[5] = t
            x_tok[m] = Q.dve(op_tensor_tensor, (t,), X[:, m, :], X[:, m, :], TM[:, i, :], ALU.add)
            q, sq = square(X[:, m, :], x_tok[m])
            if m:
                add_stat(last[0], last[1], 6, m == 1, False)
            last = (q, sq)
            yield sq
        st2 = add_stat(last[0], last[1], 6, False, True)
        yield from rms_h(st2, a_col, s_col, par)

    mem_tok = {}

    def mem_load():
        w = Q.last("pe", "act", "dve")
        mem_in = Q.dma("mem", op_dma_start, (w,), MTM[:, :, :], I["mem"][0].rearrange("(a p) d -> p a d", p=128), engine="act")
        yield mem_in
        s = small[0] % NSM
        small[0] += 1
        for a in range(2):
            for hf in range(2):
                t = Q.act(op_activation, (mem_in, sq_free[0], sq_free[1], Q.last("act"),), SQ[:, hf, :], MTM[:, a, hf * 512:(hf + 1) * 512], ACT.Square,
                    accum_out=SD[:, s, 4 + 2 * a + hf:5 + 2 * a + hf])
        sq_free[0] = sq_free[1] = t
        u = Q.dve(op_tensor_tensor, (t,), SD[:, s, 8:10], SD[:, s, 4:8:2], SD[:, s, 5:8:2], ALU.add)
        v = Q.act(op_activation, (u,), SD[:, s, 0:2], SD[:, s, 8:10], ACT.Sqrt, bias=EPS[:, 0:1],
                                         scale=1.0 / D)
        r = Q.dve(op_reciprocal, (v,), RC[:, s, 0:2], SD[:, s, 0:2])
        for a in range(2):
            sc = Q.act(op_activation, (r, t,), MTM[:, a, :], MTM[:, a, :], ACT.Copy, scale=RC[:, s, a:a + 1])
        yield sc
        for k in range(KT):
            bk = 4
            for a in range(2):
                p = Q.pe(op_transpose, (sc, free[bk] if a == 0 else None,), PB[bk][:, a * 128:(a + 1) * 128], MTM[:, a, k * 128:(k + 1) * 128], ident, mark=(a == 1))
            hi = Q.act(op_activation, (p, w,), MH[:, k, :], PB[bk][:, 0:NMEM], ACT.Copy,
                                                   scale=col(gains["mem_norm_g"] + k))
            lo = Q.dve(op_scalar_tensor_tensor, (hi, w,), out=ML[:, k, :], in0=PB[bk][:, 0:NMEM], scalar=col(gains["mem_norm_g"] + k),
                in1=f(MH[:, k, :]), op0=ALU.mult, op1=ALU.subtract)
            free[bk] = lo
            mem_tok[k] = [hi, lo]
            yield lo

    chain("s", mem_load())
    sqs, yt = [], []
    chain("w", watch(lambda m: Y[:, m, :], yt, sqs))
    for c in range(4):
        run(proj_fm(2, HH, HL, h_tok, y_evac(Y, yt), c == 0, m0=2 * c))
    drain()
    chain("s", post(Y, "post_mix_g", gcol("pre_mem_g"), None, pc_tok, sqs))
    km = {}

    def km_out(m, ps, t):
        km[m] = Q.act(op_activation, (t,), KM[:, m, :], ps, ACT.Copy)
        return km[m]

    def vm_out(c):
        def evac(b2, ps, t):
            km["v", c] = Q.act(op_activation, (t,), VM[:, :, c * 256:(c + 1) * 256], ps, ACT.Copy)
            return km["v", c]
        return evac

    for c in range(4):
        run(proj_fm(2, MH, ML, mem_tok, km_out, False, ntok=NMEM, m0=2 * c))
    for c in range(4):
        run(proj_tm(2, MH, ML, mem_tok, vm_out(c)))
    drain()

    xq = {}

    def xq_out(m, ps, t):
        xq[m] = Q.act(op_activation, (t,), XQ[:, m, :], ps, ACT.Copy)
        return xq[m]

    def x_score(h, i, sb, sst, sm, f1):
        for c in range(2):
            t = mm(PB[sb][:, 0:NMEM], XQ[:, 2 * h + c, i * 128:(i + 1) * 128], KM[:, 2 * h + c, :], c == 0,
                   c == 1, xq[2 * h + c], km[2 * h + c], free[sb] if c == 0 else None, mark=(c == 1))
        a = Q.dve(op_tensor_reduce, (t,), sm[:, 0:1], PB[sb][:, 0:NMEM], AX.X, ALU.max)
        g = Q.dve(op_tensor_scalar, (a,), sm[:, 1:2], sm[:, 0:1], -1.0 / 16, None, ALU.mult)
        x = Q.act(op_activation, (g, f1,), sst[:, 0:NMEM], PB[sb][:, 0:NMEM], ACT.Exp, bias=sm[:, 1:2],
                                         scale=1.0 / 16, accum_out=sm[:, 2:3])
        free[sb] = x
        return norm_rows(sst, sm, NMEM, x)

    ox = {}

    def x_finish(h, i, ptt, tok, blocks):
        for c in range(2):
            bk = 7 - c
            for a in range(2):
                t = mm(PB[bk][:, i * 128:(i + 1) * 128], VM[:, a, h * 256 + c * 128:h * 256 + (c + 1) * 128],
                       ptt[:, a * 128:(a + 1) * 128], a == 0, a == 1, tok, km["v", h],
                       free[bk] if i == 0 else None, mark=(a == 1))
            if i == TT - 1:
                ox[2 * h + c] = free[bk] = Q.act(op_activation, (t,), XQ[:, 2 * h + c, :], PB[bk][:, :], ACT.Copy)
        return t

    chain("s", Window(soft_attention(
        [(h, i) for h in range(4) for i in range(TT)], x_score, lambda i: NMEM,
        [XS[:, i, :] for i in range(4)], [XP[:, i, :] for i in range(4)], x_finish, 5), 4,
        gate=lambda it: (2 * (it // TT) + 1) in xq))
    for h in range(4):
        run(proj_fm(2, HH, HL, h_tok, xq_out, h == 0, m0=2 * h))
    q_done = Q.last("pe")
    drain()
    for k in range(KT):
        split_into(k, XQ[:, k, :], [ox[k], q_done])
    sqs, yt = [], []
    y_done = Q.last("act", "dve")

    def y_evac2(m, ps, t):
        return y_evac(Y, yt)(m, ps, [t, y_done])

    chain("w", watch(lambda m: Y[:, m, :], yt, sqs))
    for c in range(4):
        run(proj_fm(2, HH, HL, h_tok, y_evac2, c == 0, m0=2 * c))
    drain()
    chain("s", post(Y, "post_mem_g", gcol("pre_ffn_g"), None, pc_tok, sqs))
    drain()

    gh_free = [None] * HALF
    sg_free = [None, None]

    def ffn(down_evac):
        for half in range(2):
            g_tok = [None] * HALF

            def up(m):
                i, vh, vl, wt = next_slab()
                b2 = [take(True), take(True)]
                seq = [(k, u) for k in range(KT) for u in range(2)] if m == 0 else \
                      [(k, u) for u in range(2) for k in range(KT)]
                t2 = [None, None]
                for n, (k, u) in enumerate(seq):
                    t = mm3_w(PB[b2[u]][:, :], vh[:, k, u, :], vl[:, k, u, :], HH[:, k, :], HL[:, k, :],
                              k == 0, k == KT - 1, wt, h_tok[k], free[b2[u]] if k == 0 else None,
                              mark=(k == KT - 1))
                    if k == KT - 1:
                        t2[u] = t
                        if u == 0:
                            sg = Q.act(op_activation, (t, sg_free[m % 2],), SG[:, m % 2, :], PB[b2[0]][:, :], ACT.Silu)
                            let_go(b2[0], sg)
                    if n % 2:
                        yield
                done_slab(i, t2[1])
                p = Q.dve(op_tensor_tensor, (t2[1], sg, Q.last("dve"),), TM[:, m % 2, :], PB[b2[1]][:, :], SG[:, m % 2, :],
                                                    ALU.mult)
                sg_free[m % 2] = p
                let_go(b2[1], p)
                hi = Q.act(op_activation, (p, gh_free[m],), GH[:, m, :], TM[:, m % 2, :], ACT.Copy)
                lo = Q.dve(op_tensor_tensor, (hi, p, gh_free[m],), GL[:, m, :], TM[:, m % 2, :], f(GH[:, m, :]),
                                                     ALU.subtract)
                g_tok[m] = [hi, lo]

            for m in range(HALF):
                yield from up(m)
            for k0, kn in ((0, 4), (4, 4), (8, 3)):
                i, vh, vl, wt = next_slab()
                for kk in range(kn):
                    k = k0 + kk
                    for m in range(4):
                        t = mm3_w(PB[4 + m][:, :], vh[:, kk, m * 128:(m + 1) * 128],
                                  vl[:, kk, m * 128:(m + 1) * 128], GH[:, k, :], GL[:, k, :], k == 0,
                                  k == HALF - 1, wt, g_tok[k], free[4 + m] if k == 0 else None,
                                  mark=(k == HALF - 1 or (m == 3 and kk == kn - 1)))
                        if k == HALF - 1:
                            free[4 + m] = down_evac(half, m, PB[4 + m][:, :], t)
                        if m % 2:
                            yield
                done_slab(i, t)
            for m in range(4, 8):
                i, vh, vl, wt = next_slab()
                b = take(True)
                for k in range(HALF):
                    t = mm3_w(PB[b][:, :], vh[:, k, :], vl[:, k, :], GH[:, k, :], GL[:, k, :], k == 0,
                              k == HALF - 1, wt, g_tok[k], free[b] if k == 0 else None,
                              mark=(k == HALF - 1 or m == 7))
                    if m == 7:
                        gh_free[k] = t
                    if k % 2:
                        yield
                done_slab(i, t)
                let_go(b, down_evac(half, m, PB[b][:, :], t))

    def ffn1_evac(half, m, ps, t):
        if half == 0:
            y_tok[m] = Q.act(op_activation, (t,), Y1[:, m, :], ps, ACT.Copy)
            return y_tok[m]
        y_tok[m] = Q.dve(op_tensor_tensor, (t, y_tok[m],), Y1[:, m, :], ps, Y1[:, m, :], ALU.add)
        yt.append(y_tok[m])
        return y_tok[m]

    sqs, yt = [], []
    chain("w", watch(lambda m: Y1[:, m, :], yt, sqs, 4))
    run(ffn(ffn1_evac))
    drain()
    flush_ada()

    def mod_cols(l):
        g0 = P2["g_norm", l]
        toks = []
        for j in range(3):
            c = (3 * j + 1) * 8
            toks.append(Q.dve(op_scalar_tensor_tensor, (mod_tok[l], pc_tok, Q.last("pe", "act"),), out=MA[:, 8 * j:8 * j + 8], in0=MOD[:, l, c:c + 8], scalar=1.0, in1=PC[:, g0 + 8 * j:g0 + 8 * j + 8],
                op0=ALU.add, op1=ALU.mult))
            c2 = (3 * j + 2) * 8
            hf = 1.0 if j == 1 else 0.5
            toks.append(Q.dve(op_tensor_scalar, (mod_tok[l],), MG[:, 8 * j:8 * j + 8], MOD[:, l, c2:c2 + 8], hf, hf, ALU.mult, ALU.add))
        return toks[-1]

    def a2(j):
        return lambda k: MA[:, 8 * j + k:8 * j + k + 1]

    def s2(l, j):
        return lambda k: MOD[:, l, 24 * j + k:24 * j + k + 1]

    def g2(j):
        return lambda k: MG[:, 8 * j + k:8 * j + k + 1]

    def x_add(j, toks):
        def evac(m, ps, t, whole=True):
            x_tok[m] = Q.dve(op_scalar_tensor_tensor, (t, x_tok[m]), out=X[:, m, :], in0=ps, scalar=g2(j)(m),
                             in1=X[:, m, :], op0=ALU.mult, op1=ALU.add)
            if whole:
                toks.append(x_tok[m])
            return x_tok[m]
        return evac

    def ffn2(j, want):
        sqs, xt = [], []
        ev = x_add(j, xt)
        if want:
            chain("w", watch(lambda m: X[:, m, :], xt, sqs, 4))
        run(ffn(lambda half, m, ps, t: ev(m, ps, t, whole=half == 1)))
        drain()
        return sqs

    mt = mod_cols(0)
    chain("s", post(Y1, "post_ffn_g", a2(0), s2(0, 0), mt, sqs))
    drain()

    def mixer2(l):
        hdone = []
        an.clear()
        rp.clear()
        w_done = Q.last("pe", "act", "dve")
        lam = P2["lru_lambda_2", l]
        ring.remove(3)
        lamt = []

        def lam_consts():
            t = Q.act(op_activation, (pc_tok, w_done,), LAM[:, 0, :], PC[:, lam:lam + 4], ACT.Abs)
            t = Q.act(op_activation, (t,), LAM[:, 0, :], LAM[:, 0, :], ACT.Exp, scale=-1.0)
            t = Q.act(op_activation, (t, eps_tok,), LAM[:, 0, :], LAM[:, 0, :], ACT.Ln, bias=EPS[:, 2:3])
            u = Q.dve(op_tensor_scalar, (w_done,), LAM[:, 1, :], PC[:, lam:lam + 4], -1.0, 0.0, ALU.mult, ALU.max)
            u = Q.dve(op_tensor_tensor, (t, u,), LAM[:, 2, :], LAM[:, 1, :], LAM[:, 0, :], ALU.add)
            u = Q.dve(op_tensor_scalar, (u,), LAM[:, 3, :], LAM[:, 2, :], 8.0, None, ALU.mult)
            lamt.append(Q.dve(op_tensor_scalar, (u,), LAM[:, 1, :], LAM[:, 3, :], -1.0, None, ALU.mult))

        bz = Q.pool(op_memset, (w_done,), BD[:, :, :, :], 0.0)
        for g, nm in ((0, "w_rgate_2"), (1, "w_igate_2")):
            v = I[nm][l].rearrange("(m u) i j -> u i m j", u=2)
            for u2 in range(2):
                bd_in = Q.dma("bd", op_dma_start, (bz,), BD[64 * u2:64 * u2 + 64, g, :, 64 * u2:64 * u2 + 64], v[u2], engine="act")
        bf_in = Q.dma("bf", op_dma_start, (w_done,), BF[0:4, 0:1], I["b_fgate_2"][l:l + 1, :].rearrange("o h -> h o"), engine="act")
        fx = {}

        def fgate_logits():
            i, vh, vl, wt = next_slab()
            b = take(True)
            for k in range(KT):
                t = mm3_w(PB[b][0:4, :], vh[:, k, :], vl[:, k, :], HH[:, k, :], HL[:, k, :], k == 0, k == KT - 1,
                          wt, h_tok[k], free[b] if k == 0 else None, mark=(k == KT - 1))
                if k % 2:
                    yield
            done_slab(i, t)
            g, e, lf, F_ = (FF4[0:4, n, :] for n in range(4))
            t = Q.act(op_activation, (t, bf_in, w_done), g, PB[b][0:4, :], ACT.Identity, bias=BF[0:4, 0:1])
            let_go(b, t)
            u = Q.act(op_activation, (t,), e, g, ACT.Abs)
            u = Q.act(op_activation, (u,), e, e, ACT.Exp, scale=-1.0)
            u = Q.act(op_activation, (u,), e, e, ACT.Ln, bias=EPS[0:4, 2:3])
            u = Q.dve(op_scalar_tensor_tensor, (u, t), out=lf, in0=g, scalar=0.0, in1=e, op0=ALU.min,
                      op1=ALU.subtract)
            fx["F"] = Q.dve(op_tensor_tensor_scan, (u,), F_, lf, lf, 0.0, ALU.add, ALU.min)

        def fgates():
            yield [lambda: "F" in fx]
            yield fx["F"]
            F_ = FF4[0:4, 3, :]
            for j in range(TT):
                t = Q.pe(op_transpose, (fx["F"], free[4] if j == 0 else None), PB[4][:, 4 * j:4 * j + 4],
                         F_[:, j * 128:(j + 1) * 128], CB[0:4, C_ID:C_ID + 4], mark=(j == TT - 1))
            fx["q"] = free[4] = Q.act(op_activation, (t,), FG[:, 5, :], PB[4][:, 0:16], ACT.Copy)
            for h in range(4):
                bk = 4 + (h + 1) % 2
                t = mm(PB[bk][:, :], CB[0:4, C_ID + h:C_ID + h + 1].to_broadcast([4, 128]), F_, True, True,
                       fx["F"], free[bk], mark=True)
                fx["k", h] = free[bk] = Q.act(op_activation, (t, w_done,), FB[:, h, :], PB[bk][:, :], ACT.Copy,
                                              scale=-1.0)
                yield None
            fx["gates"] = t

        chain("s", fgates())

        def fm_out(dst, key, scale=1.0, more=()):
            def evac(m, ps, t):
                an[key, m] = Q.act(op_activation, (t, w_done, list(more)), dst[:, m, :], ps, ACT.Copy, scale=scale)
                return an[key, m]
            return evac

        def tm_out1(dst, key, *more):
            def evac(b2, ps, t):
                rp[key, b2] = Q.act(op_activation, (t, w_done, list(more)), dst[:, 2 * b2:2 * b2 + 2, :], ps, ACT.Copy)
                return rp[key, b2]
            return evac

        def fx_norm():
            gq = P2["g_qk", l]
            tiles = [(FXQ, "fq", 0, gq), (FXK, "fk", 0, gq + 1), (FXQ, "fq", 1, gq), (FXK, "fk", 1, gq + 1)]
            for n, (src, key, m, _) in enumerate(tiles):
                yield lambda key=key, m=m: (key, m) in an
                i, t = square(src[:, m, :], an[key, m])
                yield t
                u = stat(SQ[:, i, :], 6, CB[:, C_SEL:C_SEL + 2], 2, n == 0, t, col=8 * n, last=n == 3)
                sq_free[i] = u
            yield lambda: ("r", 3) in lx
            sd = FG[:, 0:2, :].rearrange("p a b -> p (a b)")
            rc = FG[:, 2:4, :].rearrange("p a b -> p (a b)")
            a_ = free[6] = Q.act(op_activation, (u, eps_tok, w_done), sd, PB[6][:, 0:32], ACT.Sqrt,
                                 bias=EPS[:, 0:1], scale=1.0 / 64)
            r = Q.dve(op_reciprocal, (a_,), rc, sd)
            yield r
            for n, (src, key, m, g) in enumerate(tiles):
                bk = (6, 5)[n % 2]
                for j in range(TT):
                    for u2 in range(2):
                        c = 8 * n + 2 * j + u2
                        t = mm(PB[bk][u2 * 64:(u2 + 1) * 64, j * 128:(j + 1) * 128],
                               FG[:, 2 + c // 16, c % 16:c % 16 + 1].to_broadcast([128, 64]), ident, True, True, r,
                               free[bk] if j == 0 else None, mark=(j == TT - 1 and u2 == 1))
                an[key, m] = free[bk] = Q.dve(op_scalar_tensor_tensor, (t, pc_tok, u), out=src[:, m, :],
                                              in0=src[:, m, :], scalar=col(g), in1=PB[bk][:, :], op0=ALU.mult,
                                              op1=ALU.mult)
                an["n", key, m] = True
                yield None

        def fox_score(h, i, sb, sst, sm, f1):
            n = 128 * (i + 1)
            po, m = 64 * (h % 2), h // 2
            mm(PB[sb][:, 0:n], FXQ[po:po + 64, m, i * 128:(i + 1) * 128], FXK[po:po + 64, m, 0:n], True, False,
               an["fq", m], an["fk", m], free[sb])
            t = mm(PB[sb][:, n - 128:n], ident, CB[:, C_CADD:C_CADD + 128], False, True, mark=True)
            a = Q.dve(op_tensor_tensor_reduce, (t, fx["k", h], fx["gates"], f1), out=sst[:, 0:n], in0=PB[sb][:, 0:n],
                      in1=FB[:, h, 0:n], scale=0.125, scalar=-3e38, op0=ALU.add, op1=ALU.max, accum_out=sm[:, 0:1])
            free[sb] = a
            fq = FG[:, 5, 4 * i + h:4 * i + h + 1]
            g = Q.dve(op_tensor_tensor, (a, fx["q"]), sm[:, 3:4], sm[:, 0:1], fq, ALU.add)
            g = Q.dve(op_tensor_tensor, (g,), sm[:, 1:2], fq, sm[:, 3:4], ALU.subtract)
            x = Q.act(op_activation, (g,), sst[:, 0:n], sst[:, 0:n], ACT.Exp, bias=sm[:, 1:2],
                                             accum_out=sm[:, 2:3])
            return norm_rows(sst, sm, n, x)

        cw, cbias = P2["conv_w", l], P2["conv_b_2", l]
        lx = {}

        def lx_out(m, ps, t):
            lx[m] = Q.act(op_activation, (t, w_done,), LA[:, m, :], ps, ACT.Copy)
            return lx[m]

        def conv(m):
            t = Q.act(op_activation, (lx[m], w_done, pc_tok), LB[:, m, :], LA[:, m, :], ACT.Identity,
                      bias=col(cbias + m), scale=col(cw + 12 + m))
            for s_ in range(1, 4):
                t = Q.dve(op_scalar_tensor_tensor, (t,), out=LB[:, m, s_:S], in0=LA[:, m, 0:S - s_],
                          scalar=col(cw + (3 - s_) * 4 + m), in1=LB[:, m, s_:S], op0=ALU.mult, op1=ALU.add)
            lx["u", m] = t

        def lru():
            for m in range(4):
                yield lambda m=m: m in lx
                conv(m)
                yield None
            for g, dst, bias in ((0, LC, "b_rgate_2"), (1, LA, "b_igate_2")):
                yield lx["u", 3]
                for m in range(4):
                    bk = take()
                    t = mm(PB[bk][:, :], BD[:, g, m, :], LB[:, m, :], True, True, bd_in, bz, lx["u", m],
                           free[bk], mark=True)
                    lx[g, m] = free[bk] = Q.act(op_activation, (t, w_done), dst[:, m, :], PB[bk][:, :], ACT.Sigmoid,
                                                bias=col(P2[bias, l] + m))
            gates.append(Q.last("pe"))
            for m in range(4):
                lx["iu", m] = Q.dve(op_tensor_tensor, (lx[1, m], gates[0]), LB[:, m, :], LB[:, m, :], LA[:, m, :],
                                    ALU.mult)
            for m in range(4):
                lx["a", m] = Q.act(op_activation, (lx[0, m], w_done, lamt), LD[:, m, :], LC[:, m, :], ACT.Exp,
                                   scale=LAM[:, 1, m:m + 1])
                lx["t", m] = Q.act(op_activation, (lx["a", m], lamt), LC[:, m, :], LC[:, m, :], ACT.Tanh,
                                   scale=LAM[:, 3, m:m + 1])
                a_ = Q.dve(op_tensor_tensor, (lx["a", m], lx["iu", m]), LA[:, m, :], LD[:, m, :], LD[:, m, :],
                           ALU.mult)
                lx["m", m] = Q.dve(op_scalar_tensor_tensor, (a_, lx["t", m]), out=LA[:, m, :], in0=LA[:, m, :],
                                   scalar=1.0, in1=LC[:, m, :], op0=ALU.add, op1=ALU.mult)
                if m % 2:
                    yield None
            for m in range(4):
                lx["r", m] = Q.act(op_activation, (lx["m", m],), LA[:, m, :], LA[:, m, :], ACT.Sqrt)
            yield None
            for m in range(4):
                t = Q.dve(op_tensor_tensor, (lx["r", m],), LB[:, m, :], LB[:, m, :], LA[:, m, :], ALU.mult)
                lx["h", m] = Q.dve(op_tensor_tensor_scan, (t, lx["t", m]), LC[:, m, :], LD[:, m, :], LB[:, m, :],
                                   0.0, ALU.mult, ALU.add)
                if m == 3:
                    lru_done.append(lx["h", 3])
                yield None

        def sb_items():
            offs = {3: 1152, 2: 896, 1: 512, 0: 0}
            st_free, w_free, sp_free = [None, None], [None, None], [None]
            spt = {}

            def item(it, h, j):
                po, m = 64 * (h % 2), h // 2
                n = S - 128 * j
                bk = (3, 5)[it % 2]

                def off(j_):
                    return 1280 if j_ == 3 and h % 2 else offs[j_]

                o = off(j)
                t = mm(PB[bk][:, 0:n], SBK[po:po + 64, m, j * 128:(j + 1) * 128], SBQ[po:po + 64, m, j * 128:S],
                       True, True, an["sq", m], an["sk", m], free[bk], mark=True)
                st = ST[:, it % 2, 0:n]
                u = Q.act(op_activation, (t, st_free[it % 2], lru_done), st, PB[bk][:, 0:n], ACT.Abs)
                u = Q.act(op_activation, (u,), st, st, ACT.Exp, scale=-1.0)
                u = Q.act(op_activation, (u,), st, st, ACT.Ln, bias=EPS[:, 2:3])
                v = Q.dve(op_scalar_tensor_tensor, (u, sp_free[0], lru_done), out=SP[:, o:o + n],
                          in0=PB[bk][:, 0:n], scalar=0.0, in1=st, op0=ALU.max, op1=ALU.add)
                st_free[it % 2] = v
                spt[h, j] = v = Q.dve(op_tensor_tensor, (v,), SP[:, o:o + 128], SP[:, o:o + 128],
                                      CB[:, C_SMUL:C_SMUL + 128], ALU.mult)
                yield v
                mm(PB[bk][:, 0:128], ident, CB[:, C_SADD:C_SADD + 128], False, False, v, skip=True)
                t = mm(PB[bk][:, 0:n], CB[:, C_NT:C_NT + 128], SP[:, o:o + n], False, j == 3, v,
                       mark=(j == 3), skip=True)
                for j2 in range(j + 1, TT):
                    n2 = S - 128 * j2
                    o2 = off(j2)
                    t = mm(PB[bk][:, n - n2:n], CB[:, C_NONE:C_NONE + 128], SP[:, o2:o2 + n2], False, j2 == 3,
                           spt[h, j2], mark=(j2 == 3), skip=True)
                w = free[bk] = Q.act(op_activation, (t, w_free[it % 2], lru_done), SW[:, it % 2, 0:n],
                                     PB[bk][:, 0:n], ACT.Exp)
                if j == 0:
                    sp_free[0] = t
                yield w
                p = mm(PB[6][po:po + 64, j * 128:S], SBV[:, j, h * 64:(h + 1) * 64], SW[:, it % 2, 0:n], j == 3,
                       j == 0, w, rp["sv", 0], rp["sv", 1], free[6] if h % 2 == 0 and j == 3 else None, mark=True,
                       skip=True)
                w_free[it % 2] = p
                if h % 2 and j == 0:
                    an["so", m] = free[6] = Q.act(op_activation, (p,), SBQ[:, m, :], PB[6][:, :], ACT.Copy)

            return [item(4 * h + 3 - j, h, j) for h in range(4) for j in (3, 2, 1, 0)]

        gates, lru_done = [], []

        def lg_out(m, ps, t):
            lx["g", m] = Q.act(op_activation, (t, fox_done), LG[:, m, :], ps, ACT.Copy)
            return lx["g", m]

        def tail():
            gm = P2["g_mix", l]
            parts = [(LC, 4, 0, 0, "ly"), (FXQ, 2, 6, 6, "fo"), (SBQ, 2, 4, 4, "so")]
            for m in range(4):
                g = Q.act(op_activation, (lx["g", m],), LG[:, m, :], LG[:, m, :], ACT.Gelu_apprx_tanh)
                an["ly", m] = Q.dve(op_tensor_tensor, (lx["h", m], g), LC[:, m, :], LC[:, m, :], LG[:, m, :],
                                    ALU.mult)
            for n, (src, width, _, _, key) in enumerate(parts):
                for m in range(width):
                    i_, t = square(src[:, m, :], an[key, m])
                    u = stat(SQ[:, i_, :], 6, one, 1, n == 0 and m == 0, t, col=4 * n, last=n == 2 and m == 1)
                    sq_free[i_] = u
            s = small[0] % NSM
            small[0] += 1
            for c0, c1, width in ((0, 4, 4), (4, 12, 2)):
                a_ = Q.act(op_activation, (u, eps_tok, Q.last("dve")), SD[:, s, c0:c1], PB[6][:, c0:c1], ACT.Sqrt,
                           bias=EPS[:, 0:1], scale=1.0 / (128 * width))
            free[6] = a_
            r = Q.dve(op_reciprocal, (a_, Q.last("pe")), RC[:, s, 0:12], SD[:, s, 0:12])
            spr = []
            for n in range(3):
                bk = (7, 5, 4)[n]
                for j in range(TT):
                    t = mm(PB[bk][:, j * 128:(j + 1) * 128],
                           RC[:, s, 4 * n + j:4 * n + j + 1].to_broadcast([128, 128]), ident, True, True, r,
                           free[bk] if j == 0 else None, mark=(j == TT - 1))
                spr.append((bk, t))
            c = 0
            for (src, width, g0, k0, key), (bk, rt) in zip(parts, spr):
                for m in range(width):
                    i_ = c % 2
                    c += 1
                    t = Q.dve(op_scalar_tensor_tensor, (rt, an[key, m], pc_tok, Q.last("act") if c == 1 else None),
                              out=TM[:, i_, :],
                              in0=src[:, m, :], scalar=col(gm + g0 + m), in1=PB[bk][:, :], op0=ALU.mult, op1=ALU.mult)
                    hi = Q.act(op_activation, (t, hdone,), HH[:, k0 + m, :], TM[:, i_, :], ACT.Copy)
                    lo = Q.dve(op_tensor_tensor, (hi, t, hdone,), HL[:, k0 + m, :], TM[:, i_, :],
                               f(HH[:, k0 + m, :]), ALU.subtract)
                    h_tok[k0 + m] = [hi, lo]
                free[bk] = t
            yield None

        chain("l", lru())
        run(proj_fm(2, HH, HL, h_tok, lx_out, True))
        run(proj_fm(2, HH, HL, h_tok, lx_out, False, m0=2))
        Q.table("natural_log_exp_and_others")
        lam_consts()
        run(fgate_logits())
        chain("s", fx_norm())
        run(proj_fm(2, HH, HL, h_tok, fm_out(FXQ, "fq"), False))
        run(proj_fm(2, HH, HL, h_tok, fm_out(FXK, "fk"), False))
        run(proj_tm(TT, HH, HL, h_tok, tm_out1(FXV, "fv")))
        while not lru_done:
            chains["l"][0].step()
        while ("n", "fk", 1) not in an:
            chains["s"][0].step()
            best()
        Q.table("natural_log_exp_and_others")
        fox_done = []

        def fox_end():
            fox_done.append(Q.last("pe", "act", "dve"))
            yield None

        chain("s", Window(soft_attention(
            [(h, i) for h in range(4) for i in (3, 2, 1, 0)], fox_score, lambda i: 128 * (i + 1),
            [FS[:, 0, :], FS[:, 1, :], FS2], [FP[:, 0, :], FP[:, 1, :]],
            head_pair_finish(FXV, lambda h: [("fv", 0), ("fv", 1)], FXQ, "fo"), None), 3))
        chain("s", fox_end())
        run(proj_fm(2, HH, HL, h_tok, fm_out(SBQ, "sq", 0.125, lru_done), False))
        run(proj_fm(2, HH, HL, h_tok, fm_out(SBK, "sk", 1.0, lru_done), False))
        run(proj_tm(TT, HH, HL, h_tok, tm_out1(SBV, "sv", gates)))
        chain("b", Window(sb_items(), 2))
        while not fox_done:
            chains["s"][0].step()
            best()
        for c in range(2):
            run(proj_fm(2, HH, HL, h_tok, lg_out, False, m0=2 * c))
        hdone.extend(Q.last("pe"))
        drain()
        chain("s", tail())
        drain()
        ring.append(3)
        sqs, xt = [], []
        chain("w", watch(lambda m: X[:, m, :], xt, sqs))
        for c in range(4):
            run(proj_fm(2, HH, HL, h_tok, x_add(1, xt), c == 0, m0=2 * c, ks=(0, 1, 2, 3, 6, 7, 4, 5)))
        drain()
        return sqs

    for l in range(2):
        if l:
            mt = mod_cols(1)
            chain("s", rms_h(sqs[-1], a2(0), s2(1, 0), mt))
            drain()
        sqs = ffn2(0, True)
        chain("s", rms_h(sqs[-1], a2(1), s2(l, 1), mt))
        drain()
        sqs = mixer2(l)
        chain("s", rms_h(sqs[-1], a2(2), s2(l, 2), mt))
        drain()
        sqs = ffn2(2, l == 0)

    for j in range(TT):
        toks = []
        for hf in range(2):
            b = take()
            for q in range(4):
                t = Q.pe(op_transpose, (x_tok[4 * hf + q], free[b] if q == 0 else None), PB[b][:, q * 128:(q + 1) * 128],
                         X[:, 4 * hf + q, j * 128:(j + 1) * 128], ident, mark=q == 3)
            o = OT[:, j, hf * 512:(hf + 1) * 512]
            if hf:
                t = Q.act(op_activation, (t,), o, PB[b][:, :], ACT.Copy)
            else:
                t = Q.dve(op_tensor_copy, (t,), o, PB[b][:, :])
            free[b] = t
            toks.append(t)
        out_tok = Q.dma("out", op_dma_start, toks, out[0, j * 128:(j + 1) * 128, :], OT[:, j, :])

    with ExitStack() as ctx:
        sems = {name: ctx.enter_context(nc.semaphore("s_" + name)) for name in Q.count}
        block = ctx.enter_context(nc.Block())

        @block.sync
        def _(e):
            Q.run("sp", e, sems)
            e.wait_ge(sems["out"], out_tok[1])

        @block.gpsimd
        def _(e):
            Q.run("pool", e, sems)

        @block.scalar
        def _(e):
            Q.run("act", e, sems)

        @block.vector
        def _(e):
            Q.run("dve", e, sems)

        @block.tensor
        def _(e):
            Q.run("pe", e, sems)


_NAMES = ["x", "mem", "pre_mix_g", "post_mix_g", "w_in", "attn_gn_g", "ret_gn_g", "w_out", "pre_mem_g",
          "post_mem_g", "mem_norm_g", "w_q_mem", "w_kv_mem", "w_o_mem", "pre_ffn_g", "post_ffn_g", "w_gate_up",
          "w_down", "c_2", "w_ada_2", "b_ada_2", "g_norm_2", "w_ffn_up_2", "w_ffn_down_2", "w_in_2", "b_fgate_2",
          "conv_w_2", "conv_b_2", "w_rgate_2", "b_rgate_2", "w_igate_2", "b_igate_2", "lru_lambda_2", "g_qk_2",
          "g_mix_out_2", "w_out_2"]


def kernel(**inputs):
    import numpy as _np
    import concourse.bacc as _bacc
    from concourse import mybir as _mybir
    from concourse.bass_utils import run_bass_kernel_spmd as _run

    nc = _bacc.Bacc("TRN2", target_bir_lowering=False, num_devices=1)
    arrays, aps = {}, {}
    cb, ct = const_tables()
    for name, a in [(n, _np.ascontiguousarray(inputs[n])) for n in _NAMES] + [("c_b", cb), ("c_t", ct)]:
        arrays["in_" + name] = a
        aps[name] = nc.dram_tensor("in_" + name, a.shape, _mybir.dt.from_np(a.dtype), kind="ExternalInput").ap()
    out = nc.dram_tensor("out_0_dram", (1, S, D), _mybir.dt.float32, kind="ExternalOutput").ap()
    build(nc, aps, out)
    r = _run(nc, [arrays], core_ids=[0])
    return r.results[0]["out_0_dram"]
```

```python
from collections import deque
from contextlib import ExitStack

import numpy as np
import concourse.bass as bass
from concourse import mybir

F32 = mybir.dt.float32
F32R = mybir.dt.float32r
ALU = mybir.AluOpType
ACT = mybir.ActivationFunctionType
AX = mybir.AxisListType

D = 1024
S = 512
KT = 8
TT = 4
NMEM = 256
FF = 2816
HALF = 11
RMS_EPS = 1e-6
GN_EPS = 1e-5
NEG = -1e30

C_ID, C_SEL, C_ONE, C_TRI, C_NT, C_NONE, C_SADD, C_CADD, C_SMUL, C_PA, C_PR = (
    0, 128, 130, 132, 644, 772, 900, 1028, 1156, 1284, 1412)
CB_W = 1540
T_MASK, T_ROPE, T_DEC = 0, 512, 512 + 4 * 512
CT_W = T_DEC + 4 * 512


def const_tables():
    p = np.arange(128)[:, None]
    c = np.arange(128)[None, :]
    cb = np.zeros((128, CB_W), np.float32)
    cb[:, C_ID:C_ID + 128] = (p == c)
    cb[:, C_TRI:C_TRI + 512] = (p <= np.arange(512)[None, :])
    cb[:, C_NT:C_NT + 128] = -1.0 * (p >= c)
    cb[:, C_NONE:C_NONE + 128] = -1.0
    cb[:, C_SADD:C_SADD + 128] = np.where(p >= c, NEG, 0.0)
    cb[:, C_CADD:C_CADD + 128] = np.where(c > p, NEG, 0.0)
    cb[:, C_SMUL:C_SMUL + 128] = (p < c)
    i = c % 64
    partner = np.where(i < 8, c + 8, np.where(i < 16, c - 8, -1))
    cb[:, C_PA:C_PA + 128] = (p == partner)
    cb[:, C_PR:C_PR + 128] = (p == (c + 64) % 128)
    cb[:, C_SEL] = (np.arange(128) < 64)
    cb[:, C_SEL + 1] = (np.arange(128) >= 64)
    cb[:, C_ONE:C_ONE + 2] = 1.0

    ct = np.zeros((128, CT_W), np.float32)
    n = np.arange(512)
    delta = 128 * (3 - n[None, :] // 128) + p - n[None, :] % 128
    count = ((delta >= 0) & (delta <= 128)).astype(int) + ((delta >= 0) & (delta % 4 == 0)) \
        + ((delta >= 0) & (delta % 16 == 0))
    ct[:, T_MASK:T_MASK + 512] = np.where(count > 0, 8.0 * np.log(np.maximum(count, 1)), NEG)
    pos = np.arange(512, dtype=np.float32)
    for at, dim, theta, width in ((0, 16, 500000.0, 64), (2, 128, 10000.0, 128)):
        inv = np.float32(theta) ** (-(np.arange(0, dim, 2, dtype=np.float32) / np.float32(dim)))
        ang = (pos[None, :] * inv.astype(np.float32)[:, None]).astype(np.float32)
        cos, sin = np.cos(ang), np.sin(ang)
        h = dim // 2
        cr = np.ones((width, 512), np.float32)
        sr = np.zeros((width, 512), np.float32)
        cr[:h], cr[h:dim] = cos, cos
        sr[:h], sr[h:dim] = -sin, sin
        ct[:, T_ROPE + at * 512:T_ROPE + (at + 1) * 512] = np.tile(cr, (128 // width, 1))
        ct[:, T_ROPE + (at + 1) * 512:T_ROPE + (at + 2) * 512] = np.tile(sr, (128 // width, 1))
    for h in range(4):
        log_g = np.log(1.0 - 2.0 ** (-5.0 - h))
        rel = n[None, :] - p
        ct[:, T_DEC + h * 512:T_DEC + (h + 1) * 512] = np.where(
            rel >= 0, np.exp(log_g * np.maximum(rel, 0)) * 128.0 ** -0.5, 0.0)
    return cb, ct


def op_matmul(e, *a, **k):
    return e.matmul(*a, **k)


def op_transpose(e, *a, **k):
    return e.transpose(*a, **k)


def op_activation(e, *a, **k):
    return e.activation(*a, **k)


def op_tensor_tensor(e, *a, **k):
    return e.tensor_tensor(*a, **k)


def op_tensor_scalar(e, *a, **k):
    return e.tensor_scalar(*a, **k)


def op_scalar_tensor_tensor(e, *a, **k):
    return e.scalar_tensor_tensor(*a, **k)


def op_tensor_tensor_scan(e, *a, **k):
    return e.tensor_tensor_scan(*a, **k)


def op_tensor_tensor_reduce(e, *a, **k):
    return e.tensor_tensor_reduce(*a, **k)


def op_tensor_reduce(e, *a, **k):
    return e.tensor_reduce(*a, **k)


def op_tensor_copy(e, *a, **k):
    return e.tensor_copy(*a, **k)


def op_reciprocal(e, *a, **k):
    return e.reciprocal(*a, **k)


def op_memset(e, *a, **k):
    return e.memset(*a, **k)


def op_preload(e, name):
    return e.preload_act_table_set(name)


def op_dma_start(e, *a, **k):
    return e.dma_start(*a, **k)


class Queues:

    def __init__(self):
        self.todo = {e: [] for e in ("sp", "pe", "act", "dve", "pool")}
        self.count = {}
        self.clock = dict.fromkeys(("sp", "pe", "act", "dve", "pool", "dma"), 0.0)
        self.done = {}
        self.set = frozenset()

    def switch(self, func):
        for members in ((ACT.Exp, ACT.Tanh), (ACT.Sigmoid, ACT.Tanh), (ACT.Sqrt,), (ACT.Ln,), (ACT.Silu,),
                        (ACT.Gelu_apprx_tanh,)):
            if func in members and func not in self.set:
                self.set = frozenset(members)
                return 1.3
        return 0.0

    def price(self, engine, op, args, kw):
        if op is op_dma_start:
            return int(np.prod(args[0].shape)) * 4 / 350e3
        if op is op_preload:
            self.set = frozenset((ACT.Exp, ACT.Ln)) if "exp" in args[0] else frozenset((ACT.Sqrt,))
            return 1.3
        out = kw["out"] if "out" in kw else args[0]
        n = int(np.prod(out.shape[1:]))
        if op is op_matmul:
            return max(n, 64) * (4 if args[1].dtype == F32 else 1) / 2400
        if op is op_transpose:
            return 0.06
        if engine == "act":
            return 0.19 + n / 1200 + self.switch(args[2] if len(args) > 2 else None)
        if engine == "pool":
            return 0.1 + n / 450
        if op is op_reciprocal:
            n *= 6
        elif op is op_tensor_tensor_scan:
            n *= 2
        return 0.07 + n / 960

    def put(self, engine, op, after, sem, by, args, kw):
        flat = []
        stack = list(after)
        while stack:
            t = stack.pop()
            if isinstance(t, list):
                stack += t
            elif t is not None:
                flat.append(t)
        if sem is not None:
            self.count[sem] = self.count.get(sem, 0) + by
        self.todo[engine].append((op, args, kw, flat, sem, by))
        unit = "dma" if op is op_dma_start else engine
        start = max([self.clock[unit]] + [self.done.get(t, 0.0) + 0.1 for t in flat])
        self.clock[unit] = start + self.price(engine, op, args, kw)
        if sem is not None:
            self.done[(sem, self.count[sem])] = self.clock[unit] + (2.0 if unit == "dma" else 0.0)
        return (sem, self.count[sem]) if sem is not None else None

    def pe(self, op, after, *args, mark=False, **kw):
        return self.put("pe", op, after, "pe" if mark else None, 1, args, kw)

    def act(self, op, after, *args, **kw):
        return self.put("act", op, after, "act", 1, args, kw)

    def table(self, name):
        self.put("act", op_preload, (), None, 0, (name,), {})

    def dve(self, op, after, *args, **kw):
        return self.put("dve", op, after, "dve", 1, args, kw)

    def pool(self, op, after, *args, **kw):
        return self.put("pool", op, after, "pool", 1, args, kw)

    def dma(self, sem, op, after, *args, engine="sp", **kw):
        return self.put(engine, op, after, sem, 16, args, kw)

    def when(self, need):
        if need is None:
            return 0.0
        if isinstance(need, list):
            return max([0.0] + [self.when(x) for x in need])
        return self.done.get(need, 0.0) + 0.1

    def last(self, *engines):
        return [(e, self.count[e]) for e in engines if self.count.get(e)]

    def run(self, name, engine, sems):
        seen = {}
        for op, args, kw, after, sem, by in self.todo[name]:
            need = {}
            for s, v in after:
                need[s] = max(need.get(s, 0), v)
            for s in sorted(need):
                if seen.get(s, 0) < need[s]:
                    engine.wait_ge(sems[s], need[s])
                    seen[s] = need[s]
            ins = op(engine, *args, **kw)
            if sem is not None:
                ins.then_inc(sems[sem], by)


def build(nc, I, out):
    Q = Queues()
    base = (nc.sbuf_base + 127) // 128 * 128
    TB = 2048

    def at(name, off_bytes, shape, dt=F32):
        return nc.alloc_sbuf_tensor_at(name, shape, dt, offset=base + off_bytes)

    X = at("X", 0, [128, KT, S])
    HH = at("HH", 8 * TB, [128, KT, S], F32R)
    HL = at("HL", 16 * TB, [128, KT, S], F32R)
    NS, NW, SLAB = 3, 3, 2048
    WS = at("WS", 24 * TB, [128, NS, SLAB])
    WH = at("WH", 36 * TB, [128, NW, SLAB], F32R)
    WL = at("WL", 48 * TB, [128, NW, SLAB], F32R)
    coff = [60 * TB]

    def const(name, shape, dt=F32):
        t = at(name, coff[0], shape, dt)
        coff[0] += (4 * int(np.prod(shape[1:])) + 31) // 32 * 32
        assert coff[0] <= 66 * TB
        return t

    CB = const("CB", [128, CB_W])
    ACC = const("ACC", [128, 512])
    PC = const("PC", [128, 340])
    MOD = const("MOD", [128, 2, 72])
    MA = const("MA", [128, 24])
    MG = const("MG", [128, 24])
    NSM = 6
    SD = const("SD", [128, NSM, 16])
    RC = const("RC", [128, NSM, 16])
    CC = const("CC", [128, 8])
    CS = const("CS", [128, 8])
    EPS = const("EPS", [128, 4])
    SM = const("SM", [128, 4, 4])
    LAM = const("LAM", [128, 4, 4])
    FG = const("FG", [128, 6, 16])
    BF = const("BF", [128, 4])

    R0 = 66

    def region(name, t, shape, dt=F32):
        n = 4 * int(np.prod(shape[1:]))
        assert (R0 + t) * TB + n <= 103 * TB
        return at(name, int((R0 + t) * TB), shape, dt)

    SQ = region("SQ", 33, [128, 2, S])
    TM = region("TM", 35, [128, 2, S])
    SQ2 = region("SQ2", 31, [128, 2, S])
    SQ3 = region("SQ3", 24, [128, 2, S])
    XTM = region("XTM", 0, [128, TT, D])
    PR = region("PR", 20, [128, 5, 128])
    AQ = region("AQ", 0, [128, 4, S])
    AK = region("AK", 4, [128, 4, S])
    RG = region("RG", 4, [128, 4, S])
    AV = region("AV", 8, [128, TT, 512])
    RQ = region("RQ", 12, [128, 4, S])
    RK = region("RK", 16, [128, 4, S])
    RV = region("RV", 20, [128, TT, 512])
    MSK = region("MSK", 24, [128, 512])
    ROPE = region("ROPE", 25, [128, 4, 512])
    SS = region("SS", 29, [128, 2, S])
    PT = region("PT", 31, [128, 2, S])
    MH = region("MH", 0, [128, KT, NMEM], F32R)
    ML = region("ML", 4, [128, KT, NMEM], F32R)
    KM = region("KM", 8, [128, KT, NMEM])
    VM = region("VM", 12, [128, 2, D])
    Y = region("Y", 16, [128, KT, S])
    XQ = region("XQ", 16, [128, KT, S])
    XS = region("XS", 24, [128, 4, NMEM])
    XP = region("XP", 26, [128, 4, NMEM])
    MTM = region("MTM", 28, [128, 2, D])
    GH = region("GH", 0, [128, HALF, S], F32R)
    GL = region("GL", 11, [128, HALF, S], F32R)
    Y1 = region("Y1", 22, [128, KT, S])
    SG = region("SG", 30, [128, 2, S])
    FXQ = region("FXQ", 0, [128, 2, S])
    FXK = region("FXK", 2, [128, 2, S])
    FXV = region("FXV", 4, [128, TT, 256])
    SBQ = region("SBQ", 6, [128, 2, S])
    SBK = region("SBK", 8, [128, 2, S])
    SBV = region("SBV", 10, [128, TT, 256])
    LA = region("LA", 12, [128, 4, S])
    LB = region("LB", 16, [128, 4, S])
    LC = region("LC", 20, [128, 4, S])
    FB = region("FB", 24, [128, 4, S])
    LD = region("LD", 6, [128, 4, S])
    BD = region("BD", 10, [128, 2, 4, 128])
    FS = region("FS", 28, [128, 2, S])
    FS2 = region("FS2", 32, [128, S])[:, :]
    FP = region("FP", 30, [128, 2, S])
    SP = region("SP", 12, [128, 1408])
    ST = region("ST", 15, [128, 2, S])
    SW = region("SW", 17, [128, 2, S])
    ST3 = region("ST3", 28, [128, S])[:, :]
    SW3 = region("SW3", 29, [128, S])[:, :]
    LG = region("LG", 24, [128, 4, S])
    FF4 = region("FF4", 28, [128, 4, S])
    OT = region("OT", 0, [128, TT, D])

    PB = [nc.alloc_psum_tensor(f"PB{i}", [128, 512], F32) for i in range(8)]
    free = {b: None for b in range(8)}
    ring = deque([0, 1, 2, 3])

    held = set()

    def take(hold=False):
        b = next(x for x in ring if x not in held)
        ring.remove(b)
        ring.append(b)
        if hold:
            held.add(b)
        return b

    def let_go(b, tok):
        free[b] = tok
        held.discard(b)

    ident = CB[:, C_ID:C_ID + 128]

    def f(ap):
        return ap.bitcast(F32)

    def mm(out_, l, r, start, stop, *after, mark=False, skip=False):
        return Q.pe(op_matmul, (*after,), out_, l, r, start=start, stop=stop, skip_group_check=skip, mark=mark)

    BLOCKED = 1e9

    def asks(need):
        if isinstance(need, list):
            return max([0.0] + [asks(x) for x in need])
        if callable(need):
            need = need()
            return (0.0 if need else BLOCKED) if isinstance(need, bool) else asks(need)
        return Q.when(need)

    class Task:
        def __init__(self, gen):
            self.gen, self.need, self.over, self.steps = gen, None, False, 0

        def at(self):
            return asks(self.need)

        def step(self):
            try:
                self.need = next(self.gen)
                self.steps += 1
            except StopIteration:
                self.over = True

    class Window:

        def __init__(self, gens, width, gate=None):
            self.rest, self.live, self.width = deque(gens), [], width
            self.over = not self.rest
            self.gate = gate
            self.begun = 0

        def options(self):
            for i, t in enumerate(self.live):
                if i == 0 or self.live[i - 1].steps > t.steps:
                    yield t.at(), t
            if self.rest and len(self.live) < self.width and (not self.live or self.live[-1].steps > 0):
                yield (0.0 if self.gate is None or self.gate(self.begun) else BLOCKED), None

        def at(self):
            return min((x[0] for x in self.options()), default=BLOCKED)

        def step(self):
            best = min(self.options(), key=lambda x: x[0])
            t = best[1]
            if t is None:
                t = Task(self.rest.popleft())
                self.live.append(t)
                self.begun += 1
            t.step()
            if t.over:
                self.live.remove(t)
            self.over = not self.rest and not self.live

    chains = {}

    def chain(name, work):
        chains.setdefault(name, deque()).append(work if isinstance(work, Window) else Task(work))

    def best():
        for c in chains.values():
            while c and c[0].over:
                c.popleft()
        live = [(c[0].at(), n) for n, c in chains.items() if c]
        return min(live) if live else (None, None)

    def pump(most=3):
        for _ in range(most):
            at_, name = best()
            if name is None or at_ > Q.clock["pe"]:
                return
            if max(Q.clock["act"], Q.clock["dve"]) > Q.clock["pe"] + AHEAD:
                return
            chains[name][0].step()

    AHEAD = 4.0

    def drain(*names):
        while True:
            at_, name = best()
            if name is None or (names and not any(chains.get(n) for n in names)):
                return
            assert at_ < BLOCKED
            chains[name][0].step()

    def run(gen):
        for _ in gen:
            pump()

    def force(known):
        while not known():
            at_, name = best()
            assert name is not None and at_ < BLOCKED
            chains[name][0].step()

    items = []

    def w_cols(w, c0, n, kt=KT):
        v = w.rearrange("(k p) c -> p k c", p=128)
        items.append(("w", v[:, 0:kt, c0:c0 + n], (kt, n)))

    def w_rows(w, k0, kn, c0, n):
        v = w.rearrange("(k p) c -> p k c", p=128)
        items.append(("w", v[:, k0:k0 + kn, c0:c0 + n], (kn, n)))

    def w_up(w, m):
        v = w.rearrange("(k p) (t c) -> p k t c", p=128, t=2)
        items.append(("w2", v[:, :, :, m * 128:(m + 1) * 128], (KT, 2, 128)))

    def plan_ffn(up, down):
        for half in range(2):
            for m in range(HALF):
                w_up(up, half * HALF + m)
            for k0, kn in ((0, 4), (4, 4), (8, 3)):
                w_rows(down, half * HALF + k0, kn, 0, 512)
            for m in range(4, 8):
                w_rows(down, half * HALF, HALF, m * 128, 128)

    def plan():
        w_in = I["w_in"][0]
        for c in range(14):
            w_cols(w_in, c * 256, 256)
        for c in range(4):
            w_cols(I["w_out"][0], c * 256, 256)
        for c in range(8):
            w_cols(I["w_kv_mem"][0], c * 256, 256)
        for c in range(4):
            w_cols(I["w_q_mem"][0], c * 256, 256)
        for c in range(4):
            w_cols(I["w_o_mem"][0], c * 256, 256)
        plan_ffn(I["w_gate_up"][0], I["w_down"][0])
        for l in range(2):
            plan_ffn(I["w_ffn_up_2"][l, 0], I["w_ffn_down_2"][l, 0])
            w2 = I["w_in_2"][l]
            w_cols(w2, 0, 256)
            w_cols(w2, 256, 256)
            w_cols(w2, 2560, 4)
            for c0 in (1792, 2048, 2304, 1024, 1280, 1536, 512, 768):
                w_cols(w2, c0, 256)
            for c in range(4):
                w_cols(I["w_out_2"][l], c * 256, 256)
            plan_ffn(I["w_ffn_up_2"][l, 1], I["w_ffn_down_2"][l, 1])

    plan()
    weights = items
    items = []
    ada = []
    for l in range(2):
        v = I["w_ada_2"][l].rearrange("(p k) n -> p k n", k=8)
        for n in range(18):
            for kh in range(2):
                ada.append(("ada", v[:, 4 * kh:4 * kh + 4, n * 512:(n + 1) * 512], (l, n, kh)))
    n1 = 14 + 4 + 8 + 4 + 4 + 36
    order = []
    ai = 0
    for wi, w in enumerate(weights):
        order.append(w)
        due = 36 * min(1.0, (wi + 1) / (n1 - 6)) if wi < n1 - 6 else 36 + 36 * min(1.0, (wi - n1 + 7) / 76)
        while ai < min(due, 72) - 1e-9:
            order.append(ada[ai])
            ai += 1
    order += ada[ai:]

    ws_free = [None] * NS
    ws_in = [None] * NS
    wh_free = [None] * NW
    ready = {}
    pos = {"dma": 0, "use": 0, "w": 0, "slab": 0}

    def emit_dma():
        i = pos["dma"]
        if i >= len(order):
            return
        pos["dma"] += 1
        kind, src, dims = order[i]
        s = i % NS
        if kind == "ada":
            dst = WS[:, s, :].rearrange("p (k n) -> p k n", k=4)
        elif kind == "w2":
            dst = WS[:, s, 0:2048].rearrange("p (k t c) -> p k t c", k=KT, t=2)
        else:
            dst = WS[:, s, 0:dims[0] * dims[1]].rearrange("p (k c) -> p k c", k=dims[0])
        if kind == "w2":
            for t in range(2):
                ws_in[s] = Q.dma(f"ws{s}", op_dma_start, (ws_free[s],), dst[:, :, t, :], src[:, :, t, :])
        else:
            ws_in[s] = Q.dma(f"ws{s}", op_dma_start, (ws_free[s],), dst, src)

    pend = []
    acc_free = [None]
    mod_tok = [None, None]

    def flush_ada():
        while pend:
            l, n, tok = pend.pop(0)
            b = take()
            for q in range(4):
                t = mm(PB[b][:, q:q + 1], ACC[:, q * 128:(q + 1) * 128], CB[:, C_ONE:C_ONE + 1],
                       True, True, free[b], tok, cb_in, mark=(q == 3))
            acc_free[0] = t
            bias = PC[:, 196 + 72 * l + 4 * n:196 + 72 * l + 4 * n + 4]
            free[b] = Q.dve(op_tensor_tensor, (t, pc_tok,), MOD[:, l, 4 * n:4 * n + 4], PB[b][:, 0:4], bias, ALU.add)
            mod_tok[l] = free[b]

    def flushing():
        yield [x[2] for x in pend]
        flush_ada()

    def emit_use():
        i = pos["use"]
        pos["use"] += 1
        kind, src, dims = order[i]
        s = i % NS
        if kind == "ada":
            l, n, kh = dims
            if kh == 0:
                flush_ada()
            t = None
            for q in range(4):
                w = WS[:, s, q * 512:(q + 1) * 512]
                c = CS[:, 4 * kh + q:4 * kh + q + 1]
                if kh == 0 and q == 0:
                    t = Q.dve(op_tensor_scalar, (ws_in[s], acc_free[0], cs_tok,), ACC[:, :], w, c, None, ALU.mult)
                else:
                    t = Q.dve(op_scalar_tensor_tensor, (ws_in[s], Q.last("dve"),), out=ACC[:, :], in0=w, scalar=c, in1=ACC[:, :], op0=ALU.mult, op1=ALU.add)
            ws_free[s] = t
            if kh == 1:
                pend.append((l, n, t))
        else:
            j = pos["w"]
            pos["w"] += 1
            n = int(np.prod(dims))
            h = j % NW
            hi = Q.act(op_activation, (ws_in[s], wh_free[h],), WH[:, h, 0:n], WS[:, s, 0:n], ACT.Copy)
            lo = Q.dve(op_tensor_tensor, (ws_in[s], hi, wh_free[h],), WL[:, h, 0:n], WS[:, s, 0:n], f(WH[:, h, 0:n]), ALU.subtract)
            ws_free[s] = lo
            ready[j] = [hi, lo]
        emit_dma()

    def use_until(j):
        while pos["w"] <= j and pos["use"] < len(order):
            emit_use()

    def next_slab(ahead=2):
        i = pos["slab"]
        pos["slab"] += 1
        use_until(i)
        use_until(i + ahead)
        if pend and not chains.get("ada"):
            chain("ada", flushing())
        kind, _, dims = weights[i]
        h = i % NW
        n = int(np.prod(dims))
        if kind == "w2":
            vh = WH[:, h, 0:n].rearrange("p (k t c) -> p k t c", k=dims[0], t=2)
            vl = WL[:, h, 0:n].rearrange("p (k t c) -> p k t c", k=dims[0], t=2)
        else:
            vh = WH[:, h, 0:n].rearrange("p (k c) -> p k c", k=dims[0])
            vl = WL[:, h, 0:n].rearrange("p (k c) -> p k c", k=dims[0])
        return i, vh, vl, ready[i]

    def done_slab(i, tok):
        wh_free[i % NW] = tok

    def mm3_w(out_, wh, wl, xh, xl, start, stop, *after, mark=False, skip=False):
        mm(out_, wh, xh, start, False, *after, skip=skip)
        mm(out_, wh, xl, False, False, skip=skip)
        return mm(out_, wl, xh, False, stop, mark=mark, skip=skip)

    def mm3_x(out_, xh, xl, wh, wl, start, stop, *after, mark=False):
        mm(out_, xh, wh, start, False, *after)
        mm(out_, xh, wl, False, False)
        return mm(out_, xl, wh, False, stop, mark=mark)

    def proj_fm(ntile, xh, xl, xt, evac, kouter, ntok=S, m0=0, unit=2, ks=tuple(range(KT))):
        if kouter:
            force(lambda: xt[ks[1]] is not None)
        i, vh, vl, wt = next_slab()
        banks = [take(True) for _ in range(ntile)]
        seq = [(k, m) for k in ks for m in range(ntile)] if kouter else \
              [(k, m) for m in range(ntile) for k in ks]
        for c, (k, m) in enumerate(seq):
            first, last = k == ks[0], k == ks[-1]
            force(lambda: xt[k] is not None)
            t = mm3_w(PB[banks[m]][:, 0:ntok], vh[:, k, m * 128:(m + 1) * 128],
                      vl[:, k, m * 128:(m + 1) * 128], xh[:, k, 0:ntok], xl[:, k, 0:ntok], first, last,
                      wt, xt[k], free[banks[m]] if first else None, mark=last)
            if last:
                let_go(banks[m], evac(m0 + m, PB[banks[m]][:, 0:ntok], t))
                done_slab(i, t)
            if c % unit == unit - 1:
                yield

    def proj_fm3(xh, xl, xt, evac, ks=tuple(range(KT)), first=0):
        force(lambda: xt[ks[first]] is not None)
        slabs = [next_slab(), next_slab(1)]
        tiles = [(0, 0), (0, 1), (1, 0)]
        banks = [take(True) for _ in tiles]
        seq = [(k, n) for k in ks for n in range(3)] + [(k, 3) for k in ks]
        for k, n in seq:
            force(lambda: xt[k] is not None)
            if n == 3 and k == ks[0]:
                tiles.append((1, 1))
                banks.append(take(True))
            i, vh, vl, wt = slabs[tiles[n][0]]
            m = tiles[n][1]
            t = mm3_w(PB[banks[n]][:, :], vh[:, k, m * 128:(m + 1) * 128], vl[:, k, m * 128:(m + 1) * 128],
                      xh[:, k, :], xl[:, k, :], k == ks[0], k == ks[-1], wt, xt[k],
                      free[banks[n]] if k == ks[0] else None, mark=k == ks[-1])
            if k == ks[-1]:
                let_go(banks[n], evac(n, PB[banks[n]][:, :], t))
                if n % 2:
                    done_slab(i, t)
            yield

    def proj_tm(ntok, xh, xl, xt, evac):
        i, vh, vl, wt = next_slab()
        for b2 in range(ntok // 2):
            b = take(True)
            for u in range(2):
                j = 2 * b2 + u
                for k in range(KT):
                    t = mm3_x(PB[b][:, u * 256:(u + 1) * 256], xh[:, k, j * 128:(j + 1) * 128],
                              xl[:, k, j * 128:(j + 1) * 128], vh[:, k, :], vl[:, k, :],
                              k == 0, k == KT - 1, wt, xt[k], free[b] if k == 0 and u == 0 else None,
                              mark=(k == KT - 1))
                    if k % 4 == 3:
                        yield
            done_slab(i, t)
            let_go(b, evac(b2, PB[b][:, :].rearrange("p (u c) -> p u c", u=2), t))

    small = [0]
    rc_read = [None] * NSM
    hread = [None]

    def stat(tile, b, sel, ng, first, tok, col=0, ntok=TT, last=True):
        for j in range(ntok):
            t = mm(PB[b][:, col + j * ng:col + (j + 1) * ng], tile[:, j * 128:(j + 1) * 128], sel,
                   first and j == 0, last and j == ntok - 1, tok, cb_in,
                   free[b] if first and j == 0 else None, mark=(j == ntok - 1), skip=True)
        return t

    def root(b, n, scale, eps, tok):
        s = small[0] % NSM
        small[0] += 1
        a = Q.act(op_activation, (tok, eps_tok, rc_read[s]), SD[:, s, 0:n], PB[b][:, 0:n], ACT.Sqrt,
                  bias=EPS[:, eps:eps + 1], scale=scale)
        free[b] = a
        r = Q.dve(op_reciprocal, (a, rc_read[s]), RC[:, s, 0:n], SD[:, s, 0:n])
        return s, r

    def spread(b, s, ng, tok, ntok=TT):
        w = 128 // ng
        for j in range(ntok):
            for g in range(ng):
                c = j * ng + g
                t = mm(PB[b][g * w:(g + 1) * w, j * 128:(j + 1) * 128], RC[:, s, c:c + 1].to_broadcast([128, w]),
                       ident, True, True, tok, free[b] if j == 0 else None,
                       mark=(j == ntok - 1 and g == ng - 1))
        rc_read[s] = t
        return t

    one = CB[:, C_ONE:C_ONE + 1]
    x_tok = [None] * KT
    sq_free = [None, None]
    h_tok = [None] * KT

    def stale():
        h_tok[:] = [None] * KT
        hread[0] = Q.last("pe", "act", "dve", "pool")

    sqn = [0]

    def square(src, tok):
        i = sqn[0] % 2
        sqn[0] += 1
        t = Q.act(op_activation, (tok, sq_free[i],), SQ[:, i, :], src, ACT.Square)
        return i, t

    def watch(tile, toks, sqs, least=1):
        for m in range(KT):
            if len(toks) <= max(m, least - 1):
                yield lambda m=m: len(toks) > max(m, least - 1)
                yield toks[m]
            i = min(m, 1)
            sq = Q.act(op_activation, (toks[m], sq_free[i]), SQ[:, i, :], tile(m), ACT.Square)
            if 0 < m < KT - 1:
                total = sq_free[1] = Q.pool(op_tensor_tensor, (sq, total), SQ[:, 0, :], SQ[:, 0, :], SQ[:, 1, :],
                                            ALU.add)
            else:
                total = sq
            if m == KT - 2:
                Q.table("sqrt_and_others")
                yield total
                add_stat(0, total, 6, True, False)
        yield sq
        sqs.append(add_stat(1, sq, 6, False, True))

    def add_stat(i, t, b, first, last):
        u = stat(SQ[:, i, :], b, one, 1, first, t, last=last)
        sq_free[i] = u
        return u

    def make_h(a_col, s_col, rb, rt, par):
        ts = {}

        def scaled(k):
            ts[k] = Q.dve(op_scalar_tensor_tensor, (rt, x_tok[k], par, hread[0] if k == 0 else None,
                          h_tok_[k - 2] if k > 1 else None),
                          out=TM[:, k % 2, :], in0=X[:, k, :], scalar=a_col(k), in1=PB[rb][:, :], op0=ALU.mult,
                          op1=ALU.mult)
            if k == KT - 1:
                free[rb] = ts[k]

        h_tok_ = {}
        h_free = hread[0]
        scaled(0)
        for k in range(KT):
            i = k % 2
            if s_col is None:
                hi = Q.act(op_activation, (ts[k], h_free), HH[:, k, :], TM[:, i, :], ACT.Copy)
            else:
                hi = Q.act(op_activation, (ts[k], h_free, par), HH[:, k, :], TM[:, i, :], ACT.Identity, bias=s_col(k))
            if k + 1 < KT:
                scaled(k + 1)
            if s_col is None:
                lo = Q.dve(op_tensor_tensor, (ts[k], hi), HL[:, k, :], TM[:, i, :], f(HH[:, k, :]), ALU.subtract)
            else:
                lo = Q.dve(op_scalar_tensor_tensor, (ts[k], hi), out=HL[:, k, :], in0=TM[:, i, :], scalar=s_col(k),
                           in1=f(HH[:, k, :]), op0=ALU.add, op1=ALU.subtract)
            h_tok_[k] = h_tok[k] = [hi, lo]
            yield

    def rms_x():
        s = small[0] % NSM
        small[0] += 1
        u = Q.dve(op_tensor_tensor, (st,), SD[:, s, 12:16], SD[:, s, 4:12:2], SD[:, s, 5:12:2], ALU.add)
        a = Q.act(op_activation, (u, eps_tok), SD[:, s, 0:TT], SD[:, s, 12:16], ACT.Sqrt, bias=EPS[:, 0:1],
                  scale=1.0 / D)
        r = Q.dve(op_reciprocal, (a,), RC[:, s, 0:TT], SD[:, s, 0:TT])
        rt = spread(5, s, 1, r)
        use_until(0)
        yield from make_h(gcol("pre_mix_g"), None, 5, rt, pc_tok)

    def rms_h(tok, a_col, s_col, par, sb=6, rb=5):
        s, r = root(sb, TT, 1.0 / D, 0, tok)
        yield r
        rt = spread(rb, s, 1, r)
        yield from make_h(a_col, s_col, rb, rt, par)

    def split_into(k, src, tok):
        hi = Q.act(op_activation, (tok,), HH[:, k, :], src, ACT.Copy)
        lo = Q.dve(op_tensor_tensor, (tok, hi,), HL[:, k, :], src, f(HH[:, k, :]), ALU.subtract)
        h_tok[k] = [hi, lo]

    x_in = [Q.dma(f"x{j}", op_dma_start, (), XTM[:, j, :], I["x"][0, j * 128:(j + 1) * 128, :])
            for j in range(2)]
    cb_in = Q.dma("cb", op_dma_start, (), CB[:, 0:C_TRI], I["c_b"][:, 0:C_TRI], engine="act")
    cc_in = Q.dma("cc", op_dma_start, (), CC[:, :], I["c_2"].rearrange("o (p k) -> p (o k)", k=8), engine="act")
    x_in += [Q.dma(f"x{j}", op_dma_start, (), XTM[:, j, :], I["x"][0, j * 128:(j + 1) * 128, :])
             for j in range(2, 4)]

    z_tok = Q.pool(op_memset, (), PR[:, :, :], 0.0)
    pr = []
    at_row = 0

    def rows(tile, r0, v, w=128):
        pr.append(Q.dma("pr" if tile else "pr0", op_dma_start, (z_tok,), PR[r0:r0 + v.shape[0], tile, 0:v.shape[1]], v,
                        engine="pool" if tile else "act"))

    gains = {}
    for name in ("pre_mix_g", "post_mix_g", "pre_mem_g", "post_mem_g", "mem_norm_g", "pre_ffn_g",
                 "post_ffn_g"):
        rows(0, at_row, I[name][0].rearrange("(a b) -> a b", b=128))
        gains[name] = at_row
        at_row += 8
    for name in ("attn_gn_g", "ret_gn_g"):
        rows(0, at_row, I[name][0].rearrange("(a b) -> a b", b=128))
        gains[name] = at_row
        at_row += 4
    P2 = {}
    pr0_tok = pr[-1]
    for l in range(2):
        at_row = 0

        def add(name, v, n):
            nonlocal at_row
            rows(1 + l, at_row, v)
            P2[(name, l)] = 64 + 66 * l + at_row
            at_row += n

        add("g_norm", I["g_norm_2"][l].rearrange("j (a b) -> (j a) b", b=128), 24)
        add("conv_w", I["conv_w_2"][l].rearrange("j (a b) -> (j a) b", b=128), 16)
        for nm in ("conv_b_2", "b_rgate_2", "b_igate_2", "lru_lambda_2"):
            add(nm, I[nm][l].rearrange("(a b) -> a b", b=128), 4)
        add("g_mix", I["g_mix_out_2"][l].rearrange("(a b) -> a b", b=128), 8)
        for u in range(2):
            pr.append(Q.dma("pr", op_dma_start, (z_tok,), PR[at_row:at_row + 2, 1 + l, 64 * u:64 * u + 64], I["g_qk_2"][l], engine="pool"))
        P2[("g_qk", l)] = 64 + 66 * l + at_row
        rows(3 + l, 0, I["b_ada_2"][l].rearrange("(a b) -> a b", b=128))
    pr_tok = pr[-1]
    cb2_in = Q.dma("cb2", op_dma_start, (), CB[:, C_TRI:CB_W], I["c_b"][:, C_TRI:CB_W], engine="act")
    msk_in = Q.dma("ct", op_dma_start, (), MSK[:, :], I["c_t"][:, T_MASK:T_MASK + 512], engine="act")
    rope_in = Q.dma("ct", op_dma_start, (), ROPE[:, :, :], I["c_t"][:, T_ROPE:T_DEC].rearrange("p (a b) -> p a b", a=4), engine="act")
    for _ in range(NS):
        emit_dma()

    e0 = Q.dve(op_memset, (), EPS[:, 0:1], RMS_EPS)
    e0 = Q.dve(op_memset, (), EPS[:, 1:2], GN_EPS)
    eps_tok = Q.dve(op_memset, (), EPS[:, 2:3], 1.0)

    cs_tok = Q.act(op_activation, (cc_in,), CS[:, :], CC[:, :], ACT.Silu)
    for j in range(TT):
        for hf in range(2):
            t = Q.act(op_activation, (x_in[j], sq_free[hf]), SQ[:, hf, :], XTM[:, j, hf * 512:(hf + 1) * 512],
                      ACT.Square, accum_out=SD[:, 0, 4 + 2 * j + hf:5 + 2 * j + hf])
            sq_free[hf] = t
    st = t
    for m in range(KT):
        b = take()
        for j in range(TT):
            t = Q.pe(op_transpose, (x_in[j], cb_in, free[b] if j == 0 else None,), PB[b][:, j * 128:(j + 1) * 128], XTM[:, j, m * 128:(m + 1) * 128], ident, mark=(j == TT - 1))
        x_tok[m] = free[b] = Q.dve(op_tensor_copy, (t,), X[:, m, :], PB[b][:, :])

    t = Q.pe(op_transpose, (pr0_tok, z_tok, cb_in), PB[4][:, 0:128], PR[:, 0, :], ident, mark=True)
    pc_tok = free[4] = Q.dve(op_tensor_copy, (t,), PC[:, 0:64], PB[4][:, 0:64])

    def params():
        nonlocal pc_tok
        t = None
        for n, (tl, c0, w) in enumerate([(1, 64, 66), (2, 130, 66), (3, 196, 72), (4, 268, 72)]):
            t = Q.pe(op_transpose, (pr_tok, z_tok, cb_in, free[6] if n == 0 else None), PB[6][:, n * 128:(n + 1) * 128],
                     PR[:, tl, :], ident, mark=n == 3)
        for n, (tl, c0, w) in enumerate([(1, 64, 66), (2, 130, 66), (3, 196, 72), (4, 268, 72)]):
            pc_tok = free[6] = Q.dve(op_tensor_copy, (t,), PC[:, c0:c0 + w], PB[6][:, n * 128:n * 128 + w])
        yield None

    def col(c):
        return PC[:, c:c + 1]

    def gcol(name):
        return lambda k: col(gains[name] + k)

    chain("s", rms_x())
    force(lambda: h_tok[KT - 1] is not None)
    Task(params()).step()

    rp = {}
    rope_n, rope_over = [0], [0]
    tm_free = [None, None]

    def after(need, fn):
        yield need
        fn()

    def rope_out(dst, table, perm, banks, key):
        def evac(m, ps, t):
            nth = rope_n[0]
            i = nth % 2
            rope_n[0] += 1
            while rope_over[0] < nth - 1:
                chains["rope"][0].step()
                best()
            c = Q.act(op_activation, (t, sq_free[i], Q.last("dve"),), SQ[:, i, :], ps, ACT.Copy)

            def rest():
                bk = banks[i % len(banks)] if banks else take()
                p = mm(PB[bk][:, :], CB[:, perm:perm + 128], SQ[:, i, :], True, True, c, cb2_in, free[bk], mark=True)
                u = Q.dve(op_tensor_tensor, (c, rope_in, tm_free[i],), TM[:, i, :], SQ[:, i, :], ROPE[:, table, :], ALU.mult)
                v = Q.dve(op_tensor_tensor, (p,), dst[:, m, :], PB[bk][:, :], ROPE[:, table + 1, :],
                                                    ALU.mult)
                free[bk] = v
                sq_free[i] = [u, p]
                rp[key, m] = Q.dve(op_tensor_tensor, (u, v,), dst[:, m, :], dst[:, m, :], TM[:, i, :],
                                                             ALU.add)
                tm_free[i] = rp[key, m]
                rope_over[0] += 1
            chain("rope", after(c, rest))
            return c
        return evac

    for c in range(2):
        run(proj_fm(2, HH, HL, h_tok, rope_out(AQ, 0, C_PA, (4, 5), "aq"), c == 0, m0=2 * c))
    for c in range(2):
        run(proj_fm(2, HH, HL, h_tok, rope_out(AK, 0, C_PA, (4, 5), "ak"), False, m0=2 * c))

    def tm_out(dst, c, key):
        def evac(b2, ps, t):
            tk = Q.act(op_activation, (t,), dst[:, 2 * b2:2 * b2 + 2, c * 256:(c + 1) * 256], ps, ACT.Copy)
            rp[key, c, b2] = tk
            return tk
        return evac

    for c in range(2):
        run(proj_tm(TT, HH, HL, h_tok, tm_out(AV, c, "av")))
    pump(3)

    def soft_attention(items, score, n_of, ss, pt, finish, sbanks, values=None):
        ssf = [None] * len(ss)
        ptf = [None] * len(pt)
        over = set()

        def item(it, h, i):
            a, p, sm = it % len(ss), it % len(pt), it % 4
            n = n_of(i)
            sb = sbanks[it % len(sbanks)]
            yield lambda: free[sb] or True
            tok = score(h, i, sb, ss[a], SM[:, sm, :], ssf[a])
            yield [tok, lambda: it < len(pt) or it - len(pt) in over]
            tb = take()
            for j in range(n // 128):
                t = Q.pe(op_transpose, (tok, free[tb] if j == 0 else None), PB[tb][:, j * 128:(j + 1) * 128],
                         ss[a][:, j * 128:(j + 1) * 128], ident, mark=(j == n // 128 - 1))
            ssf[a] = t
            c = free[tb] = Q.act(op_activation, (t, ptf[p]), pt[p][:, 0:n], PB[tb][:, 0:n], ACT.Copy)
            yield [c, values or (lambda: True)]
            ptf[p] = finish(h, i, pt[p], c, n // 128)
            over.add(it)

        return [item(it, h, i) for it, (h, i) in enumerate(items)]

    def norm_rows(sstile, sm, n, tok):
        r = Q.dve(op_reciprocal, (tok,), sm[:, 3:4], sm[:, 2:3])
        return Q.dve(op_tensor_scalar, (tok, r,), sstile[:, 0:n], sstile[:, 0:n], sm[:, 3:4], None, ALU.mult)

    def dil_score(h, i, sb, sst, sm, f1):
        n = 128 * (i + 1)
        po, m = 64 * (h % 2), h // 2
        t = mm(PB[sb][:, 0:n], AQ[po:po + 64, m, i * 128:(i + 1) * 128], AK[po:po + 64, m, 0:n], True, True,
               rp["aq", m], rp["ak", m], free[sb], mark=True)
        a = Q.dve(op_tensor_tensor_reduce, (t, msk_in, f1), out=sst[:, 0:n], in0=PB[sb][:, 0:n], in1=MSK[:, 512 - n:512], scale=0.125, scalar=-3e38,
            op0=ALU.add, op1=ALU.max, accum_out=sm[:, 0:1])
        free[sb] = a
        g = Q.dve(op_tensor_scalar, (a,), sm[:, 1:2], sm[:, 0:1], -1.0, None, ALU.mult)
        x = Q.act(op_activation, (g,), sst[:, 0:n], sst[:, 0:n], ACT.Exp, bias=sm[:, 1:2],
                                         accum_out=sm[:, 2:3])
        return norm_rows(sst, sm, n, x)

    an = {}

    def many_norm(tiles, wait, scale, done):
        sd = FG[:, 0:2, :].rearrange("p a b -> p (a b)")
        rc = FG[:, 2:4, :].rearrange("p a b -> p (a b)")
        for n, (src, key, m, _) in enumerate(tiles):
            yield lambda key=key, m=m: (key, m) in an
            i, t = square(src[:, m, :], an[key, m])
            yield t
            u = stat(SQ[:, i, :], 5, CB[:, C_SEL:C_SEL + 2], 2, n == 0, t, col=8 * n, last=n == 3)
            sq_free[i] = u
        yield wait
        a_ = free[5] = Q.act(op_activation, (u, eps_tok, Q.last("dve")), sd, PB[5][:, 0:32], ACT.Sqrt,
                             bias=EPS[:, 0:1], scale=scale)
        r = Q.dve(op_reciprocal, (a_,), rc, sd)
        yield r
        for n, (src, key, m, g) in enumerate(tiles):
            for j in range(TT):
                for u2 in range(2):
                    c = 8 * n + 2 * j + u2
                    t = mm(PB[5][u2 * 64:(u2 + 1) * 64, j * 128:(j + 1) * 128],
                           FG[:, 2 + c // 16, c % 16:c % 16 + 1].to_broadcast([128, 64]), ident, True, True, r,
                           free[5] if j == 0 else None, mark=(j == TT - 1 and u2 == 1))
            done[key, m] = free[5] = Q.dve(op_scalar_tensor_tensor, (t, pc_tok, u), out=src[:, m, :],
                                           in0=src[:, m, :], scalar=g, in1=PB[5][:, :], op0=ALU.mult, op1=ALU.mult)
            yield done[key, m]

    def head_pair_finish(v, vkeys, dst, key):
        def finish(h, i, ptt, tok, blocks):
            po, m = 64 * (h % 2), h // 2
            for j in range(blocks):
                t = mm(PB[7][po:po + 64, i * 128:(i + 1) * 128], v[:, j, h * 64:(h + 1) * 64],
                       ptt[:, j * 128:(j + 1) * 128], j == 0, j == blocks - 1, tok,
                       [rp[k] for k in vkeys(h)], free[7] if h % 2 == 0 and i == TT - 1 else None,
                       mark=(j == blocks - 1))
            if h % 2 == 1 and i == 0:
                an[key, m] = free[7] = Q.act(op_activation, (t,), dst[:, m, :], PB[7][:, :], ACT.Copy)
            return t
        return finish

    SSX = region("SSX", 25, [128, 2, S])
    chain("s", Window(soft_attention(
        [(h, i) for h in range(8) for i in (3, 2, 1, 0)], dil_score, lambda i: 128 * (i + 1),
        [SS[:, 0, :], SS[:, 1, :], SSX[:, 0, :], SSX[:, 1, :]], [PT[:, 0, :], PT[:, 1, :]],
        head_pair_finish(AV, lambda h: [("av", h // 4, 0), ("av", h // 4, 1)], AQ, "a"), (4,)), 4))
    for c in range(2):
        run(proj_fm(2, HH, HL, h_tok, rope_out(RQ, 2, C_PR, (), "rq"), False, m0=2 * c))
    for c in range(2):
        run(proj_fm(2, HH, HL, h_tok, rope_out(RK, 2, C_PR, (), "rk"), False, m0=2 * c))
    drain("rope")
    rope_done = Q.last("dve")
    DEC = region("DEC", 27, [128, 2, 512])
    dec_free = [rope_done, rope_done]
    dec_in = {}

    def load_dec(h):
        dec_in[h] = Q.dma(f"dec{h % 2}", op_dma_start, (dec_free[h % 2],), DEC[:, h % 2, :],
                          I["c_t"][:, T_DEC + h * 512:T_DEC + (h + 1) * 512])

    for h in range(2):
        load_dec(h)
    for c in range(2):
        run(proj_tm(TT, HH, HL, h_tok, tm_out(RV, c, "rv")))

    def ret():
        bufs = [TM[:, 0, :], TM[:, 1, :], SS[:, 0, :], SS[:, 1, :]]
        ssf = [rope_done, rope_done, None, None]
        busy = set()

        def dil_over():
            return ("a", 3) in an

        def item(it, h, j):
            n = S - 128 * j
            if dil_over() and not ssf[2]:
                ssf[2] = ssf[3] = Q.last("pe", "act", "dve")
            c = min((x for x in range(4 if dil_over() else 2) if x not in busy), key=lambda x: Q.when(ssf[x]))
            busy.add(c)
            sb = (4, 7)[it % 2] if dil_over() else 4
            if j == 0 and 1 <= h < 3:
                dec_free[(h + 1) % 2] = Q.last("dve")
                load_dec(h + 1)
            t = mm(PB[sb][:, 0:n], RK[:, h, j * 128:(j + 1) * 128], RQ[:, h, j * 128:S], True, True,
                   rp["rq", h], rp["rk", h], free[sb], mark=True)
            sc = free[sb] = Q.dve(op_tensor_tensor, (t, dec_in[h], ssf[c]), bufs[c][:, 0:n], PB[sb][:, 0:n],
                                  DEC[:, h % 2, 0:n], ALU.mult)
            yield [sc, lambda: j > 0 or h == 0 or ("r", h - 1) in rp]
            t = mm(PB[6][:, j * 128:S], RV[:, j, h * 128:(h + 1) * 128], bufs[c][:, 0:n], j == 0, j == 3,
                   sc, rp["rv", h // 2, 0], rp["rv", h // 2, 1], free[6] if j == 0 else None, mark=True)
            ssf[c] = t
            busy.discard(c)
            if j == 3:
                rp["r", h] = free[6] = Q.act(op_activation, (t,), RQ[:, h, :], PB[6][:, :], ACT.Copy)

        return Window([item(4 * h + j, h, j) for h in range(4) for j in range(4)], 4,
                      lambda n: len(busy) < (4 if dil_over() else 2))

    def ret_norm():
        sv = small[0] % NSM
        small[0] += 1
        vb = 5
        for h in range(4):
            yield lambda: ("r", h) in rp
            s = small[0] % NSM
            small[0] += 1
            b = take(True)
            u = stat(RQ[:, h, :], b, one, 1, True, rp["r", h])
            c = Q.dve(op_tensor_scalar, (u, rc_read[s]), RC[:, s, 0:TT], PB[b][:, 0:TT], 1.0 / 128, None, ALU.mult)
            free[b] = c
            yield c
            rt = spread(b, s, 1, c)
            d = Q.dve(op_tensor_tensor, (rt, rp["r", h]), RQ[:, h, :], RQ[:, h, :], PB[b][:, :], ALU.subtract)
            let_go(b, d)
            i, t = square(RQ[:, h, :], d)
            yield t
            u = stat(SQ[:, i, :], vb, one, 1, h == 0, t, col=4 * h, last=h == 3)
            sq_free[i] = u
        a = free[vb] = Q.act(op_activation, (u, eps_tok, rc_read[sv]), SD[:, sv, 0:16], PB[vb][:, 0:16], ACT.Sqrt,
                             bias=EPS[:, 1:2], scale=1.0 / 128)
        r = Q.dve(op_reciprocal, (a, rc_read[sv]), RC[:, sv, 0:16], SD[:, sv, 0:16])
        yield r
        for h in range(4):
            for j in range(TT):
                bk = (5, 7)[h % 2]
                rt = mm(PB[bk][:, j * 128:(j + 1) * 128], RC[:, sv, 4 * h + j:4 * h + j + 1].to_broadcast([128, 128]),
                        ident, True, True, r, free[bk] if j == 0 else None, mark=j == TT - 1)
            v = free[bk] = Q.dve(op_scalar_tensor_tensor, (rt, t, d), out=RQ[:, h, :], in0=RQ[:, h, :],
                                 scalar=col(gains["ret_gn_g"] + h), in1=PB[bk][:, :], op0=ALU.mult, op1=ALU.mult)
            rp["rn", h] = v
            yield None
        rc_read[sv] = rt

    chain("r", ret())
    chain("n", many_norm([(AQ, "a", m, col(gains["attn_gn_g"] + m)) for m in range(4)], None, 1.0 / 64, rp))
    chain("n", ret_norm())

    def rg_out(m, ps, t):
        rp["rg", m] = Q.act(op_activation, (t, dil_done,), RG[:, m, :], ps, ACT.Copy)
        return rp["rg", m]

    force(lambda: ("a", 3) in an)
    dil_done = Q.last("pe", "dve")
    for c in range(2):
        run(proj_fm(2, HH, HL, h_tok, rg_out, False, m0=2 * c))
    h_free = Q.last("pe")
    stale()

    def mix_h():
        for m in range(4):
            yield lambda: ("a", m) in rp
            yield rp["a", m]
            split_into(m, AQ[:, m, :], [rp["a", m], h_free])
        yield rp["rg", 3]
        for m in range(4):
            rp["rg", m] = Q.act(op_activation, (rp["rg", m],), RG[:, m, :], RG[:, m, :], ACT.Silu)
        for h in range(4):
            yield lambda: ("rn", h) in rp
            g = Q.dve(op_tensor_tensor, (rp["rn", h], rp["rg", h]), RQ[:, h, :], RQ[:, h, :], RG[:, h, :], ALU.mult)
            split_into(4 + h, RQ[:, h, :], [g, h_free])

    chain("h", mix_h())

    y_tok = {}

    def y_evac(dst, toks):
        def evac(m, ps, t):
            y_tok[m] = Q.act(op_activation, (t,), dst[:, m, :], ps, ACT.Copy)
            toks.append(y_tok[m])
            return y_tok[m]
        return evac

    def post(src, gname, a_col, s_col, par, sqs, more=None):
        more = SQ2 if more is None else more
        s, r = root(6, TT, 1.0 / D, 0, sqs[-1])
        yield r
        rt = spread(5, s, 1, r)
        sq4 = [sq_free[0], sq_free[1], hread[0], hread[0]]
        ys = {}

        def scaled(m):
            ys[m] = Q.dve(op_scalar_tensor_tensor, (rt, y_tok[m], pc_tok, x_tok[m - 2] if m > 1 else None),
                          out=TM[:, m % 2, :], in0=src[:, m, :], scalar=col(gains[gname] + m), in1=PB[5][:, :],
                          op0=ALU.mult, op1=ALU.mult)
            if m == KT - 1:
                free[5] = ys[m]

        scaled(0)
        for m in range(KT):
            if m + 1 < KT:
                scaled(m + 1)
            x_tok[m] = Q.dve(op_tensor_tensor, (ys[m],), X[:, m, :], X[:, m, :], TM[:, m % 2, :], ALU.add)
            bufs = [SQ[:, 0, :], SQ[:, 1, :], more[:, 0, :], more[:, 1, :]]
            sq = Q.act(op_activation, (x_tok[m], sq4[m % 4]), bufs[m % 4], X[:, m, :], ACT.Square)
            if m % 2 == 0:
                even = sq
                if m:
                    u = stat(bufs[(m + 2) % 4], 6, one, 1, m == 2, pair, last=False)
                    sq4[(m + 2) % 4] = u
            else:
                add = Q.dve if m == KT - 1 else Q.pool
                pair = add(op_tensor_tensor, (even, sq), bufs[(m - 1) % 4], bufs[(m - 1) % 4], bufs[m % 4], ALU.add)
                sq4[m % 4] = pair
            yield
        st2 = stat(bufs[(KT - 2) % 4], 6, one, 1, False, pair)
        sq_free[0], sq_free[1] = [sq4[0], st2], [sq4[1], st2]
        yield from rms_h(st2, a_col, s_col, par)

    mem_tok = [None] * KT

    def mem_load():
        w = y_free
        mem_in = Q.dma("mem", op_dma_start, (w,), MTM[:, :, :], I["mem"][0].rearrange("(a p) d -> p a d", p=128), engine="act")
        yield mem_in
        s = small[0] % NSM
        small[0] += 1
        for a in range(2):
            for hf in range(2):
                t = Q.act(op_activation, (mem_in, Q.last("act"),), VM[:, hf, 0:512], MTM[:, a, hf * 512:(hf + 1) * 512], ACT.Square,
                    accum_out=SD[:, s, 4 + 2 * a + hf:5 + 2 * a + hf])
        u = Q.dve(op_tensor_tensor, (t,), SD[:, s, 8:10], SD[:, s, 4:8:2], SD[:, s, 5:8:2], ALU.add)
        v = Q.act(op_activation, (u,), SD[:, s, 0:2], SD[:, s, 8:10], ACT.Sqrt, bias=EPS[:, 0:1],
                                         scale=1.0 / D)
        r = Q.dve(op_reciprocal, (v,), RC[:, s, 0:2], SD[:, s, 0:2])
        for a in range(2):
            sc = Q.act(op_activation, (r, t,), MTM[:, a, :], MTM[:, a, :], ACT.Copy, scale=RC[:, s, a:a + 1])
        yield sc
        for k in range(KT):
            bk = (4, 7)[k % 2]
            for a in range(2):
                p = Q.pe(op_transpose, (sc, free[bk] if a == 0 else None,), PB[bk][:, a * 128:(a + 1) * 128], MTM[:, a, k * 128:(k + 1) * 128], ident, mark=(a == 1))
            hi = Q.act(op_activation, (p, w,), MH[:, k, :], PB[bk][:, 0:NMEM], ACT.Copy,
                                                   scale=col(gains["mem_norm_g"] + k))
            lo = Q.dve(op_scalar_tensor_tensor, (hi, w,), out=ML[:, k, :], in0=PB[bk][:, 0:NMEM], scalar=col(gains["mem_norm_g"] + k),
                in1=f(MH[:, k, :]), op0=ALU.mult, op1=ALU.subtract)
            free[bk] = lo
            mem_tok[k] = [hi, lo]
            yield lo

    force(lambda: h_tok[7] is not None or not chains["r"])
    y_free = []

    def y_evac1(m, ps, t):
        if not y_free:
            y_free.append(Q.last("pe", "act", "dve"))
        return y_evac(Y, yt)(m, ps, [t, y_free])

    sqs, yt = [], []
    run(proj_fm3(HH, HL, h_tok, y_evac1, first=3))
    chain("s", mem_load())
    chain("w", watch(lambda m: Y[:, m, :], yt, sqs))
    for c in range(2, 4):
        run(proj_fm(2, HH, HL, h_tok, y_evac1, False, m0=2 * c))
    force(lambda: mem_tok[KT - 1] is not None)
    force(lambda: sqs)
    stale()
    chain("p", post(Y, "post_mix_g", gcol("pre_mem_g"), None, pc_tok, sqs, SQ3))
    km = {}

    def km_out(m, ps, t):
        km[m] = Q.act(op_activation, (t,), KM[:, m, :], ps, ACT.Copy)
        return km[m]

    def vm_out(c):
        def evac(b2, ps, t):
            km["v", c] = Q.act(op_activation, (t,), VM[:, :, c * 256:(c + 1) * 256], ps, ACT.Copy)
            return km["v", c]
        return evac

    for c in range(4):
        run(proj_fm(2, MH, ML, mem_tok, km_out, False, ntok=NMEM, m0=2 * c))
    for c in range(4):
        run(proj_tm(2, MH, ML, mem_tok, vm_out(c)))
    drain()

    xq = {}

    def xq_out(m, ps, t):
        xq[m] = Q.act(op_activation, (t,), XQ[:, m, :], ps, ACT.Copy)
        return xq[m]

    def x_score(h, i, sb, sst, sm, f1):
        for c in range(2):
            t = mm(PB[sb][:, 0:NMEM], XQ[:, 2 * h + c, i * 128:(i + 1) * 128], KM[:, 2 * h + c, :], c == 0,
                   c == 1, xq[2 * h + c], km[2 * h + c], free[sb] if c == 0 else None, mark=(c == 1))
        a = Q.dve(op_tensor_reduce, (t,), sm[:, 0:1], PB[sb][:, 0:NMEM], AX.X, ALU.max)
        g = Q.dve(op_tensor_scalar, (a,), sm[:, 1:2], sm[:, 0:1], -1.0 / 16, None, ALU.mult)
        x = Q.act(op_activation, (g, f1,), sst[:, 0:NMEM], PB[sb][:, 0:NMEM], ACT.Exp, bias=sm[:, 1:2],
                                         scale=1.0 / 16, accum_out=sm[:, 2:3])
        free[sb] = x
        return norm_rows(sst, sm, NMEM, x)

    ox = {}

    def x_finish(h, i, ptt, tok, blocks):
        for c in range(2):
            bk = 7 - c
            for a in range(2):
                t = mm(PB[bk][:, i * 128:(i + 1) * 128], VM[:, a, h * 256 + c * 128:h * 256 + (c + 1) * 128],
                       ptt[:, a * 128:(a + 1) * 128], a == 0, a == 1, tok, km["v", h],
                       free[bk] if i == 0 else None, mark=(a == 1))
            if i == TT - 1:
                ox[2 * h + c] = free[bk] = Q.act(op_activation, (t,), XQ[:, 2 * h + c, :], PB[bk][:, :], ACT.Copy)
        return t

    chain("s", Window(soft_attention(
        [(h, i) for h in range(4) for i in range(TT)], x_score, lambda i: NMEM,
        [XS[:, i, :] for i in range(4)], [XP[:, i, :] for i in range(4)], x_finish, (4, 5)), 4,
        gate=lambda it: (2 * (it // TT) + 1) in xq))
    for h in range(4):
        run(proj_fm(2, HH, HL, h_tok, xq_out, h == 0, m0=2 * h))
    q_done = Q.last("pe")
    stale()

    def x_split():
        for k in range(KT):
            yield lambda: k in ox
            yield ox[k]
            split_into(k, XQ[:, k, :], [ox[k], q_done])

    chain("h", x_split())
    sqs, yt = [], []
    y_free = []
    run(proj_fm3(HH, HL, h_tok, y_evac1))
    chain("w", watch(lambda m: Y[:, m, :], yt, sqs))
    for c in range(2, 4):
        run(proj_fm(2, HH, HL, h_tok, y_evac1, False, m0=2 * c))
    drain()
    stale()
    chain("s", post(Y, "post_mem_g", gcol("pre_ffn_g"), None, pc_tok, sqs))

    gh_free = [None] * HALF
    sg_free = [None, None]

    def ffn(down_evac):
        for half in range(2):
            g_tok = [None] * HALF

            def up(m):
                force(lambda: h_tok[7] is not None)
                i, vh, vl, wt = next_slab()
                b2 = [take(True), take(True)]
                seq = [(k, u) for k in range(KT) for u in range(2)] if m == 0 else \
                      [(k, u) for u in range(2) for k in range(KT)]
                t2 = [None, None]
                for n, (k, u) in enumerate(seq):
                    force(lambda: h_tok[k] is not None)
                    t = mm3_w(PB[b2[u]][:, :], vh[:, k, u, :], vl[:, k, u, :], HH[:, k, :], HL[:, k, :],
                              k == 0, k == KT - 1, wt, h_tok[k], free[b2[u]] if k == 0 else None,
                              mark=(k == KT - 1))
                    if k == KT - 1:
                        t2[u] = t
                        if u == 0:
                            sg = Q.act(op_activation, (t, sg_free[m % 2],), SG[:, m % 2, :], PB[b2[0]][:, :], ACT.Silu)
                            let_go(b2[0], sg)
                    if n % 2:
                        yield
                done_slab(i, t2[1])
                p = Q.dve(op_tensor_tensor, (t2[1], sg, Q.last("dve"),), TM[:, m % 2, :], PB[b2[1]][:, :], SG[:, m % 2, :],
                                                    ALU.mult)
                sg_free[m % 2] = p
                let_go(b2[1], p)
                hi = Q.act(op_activation, (p, gh_free[m],), GH[:, m, :], TM[:, m % 2, :], ACT.Copy)
                lo = Q.dve(op_tensor_tensor, (hi, p, gh_free[m],), GL[:, m, :], TM[:, m % 2, :], f(GH[:, m, :]),
                                                     ALU.subtract)
                g_tok[m] = [hi, lo]

            for m in range(HALF):
                yield from up(m)
            for k0, kn in ((0, 4), (4, 4), (8, 3)):
                i, vh, vl, wt = next_slab()
                for kk in range(kn):
                    k = k0 + kk
                    for m in range(4):
                        t = mm3_w(PB[4 + m][:, :], vh[:, kk, m * 128:(m + 1) * 128],
                                  vl[:, kk, m * 128:(m + 1) * 128], GH[:, k, :], GL[:, k, :], k == 0,
                                  k == HALF - 1, wt, g_tok[k], free[4 + m] if k == 0 else None,
                                  mark=(k == HALF - 1 or (m == 3 and kk == kn - 1)))
                        if k == HALF - 1:
                            free[4 + m] = down_evac(half, m, PB[4 + m][:, :], t)
                        if m % 2:
                            yield
                done_slab(i, t)
            for m in range(4, 8):
                i, vh, vl, wt = next_slab()
                b = take(True)
                for k in range(HALF):
                    t = mm3_w(PB[b][:, :], vh[:, k, :], vl[:, k, :], GH[:, k, :], GL[:, k, :], k == 0,
                              k == HALF - 1, wt, g_tok[k], free[b] if k == 0 else None,
                              mark=(k == HALF - 1 or m == 7))
                    if m == 7:
                        gh_free[k] = t
                    if k % 2:
                        yield
                done_slab(i, t)
                let_go(b, down_evac(half, m, PB[b][:, :], t))

    def ffn1_evac(half, m, ps, t):
        if half == 0:
            y_tok[m] = Q.act(op_activation, (t,), Y1[:, m, :], ps, ACT.Copy)
            return y_tok[m]
        y_tok[m] = Q.dve(op_tensor_tensor, (t, y_tok[m],), Y1[:, m, :], ps, Y1[:, m, :], ALU.add)
        yt.append(y_tok[m])
        return y_tok[m]

    sqs, yt = [], []
    chain("w", watch(lambda m: Y1[:, m, :], yt, sqs, 4))
    run(ffn(ffn1_evac))
    drain()
    flush_ada()

    def mod_cols(l):
        g0 = P2["g_norm", l]
        toks = []
        for j in range(3):
            c = (3 * j + 1) * 8
            toks.append(Q.dve(op_scalar_tensor_tensor, (mod_tok[l], pc_tok, Q.last("pe", "act"),), out=MA[:, 8 * j:8 * j + 8], in0=MOD[:, l, c:c + 8], scalar=1.0, in1=PC[:, g0 + 8 * j:g0 + 8 * j + 8],
                op0=ALU.add, op1=ALU.mult))
            c2 = (3 * j + 2) * 8
            hf = 1.0 if j == 1 else 0.5
            toks.append(Q.dve(op_tensor_scalar, (mod_tok[l],), MG[:, 8 * j:8 * j + 8], MOD[:, l, c2:c2 + 8], hf, hf, ALU.mult, ALU.add))
        return toks[-1]

    def a2(j):
        return lambda k: MA[:, 8 * j + k:8 * j + k + 1]

    def s2(l, j):
        return lambda k: MOD[:, l, 24 * j + k:24 * j + k + 1]

    def g2(j):
        return lambda k: MG[:, 8 * j + k:8 * j + k + 1]

    def x_add(j, toks):
        def evac(m, ps, t, whole=True):
            x_tok[m] = Q.dve(op_scalar_tensor_tensor, (t, x_tok[m]), out=X[:, m, :], in0=ps, scalar=g2(j)(m),
                             in1=X[:, m, :], op0=ALU.mult, op1=ALU.add)
            if whole:
                toks.append(x_tok[m])
            return x_tok[m]
        return evac

    def ffn2(j, want):
        sqs, xt = [], []
        ev = x_add(j, xt)
        if want:
            chain("w", watch(lambda m: X[:, m, :], xt, sqs, 4))
        run(ffn(lambda half, m, ps, t: ev(m, ps, t, whole=half == 1)))
        drain()
        return sqs

    mt = mod_cols(0)
    stale()
    chain("s", post(Y1, "post_ffn_g", a2(0), s2(0, 0), mt, sqs))

    def mixer2(l):
        hdone = []
        an.clear()
        rp.clear()
        w_done = Q.last("pe", "act", "dve")
        lam = P2["lru_lambda_2", l]
        ring.remove(3)
        lamt = []

        def lam_consts():
            t = Q.act(op_activation, (pc_tok, w_done,), LAM[:, 0, :], PC[:, lam:lam + 4], ACT.Abs)
            t = Q.act(op_activation, (t,), LAM[:, 0, :], LAM[:, 0, :], ACT.Exp, scale=-1.0)
            t = Q.act(op_activation, (t, eps_tok,), LAM[:, 0, :], LAM[:, 0, :], ACT.Ln, bias=EPS[:, 2:3])
            u = Q.dve(op_tensor_scalar, (w_done,), LAM[:, 1, :], PC[:, lam:lam + 4], -1.0, 0.0, ALU.mult, ALU.max)
            u = Q.dve(op_tensor_tensor, (t, u,), LAM[:, 2, :], LAM[:, 1, :], LAM[:, 0, :], ALU.add)
            u = Q.dve(op_tensor_scalar, (u,), LAM[:, 3, :], LAM[:, 2, :], 8.0, None, ALU.mult)
            lamt.append(Q.dve(op_tensor_scalar, (u,), LAM[:, 1, :], LAM[:, 3, :], -1.0, None, ALU.mult))

        bz = Q.pool(op_memset, (w_done,), BD[:, :, :, :], 0.0)
        for g, nm in ((0, "w_rgate_2"), (1, "w_igate_2")):
            v = I[nm][l].rearrange("(m u) i j -> u i m j", u=2)
            for u2 in range(2):
                bd_in = Q.dma("bd", op_dma_start, (bz,), BD[64 * u2:64 * u2 + 64, g, :, 64 * u2:64 * u2 + 64], v[u2], engine="act")
        bf_in = Q.dma("bf", op_dma_start, (w_done,), BF[0:4, 0:1], I["b_fgate_2"][l:l + 1, :].rearrange("o h -> h o"), engine="act")
        fx = {}

        def fgate_logits():
            i, vh, vl, wt = next_slab()
            b = take(True)
            for k in range(KT):
                t = mm3_w(PB[b][0:4, :], vh[:, k, :], vl[:, k, :], HH[:, k, :], HL[:, k, :], k == 0, k == KT - 1,
                          wt, h_tok[k], free[b] if k == 0 else None, mark=(k == KT - 1))
                if k % 2:
                    yield
            done_slab(i, t)
            g, e, lf, F_ = (FF4[0:4, n, :] for n in range(4))
            t = Q.act(op_activation, (t, bf_in, w_done), g, PB[b][0:4, :], ACT.Identity, bias=BF[0:4, 0:1])
            let_go(b, t)
            u = Q.act(op_activation, (t,), e, g, ACT.Abs)
            u = Q.act(op_activation, (u,), e, e, ACT.Exp, scale=-1.0)
            u = Q.act(op_activation, (u,), e, e, ACT.Ln, bias=EPS[0:4, 2:3])
            u = Q.dve(op_scalar_tensor_tensor, (u, t), out=lf, in0=g, scalar=0.0, in1=e, op0=ALU.min,
                      op1=ALU.subtract)
            fx["F"] = Q.dve(op_tensor_tensor_scan, (u,), F_, lf, lf, 0.0, ALU.add, ALU.min)

        def fgates():
            yield [lambda: "F" in fx]
            yield fx["F"]
            F_ = FF4[0:4, 3, :]
            for j in range(TT):
                t = Q.pe(op_transpose, (fx["F"], free[4] if j == 0 else None), PB[4][:, 4 * j:4 * j + 4],
                         F_[:, j * 128:(j + 1) * 128], CB[0:4, C_ID:C_ID + 4], mark=(j == TT - 1))
            fx["q"] = free[4] = Q.act(op_activation, (t,), FG[:, 5, :], PB[4][:, 0:16], ACT.Copy)
            for h in range(4):
                bk = 4 + (h + 1) % 2
                t = mm(PB[bk][:, :], CB[0:4, C_ID + h:C_ID + h + 1].to_broadcast([4, 128]), F_, True, True,
                       fx["F"], free[bk], mark=True)
                fx["k", h] = free[bk] = Q.act(op_activation, (t, w_done,), FB[:, h, :], PB[bk][:, :], ACT.Copy,
                                              scale=-1.0)
                yield None
            fx["gates"] = t

        chain("s", fgates())

        def fm_out(dst, key, scale=1.0, more=()):
            def evac(m, ps, t):
                an[key, m] = Q.act(op_activation, (t, w_done, list(more)), dst[:, m, :], ps, ACT.Copy, scale=scale)
                return an[key, m]
            return evac

        def tm_out1(dst, key, *more):
            def evac(b2, ps, t):
                rp[key, b2] = Q.act(op_activation, (t, w_done, list(more)), dst[:, 2 * b2:2 * b2 + 2, :], ps, ACT.Copy)
                return rp[key, b2]
            return evac

        def fox_score(h, i, sb, sst, sm, f1):
            n = 128 * (i + 1)
            po, m = 64 * (h % 2), h // 2
            mm(PB[sb][:, 0:n], FXQ[po:po + 64, m, i * 128:(i + 1) * 128], FXK[po:po + 64, m, 0:n], True, False,
               an["fq", m], an["fk", m], free[sb])
            t = mm(PB[sb][:, n - 128:n], ident, CB[:, C_CADD:C_CADD + 128], False, True, mark=True)
            a = Q.dve(op_tensor_tensor_reduce, (t, fx["k", h], fx["gates"], f1), out=sst[:, 0:n], in0=PB[sb][:, 0:n],
                      in1=FB[:, h, 0:n], scale=0.125, scalar=-3e38, op0=ALU.add, op1=ALU.max, accum_out=sm[:, 0:1])
            free[sb] = a
            fq = FG[:, 5, 4 * i + h:4 * i + h + 1]
            g = Q.dve(op_tensor_tensor, (a, fx["q"]), sm[:, 3:4], sm[:, 0:1], fq, ALU.add)
            g = Q.dve(op_tensor_tensor, (g,), sm[:, 1:2], fq, sm[:, 3:4], ALU.subtract)
            x = Q.act(op_activation, (g,), sst[:, 0:n], sst[:, 0:n], ACT.Exp, bias=sm[:, 1:2],
                                             accum_out=sm[:, 2:3])
            return norm_rows(sst, sm, n, x)

        cw, cbias = P2["conv_w", l], P2["conv_b_2", l]
        lx = {}

        def lx_out(m, ps, t):
            lx[m] = Q.act(op_activation, (t, w_done,), LA[:, m, :], ps, ACT.Copy)
            return lx[m]

        def conv(m):
            t = Q.act(op_activation, (lx[m], w_done, pc_tok), LB[:, m, :], LA[:, m, :], ACT.Identity,
                      bias=col(cbias + m), scale=col(cw + 12 + m))
            for s_ in range(1, 4):
                t = Q.dve(op_scalar_tensor_tensor, (t,), out=LB[:, m, s_:S], in0=LA[:, m, 0:S - s_],
                          scalar=col(cw + (3 - s_) * 4 + m), in1=LB[:, m, s_:S], op0=ALU.mult, op1=ALU.add)
            lx["u", m] = t

        def lru():
            for m in range(4):
                yield lambda m=m: m in lx
                conv(m)
                yield None
            yield lambda: "F" in fx
            for g, dst, bias in ((0, LC, "b_rgate_2"), (1, LA, "b_igate_2")):
                for m in range(4):
                    yield lx["u", m]
                    bk = take()
                    t = mm(PB[bk][:, :], BD[:, g, m, :], LB[:, m, :], True, True, bd_in, bz, lx["u", m],
                           free[bk], mark=True)
                    lx[g, m] = free[bk] = Q.act(op_activation, (t, w_done), dst[:, m, :], PB[bk][:, :], ACT.Sigmoid,
                                                bias=col(P2[bias, l] + m))
            gates.append(Q.last("pe"))
            for m in range(4):
                lx["iu", m] = Q.dve(op_tensor_tensor, (lx[1, m], gates[0]), LB[:, m, :], LB[:, m, :], LA[:, m, :],
                                    ALU.mult)
            for m in range(4):
                lx["a", m] = Q.act(op_activation, (lx[0, m], w_done, lamt), LD[:, m, :], LC[:, m, :], ACT.Exp,
                                   scale=LAM[:, 1, m:m + 1])
                lx["t", m] = Q.act(op_activation, (lx["a", m], lamt), LC[:, m, :], LC[:, m, :], ACT.Tanh,
                                   scale=LAM[:, 3, m:m + 1])
                a_ = Q.dve(op_tensor_tensor, (lx["a", m], lx["iu", m]), LA[:, m, :], LD[:, m, :], LD[:, m, :],
                           ALU.mult)
                lx["m", m] = Q.dve(op_scalar_tensor_tensor, (a_, lx["t", m]), out=LA[:, m, :], in0=LA[:, m, :],
                                   scalar=1.0, in1=LC[:, m, :], op0=ALU.add, op1=ALU.mult)
                yield None
            for m in range(4):
                lx["r", m] = Q.act(op_activation, (lx["m", m],), LA[:, m, :], LA[:, m, :], ACT.Sqrt)
            yield None
            for m in range(4):
                t = Q.dve(op_tensor_tensor, (lx["r", m],), LB[:, m, :], LB[:, m, :], LA[:, m, :], ALU.mult)
                lx["h", m] = Q.dve(op_tensor_tensor_scan, (t, lx["t", m]), LC[:, m, :], LD[:, m, :], LB[:, m, :],
                                   0.0, ALU.mult, ALU.add)
                if m == 3:
                    lru_done.append(lx["h", 3])
                yield None

        def sb_items():
            offs = {3: 1152, 2: 896, 1: 512, 0: 0}
            st_free, w_free, sp_free = [lru_done, lru_done, fox_done], [lru_done, lru_done, fox_done], [None]
            spt = {}
            summed = set()
            st_buf = [ST[:, 0, :], ST[:, 1, :], ST3]
            sw_buf = [SW[:, 0, :], SW[:, 1, :], SW3]
            busy = set()

            def item(it, h, j):
                po, m = 64 * (h % 2), h // 2
                n = S - 128 * j
                yield lambda: len(busy) < (3 if fox_done else 2) and (j == 3 or h == 0 or h - 1 in summed)
                c = min((x for x in range(3 if fox_done else 2) if x not in busy), key=lambda x: Q.when(w_free[x]))
                busy.add(c)
                bk = (3, 5, 4)[c]

                def off(j_):
                    return 1280 if j_ == 3 and h % 2 else offs[j_]

                o = off(j)
                t = mm(PB[bk][:, 0:n], SBK[po:po + 64, m, j * 128:(j + 1) * 128], SBQ[po:po + 64, m, j * 128:S],
                       True, True, an["sq", m], an["sk", m], free[bk], mark=True)
                st = st_buf[c][:, 0:n]
                u = Q.act(op_activation, (t, st_free[c], w_free[c]), st, PB[bk][:, 0:n], ACT.Abs)
                u = Q.act(op_activation, (u,), st, st, ACT.Exp, scale=-1.0)
                u = Q.act(op_activation, (u,), st, st, ACT.Ln, bias=EPS[:, 2:3])
                v = Q.dve(op_scalar_tensor_tensor, (u, sp_free[0], lru_done), out=SP[:, o:o + n],
                          in0=PB[bk][:, 0:n], scalar=0.0, in1=st, op0=ALU.max, op1=ALU.add)
                st_free[c] = v
                spt[h, j] = v = Q.dve(op_tensor_tensor, (v,), SP[:, o:o + 128], SP[:, o:o + 128],
                                      CB[:, C_SMUL:C_SMUL + 128], ALU.mult)
                yield v
                mm(PB[bk][:, 0:128], ident, CB[:, C_SADD:C_SADD + 128], False, False, v, skip=True)
                t = mm(PB[bk][:, 0:n], CB[:, C_NT:C_NT + 128], SP[:, o:o + n], False, j == 3, v,
                       mark=(j == 3), skip=True)
                for j2 in range(j + 1, TT):
                    n2 = S - 128 * j2
                    o2 = off(j2)
                    t = mm(PB[bk][:, n - n2:n], CB[:, C_NONE:C_NONE + 128], SP[:, o2:o2 + n2], False, j2 == 3,
                           spt[h, j2], mark=(j2 == 3), skip=True)
                w = free[bk] = Q.act(op_activation, (t, w_free[c]), sw_buf[c][:, 0:n],
                                     PB[bk][:, 0:n], ACT.Exp)
                if j == 0:
                    sp_free[0] = t
                    summed.add(h)
                yield [w, lambda: ("sv", 1) in rp]
                p = mm(PB[6][po:po + 64, j * 128:S], SBV[:, j, h * 64:(h + 1) * 64], sw_buf[c][:, 0:n], j == 3,
                       j == 0, w, rp["sv", 0], rp["sv", 1], free[6] if h % 2 == 0 and j == 3 else None, mark=True,
                       skip=True)
                w_free[c] = p
                busy.discard(c)
                if h % 2 and j == 0:
                    an["so", m] = free[6] = Q.act(op_activation, (p,), SBQ[:, m, :], PB[6][:, :], ACT.Copy)

            return Window([item(4 * h + 3 - j, h, j) for h in range(4) for j in (3, 2, 1, 0)], 3,
                          lambda n: len(busy) < (3 if fox_done else 2))

        gates, lru_done = [], []

        def lg_out(m, ps, t):
            lx["g", m] = Q.act(op_activation, (t, fox_done), LG[:, m, :], ps, ACT.Copy)
            return lx["g", m]

        gm = P2["g_mix", l]

        def part_norm(parts, bank, early, need, bufs, buf_free):
            s = small[0] % NSM
            small[0] += 1
            done = list(buf_free)
            for n, (src, width, _, _, key) in enumerate(parts):
                for m in range(width):
                    yield need(key, m)
                    i_ = min(m, 1)
                    t = Q.act(op_activation, (an[key, m], done[i_]), bufs[:, i_, :], src[:, m, :], ACT.Square)
                    if m:
                        t = done[1] = Q.dve(op_tensor_tensor, (t,), bufs[:, 0, :], bufs[:, 0, :], bufs[:, 1, :],
                                            ALU.add)
                    yield t
                u = done[0] = stat(bufs[:, 0, :], bank, one, 1, n == 0, t, col=4 * n, last=n == len(parts) - 1)
            if early:
                sq_free[0], sq_free[1] = done
            for n, (_, width, _, _, _) in enumerate(parts):
                a_ = Q.act(op_activation, (u, eps_tok, rc_read[s]), SD[:, s, 4 * n:4 * n + 4],
                           PB[bank][:, 4 * n:4 * n + 4], ACT.Sqrt, bias=EPS[:, 0:1], scale=1.0 / (128 * width))
            free[bank] = a_
            if early:
                Q.table("natural_log_exp_and_others")
            r = Q.dve(op_reciprocal, (a_, rc_read[s]), RC[:, s, 0:4 * len(parts)], SD[:, s, 0:4 * len(parts)])
            yield r
            for n, (src, width, g0, k0, key) in enumerate(parts):
                for j in range(TT):
                    rt = mm(PB[bank][:, j * 128:(j + 1) * 128],
                            RC[:, s, 4 * n + j:4 * n + j + 1].to_broadcast([128, 128]), ident, True, True, r,
                            free[bank] if j == 0 else None, mark=(j == TT - 1))
                ts = {}

                def scaled(m):
                    ts[m] = Q.dve(op_scalar_tensor_tensor, (rt, an[key, m], pc_tok, tm_read[m % 2]),
                                  out=TM[:, m % 2, :], in0=src[:, m, :], scalar=col(gm + g0 + m),
                                  in1=PB[bank][:, :], op0=ALU.mult, op1=ALU.mult)

                scaled(0)
                for m in range(width):
                    i_ = m % 2
                    hi = Q.act(op_activation, (ts[m], hdone), HH[:, k0 + m, :], TM[:, i_, :], ACT.Copy)
                    if m + 1 < width:
                        scaled(m + 1)
                    lo = Q.dve(op_tensor_tensor, (hi, ts[m], hdone), HL[:, k0 + m, :], TM[:, i_, :],
                               f(HH[:, k0 + m, :]), ALU.subtract)
                    tm_read[i_] = [hi, lo]
                    h_tok[k0 + m] = [hi, lo]
                    if m % 2:
                        yield None
                free[bank] = ts[width - 1]
            rc_read[s] = rt

        def gelus():
            yield lambda: ("g", 3) in lx
            yield lx["g", 3]
            for m in range(4):
                g = Q.act(op_activation, (lx["g", m],), LG[:, m, :], LG[:, m, :], ACT.Gelu_apprx_tanh)
                an["ly", m] = Q.dve(op_tensor_tensor, (lx["h", m], g), LC[:, m, :], LC[:, m, :], LG[:, m, :],
                                    ALU.mult)
            Q.table("natural_log_exp_and_others")

        def known(key, m):
            return lambda: (key, m) in an

        tm_read = [hread[0], hread[0]]

        chain("l", lru())
        run(proj_fm(2, HH, HL, h_tok, lx_out, True))
        run(proj_fm(2, HH, HL, h_tok, lx_out, False, m0=2))
        Q.table("natural_log_exp_and_others")
        lam_consts()
        run(fgate_logits())
        gq = P2["g_qk", l]
        fn = {}
        chain("s", many_norm([(FXQ, "fq", 0, col(gq)), (FXK, "fk", 0, col(gq + 1)), (FXQ, "fq", 1, col(gq)),
                              (FXK, "fk", 1, col(gq + 1))], lambda: ("r", 3) in lx, 1.0 / 64, fn))
        run(proj_fm(2, HH, HL, h_tok, fm_out(FXQ, "fq"), False))
        run(proj_fm(2, HH, HL, h_tok, fm_out(FXK, "fk"), False))
        fox_done = []

        def fox_table():
            yield lambda: bool(lru_done)
            an.update(fn)
            Q.table("natural_log_exp_and_others")

        def fox_end():
            fox_done.append(Q.last("pe", "act", "dve"))
            yield None

        chain("s", fox_table())
        chain("s", Window(soft_attention(
            [(h, i) for h in range(4) for i in (3, 2, 1, 0)], fox_score, lambda i: 128 * (i + 1),
            [FS[:, 0, :], FS[:, 1, :], FS2], [FP[:, 0, :], FP[:, 1, :]],
            head_pair_finish(FXV, lambda h: [("fv", 0), ("fv", 1)], FXQ, "fo"), (4,),
            lambda: ("fv", 1) in rp), 3))
        chain("s", fox_end())
        run(proj_tm(TT, HH, HL, h_tok, tm_out1(FXV, "fv")))
        force(lambda: lru_done)
        run(proj_fm(2, HH, HL, h_tok, fm_out(SBQ, "sq", 0.125, lru_done), False))
        run(proj_fm(2, HH, HL, h_tok, fm_out(SBK, "sk", 1.0, lru_done), False))
        chain("b", sb_items())
        run(proj_tm(TT, HH, HL, h_tok, tm_out1(SBV, "sv", gates)))
        while not fox_done:
            chains["s"][0].step()
            best()
        for c in range(2):
            run(proj_fm(2, HH, HL, h_tok, lg_out, False, m0=2 * c))
        hdone.extend(Q.last("pe"))
        stale()
        tm_read = [hread[0], hread[0]]
        chain("l", gelus())
        chain("l", part_norm([(LC, 4, 0, 0, "ly"), (FXQ, 2, 6, 6, "fo")], 7, True, known, SQ, sq_free))
        chain("b", part_norm([(SBQ, 2, 4, 4, "so")], 4, False, known, SQ2, [fox_done, fox_done]))
        sqs, xt = [], []
        order_k = (0, 1, 2, 3, 6, 7, 4, 5)
        run(proj_fm3(HH, HL, h_tok, x_add(1, xt), ks=order_k, first=3))
        ring.append(3)
        chain("w", watch(lambda m: X[:, m, :], xt, sqs))
        for c in range(2, 4):
            run(proj_fm(2, HH, HL, h_tok, x_add(1, xt), False, m0=2 * c, ks=order_k))
        drain()
        return sqs

    for l in range(2):
        if l:
            mt = mod_cols(1)
            chain("s", rms_h(sqs[-1], a2(0), s2(1, 0), mt))
            stale()
        sqs = ffn2(0, True)
        chain("s", rms_h(sqs[-1], a2(1), s2(l, 1), mt))
        stale()
        sqs = mixer2(l)
        chain("s", rms_h(sqs[-1], a2(2), s2(l, 2), mt))
        stale()
        sqs = ffn2(2, l == 0)

    for j in range(TT):
        toks = []
        for hf in range(2):
            b = take()
            for q in range(4):
                t = Q.pe(op_transpose, (x_tok[4 * hf + q], free[b] if q == 0 else None), PB[b][:, q * 128:(q + 1) * 128],
                         X[:, 4 * hf + q, j * 128:(j + 1) * 128], ident, mark=q == 3)
            o = OT[:, j, hf * 512:(hf + 1) * 512]
            if hf:
                t = Q.act(op_activation, (t,), o, PB[b][:, :], ACT.Copy)
            else:
                t = Q.dve(op_tensor_copy, (t,), o, PB[b][:, :])
            free[b] = t
            toks.append(t)
        out_tok = Q.dma("out", op_dma_start, toks, out[0, j * 128:(j + 1) * 128, :], OT[:, j, :])

    with ExitStack() as ctx:
        sems = {name: ctx.enter_context(nc.semaphore("s_" + name)) for name in Q.count}
        block = ctx.enter_context(nc.Block())

        @block.sync
        def _(e):
            Q.run("sp", e, sems)
            e.wait_ge(sems["out"], out_tok[1])

        @block.gpsimd
        def _(e):
            Q.run("pool", e, sems)

        @block.scalar
        def _(e):
            Q.run("act", e, sems)

        @block.vector
        def _(e):
            Q.run("dve", e, sems)

        @block.tensor
        def _(e):
            Q.run("pe", e, sems)


_NAMES = ["x", "mem", "pre_mix_g", "post_mix_g", "w_in", "attn_gn_g", "ret_gn_g", "w_out", "pre_mem_g",
          "post_mem_g", "mem_norm_g", "w_q_mem", "w_kv_mem", "w_o_mem", "pre_ffn_g", "post_ffn_g", "w_gate_up",
          "w_down", "c_2", "w_ada_2", "b_ada_2", "g_norm_2", "w_ffn_up_2", "w_ffn_down_2", "w_in_2", "b_fgate_2",
          "conv_w_2", "conv_b_2", "w_rgate_2", "b_rgate_2", "w_igate_2", "b_igate_2", "lru_lambda_2", "g_qk_2",
          "g_mix_out_2", "w_out_2"]


def kernel(**inputs):
    import numpy as _np
    import concourse.bacc as _bacc
    from concourse import mybir as _mybir
    from concourse.bass_utils import run_bass_kernel_spmd as _run

    nc = _bacc.Bacc("TRN2", target_bir_lowering=False, num_devices=1)
    arrays, aps = {}, {}
    cb, ct = const_tables()
    for name, a in [(n, _np.ascontiguousarray(inputs[n])) for n in _NAMES] + [("c_b", cb), ("c_t", ct)]:
        arrays["in_" + name] = a
        aps[name] = nc.dram_tensor("in_" + name, a.shape, _mybir.dt.from_np(a.dtype), kind="ExternalInput").ap()
    out = nc.dram_tensor("out_0_dram", (1, S, D), _mybir.dt.float32, kind="ExternalOutput").ap()
    build(nc, aps, out)
    r = _run(nc, [arrays], core_ids=[0])
    return r.results[0]["out_0_dram"]
```
